# Optimizing a Trainium2 kernel written in Bass

```python
import math
import jax, jax.numpy as jnp
from jax import lax
import numpy as np

D_MODEL = 1024
BATCH = 1
SEQ = 1024
DEPTH = 1

EPS = 1e-6
A_WIDTH = 768
A_GROUPS = 4
A_GROUP_DIM = A_WIDTH // A_GROUPS
CHUNK = 128
B_PATTERNS = ((128, 1), (512, 4), (2048, 16))
B_GROUPS = len(B_PATTERNS)
B_HEADS_PER_GROUP = 4
B_HEADS = B_GROUPS * B_HEADS_PER_GROUP
B_HEAD_DIM = 64
B_QKV_WIDTH = B_HEADS * B_HEAD_DIM
B_OUT_WIDTH = B_HEADS_PER_GROUP * B_HEAD_DIM
BLOCK = 128
MEM_LEN = 256
M_HEADS = 4
M_HEAD_DIM = 128
M_WIDTH = M_HEADS * M_HEAD_DIM
N_BRANCHES = 3
REL_BUCKETS = 32
REL_MAX_DISTANCE = 2048
IN_SIZES = (A_WIDTH, A_WIDTH, A_WIDTH,
            B_QKV_WIDTH, B_QKV_WIDTH, B_QKV_WIDTH, B_OUT_WIDTH,
            M_WIDTH, M_WIDTH,
            N_BRANCHES * D_MODEL)
IN_TOTAL = sum(IN_SIZES)


def rms_norm(x, w):
    xf = x.astype(jnp.float32)
    y = xf * lax.rsqrt(jnp.mean(xf * xf, axis=-1, keepdims=True) + EPS)
    return (y * w.astype(jnp.float32)).astype(x.dtype)

def layer_norm(x, w, b):
    xf = x.astype(jnp.float32)
    mu = jnp.mean(xf, axis=-1, keepdims=True)
    xc = xf - mu
    y = xc * lax.rsqrt(jnp.mean(xc * xc, axis=-1, keepdims=True) + EPS)
    return (y * w.astype(jnp.float32) + b.astype(jnp.float32)).astype(x.dtype)

def t5_causal_bucket(dist):
    max_exact = REL_BUCKETS // 2
    is_small = dist < max_exact
    df = jnp.maximum(dist, 1).astype(jnp.float32)
    large = max_exact + (jnp.log(df / max_exact) / math.log(REL_MAX_DISTANCE / max_exact)
                         * (REL_BUCKETS - max_exact)).astype(jnp.int32)
    large = jnp.minimum(large, REL_BUCKETS - 1)
    return jnp.where(is_small, dist, large)

def chunked_spatial_gating(u, v, w_s, b_s):
    bn, s, _ = u.shape
    nc = s // CHUNK
    causal = jnp.tril(jnp.ones((CHUNK, CHUNK), dtype=bool))
    w = jnp.where(causal[None], w_s, 0).astype(v.dtype)
    vc = v.reshape(bn, nc, CHUNK, A_GROUPS, A_GROUP_DIM)
    mixed = jnp.einsum('gts,bcsgd->bctgd', w, vc) + b_s.T.astype(v.dtype)[None, None, :, :, None]
    return u * mixed.reshape(bn, s, A_WIDTH)

def dilated_window_attention(q, k, v, bias_table, dilation, win_steps):
    bn, s, h, hd = q.shape
    L = s // dilation
    bd = bn * dilation

    def to_residue(t):
        return jnp.moveaxis(t.reshape((bn, L, dilation) + t.shape[2:]), 2, 1).reshape((bd, L) + t.shape[2:])

    def from_residue(t):
        t = t.reshape((bn, dilation, L) + t.shape[2:])
        return jnp.moveaxis(t, 1, 2).reshape((bn, s) + t.shape[3:])

    qs, ks, vs = to_residue(q), to_residue(k), to_residue(v)
    nb = -(-L // BLOCK)
    lp = nb * BLOCK
    pad = lp - L
    qb = jnp.pad(qs, ((0, 0), (0, pad), (0, 0), (0, 0))).reshape(bd, nb, BLOCK, h, hd)

    def kv_blocks(t):
        tp = jnp.pad(t, ((0, 0), (BLOCK, pad), (0, 0), (0, 0))).reshape(bd, nb + 1, BLOCK, h, hd)
        return jnp.concatenate([tp[:, :-1], tp[:, 1:]], axis=2)

    kb, vb = kv_blocks(ks), kv_blocks(vs)
    qi = jnp.arange(BLOCK)[:, None]
    kj = jnp.arange(2 * BLOCK)[None, :]
    step = qi + BLOCK - kj
    in_window = (step >= 0) & (step <= win_steps)
    key_pos = jnp.arange(nb)[:, None, None] * BLOCK - BLOCK + kj[None]
    valid = in_window[None] & (key_pos >= 0)
    bucket = t5_causal_bucket(jnp.maximum(step, 0) * dilation)
    bias = jnp.transpose(bias_table[bucket], (2, 0, 1)).astype(jnp.float32)

    scores = jnp.einsum('bnqhd,bnkhd->bnhqk', qb.astype(jnp.float32), kb.astype(jnp.float32)) * (hd ** -0.5)
    scores = jnp.where(valid[None, :, None], scores + bias[None, None], -1e30)
    m = jnp.max(scores, axis=-1, keepdims=True)
    p = jnp.exp(scores - m)
    l = jnp.sum(p, axis=-1)
    o = jnp.einsum('bnhqk,bnkhd->bnqhd', p, vb.astype(jnp.float32))
    o = o / jnp.transpose(l, (0, 1, 3, 2))[..., None]
    lse = jnp.transpose(m[..., 0] + jnp.log(l), (0, 1, 3, 2))
    o = o.reshape(bd, lp, h, hd)[:, :L]
    lse = lse.reshape(bd, lp, h)[:, :L]
    return from_residue(o), from_residue(lse)

def first_inputs(seed: int = 0) -> dict:
    key = jax.random.key(seed)
    ks = jax.random.split(key, 22)
    f32 = jnp.float32
    n = lambda k, shape: jax.random.normal(k, shape, f32)
    return {
        "x": n(ks[0], (BATCH, SEQ, D_MODEL)),
        "mem": n(ks[1], (BATCH, MEM_LEN, D_MODEL)),
        "norm_w": 1.0 + 0.02 * n(ks[2], (D_MODEL,)),
        "w_in": n(ks[3], (D_MODEL, IN_TOTAL)) * D_MODEL ** -0.5,
        "gate_b": 0.01 * n(ks[4], (N_BRANCHES, D_MODEL)),
        "a_v_norm_w": 1.0 + 0.02 * n(ks[5], (A_WIDTH,)),
        "a_v_norm_b": 0.02 * n(ks[6], (A_WIDTH,)),
        "a_spatial_w": n(ks[7], (A_GROUPS, CHUNK, CHUNK)) * CHUNK ** -0.5,
        "a_spatial_b": 1.0 + 0.02 * n(ks[8], (A_GROUPS, CHUNK)),
        "b_q_norm_w": 1.0 + 0.02 * n(ks[9], (B_HEAD_DIM,)),
        "b_k_norm_w": 1.0 + 0.02 * n(ks[10], (B_HEAD_DIM,)),
        "rel_bias": 0.2 * n(ks[11], (REL_BUCKETS, B_HEADS)),
        "mem_norm_w": 1.0 + 0.02 * n(ks[12], (D_MODEL,)),
        "m_w_kv": n(ks[13], (D_MODEL, 2 * M_WIDTH)) * D_MODEL ** -0.5,
        "m_q_norm_w": 1.0 + 0.02 * n(ks[14], (M_HEAD_DIM,)),
        "m_k_norm_w": 1.0 + 0.02 * n(ks[15], (M_HEAD_DIM,)),
        "proj_a": n(ks[16], (A_WIDTH, D_MODEL)) * A_WIDTH ** -0.5,
        "proj_b": n(ks[17], (B_OUT_WIDTH, D_MODEL)) * B_OUT_WIDTH ** -0.5,
        "proj_m": n(ks[18], (M_WIDTH, D_MODEL)) * M_WIDTH ** -0.5,
        "w_out": n(ks[19], (D_MODEL, D_MODEL)) * D_MODEL ** -0.5,
    }

def first_block(x, mem, norm_w, w_in, gate_b, a_v_norm_w, a_v_norm_b, a_spatial_w, a_spatial_b,
              b_q_norm_w, b_k_norm_w, rel_bias, mem_norm_w, m_w_kv, m_q_norm_w, m_k_norm_w,
              proj_a, proj_b, proj_m, w_out):
    bn, s, _ = x.shape
    split_at = np.cumsum(IN_SIZES)[:-1].tolist()
    for _layer in range(DEPTH):
        h = rms_norm(x, norm_w)
        proj = h @ w_in
        a_u, a_v, a_z, b_q, b_k, b_v, b_z, m_q, m_z, g = jnp.split(proj, split_at, axis=-1)

        u = jax.nn.gelu(a_u, approximate=False)
        vv = layer_norm(jax.nn.gelu(a_v, approximate=False), a_v_norm_w, a_v_norm_b)
        y_a = chunked_spatial_gating(u, vv, a_spatial_w, a_spatial_b) * jax.nn.silu(a_z)

        q = rms_norm(b_q.reshape(bn, s, B_HEADS, B_HEAD_DIM), b_q_norm_w)
        k = rms_norm(b_k.reshape(bn, s, B_HEADS, B_HEAD_DIM), b_k_norm_w)
        v = b_v.reshape(bn, s, B_HEADS, B_HEAD_DIM)
        outs, lses = [], []
        for gi, (window, dilation) in enumerate(B_PATTERNS):
            hs = slice(gi * B_HEADS_PER_GROUP, (gi + 1) * B_HEADS_PER_GROUP)
            o_g, lse_g = dilated_window_attention(q[:, :, hs], k[:, :, hs], v[:, :, hs],
                                                  rel_bias[:, hs], dilation, window // dilation)
            outs.append(o_g)
            lses.append(lse_g)
        o_all = jnp.stack(outs, axis=0)
        wts = jax.nn.softmax(jnp.stack(lses, axis=0), axis=0)
        y_b = jnp.sum(wts[..., None] * o_all, axis=0).reshape(bn, s, B_OUT_WIDTH).astype(x.dtype)
        y_b = y_b * jax.nn.silu(b_z)

        kv = rms_norm(mem, mem_norm_w) @ m_w_kv
        mk, mv = jnp.split(kv, 2, axis=-1)
        mq = rms_norm(m_q.reshape(bn, s, M_HEADS, M_HEAD_DIM), m_q_norm_w)
        mk = rms_norm(mk.reshape(bn, MEM_LEN, M_HEADS, M_HEAD_DIM), m_k_norm_w)
        mv = mv.reshape(bn, MEM_LEN, M_HEADS, M_HEAD_DIM)
        sc = jnp.einsum('bshd,bmhd->bhsm', mq.astype(jnp.float32), mk.astype(jnp.float32)) * (M_HEAD_DIM ** -0.5)
        pm = jax.nn.softmax(sc, axis=-1)
        y_m = jnp.einsum('bhsm,bmhd->bshd', pm, mv.astype(jnp.float32)).reshape(bn, s, M_WIDTH).astype(x.dtype)
        y_m = y_m * jax.nn.silu(m_z)

        gates = jax.nn.sigmoid((g.reshape(bn, s, N_BRANCHES, D_MODEL) + gate_b).astype(jnp.float32)).astype(x.dtype)
        merged = (gates[:, :, 0] * (y_a @ proj_a)
                  + gates[:, :, 1] * (y_b @ proj_b)
                  + gates[:, :, 2] * (y_m @ proj_m))
        x = x + merged @ w_out
    return x


_first_inputs = first_inputs


def first_inputs(seed=0):
    import zlib

    import numpy as np

    out = dict(_first_inputs(seed))
    spreads = {}
    factors = {'norm_w': 6.546,
     'gate_b': 8.0,
     'a_v_norm_w': 8.0,
     'a_v_norm_b': 8.0,
     'a_spatial_b': 8.0,
     'b_q_norm_w': 8.0,
     'b_k_norm_w': 8.0,
     'rel_bias': 8.0,
     'mem_norm_w': 8.0,
     'm_q_norm_w': 8.0,
     'm_k_norm_w': 8.0}
    for name, (base, spread) in spreads.items():
        noise = np.random.default_rng([zlib.crc32(name.encode()), seed]).standard_normal(out[name].shape)
        drawn = base * np.exp(spread * noise) if base else spread * noise
        out[name] = __import__('jax').numpy.asarray(drawn.astype(out[name].dtype))
    for name, factor in factors.items():
        out[name] = (out[name] * factor).astype(out[name].dtype)
    return out


_narrow_inputs = first_inputs


def first_inputs(seed=0):

    out = dict(_narrow_inputs(seed))
    wider = {'gate_b': 5.22,
     'a_v_norm_w': 5.71,
     'a_v_norm_b': 5.35,
     'a_spatial_b': 4.19,
     'b_q_norm_w': 3.09,
     'rel_bias': 3.08}
    for name, times in wider.items():
        mean = out[name].mean()
        out[name] = (mean + times * (out[name] - mean)).astype(out[name].dtype)
    return out


SSM_GROUP = 16
SSM_GROUPS = D_MODEL // 64
SSM_WIDTH = SSM_GROUPS * SSM_GROUP
SSM_STATE = 64
DIFF_HEADS = D_MODEL // 256
DIFF_HEAD_DIM = 64
DIFF_WIDTH = DIFF_HEADS * 2 * DIFF_HEAD_DIM
SWA_Q_HEADS = D_MODEL // 256
SWA_KV_HEADS = 2
SWA_GROUP = SWA_Q_HEADS // SWA_KV_HEADS
SWA_HEAD_DIM = 64
SWA_WIDTH = SWA_Q_HEADS * SWA_HEAD_DIM
SWA_KV_WIDTH = SWA_KV_HEADS * SWA_HEAD_DIM
WINDOW = 128
Q_BLOCK = 128
D_MIX = SSM_WIDTH + DIFF_WIDTH + SWA_WIDTH
IN_COLS = 2 * SSM_WIDTH + 4 * DIFF_WIDTH + 2 * SWA_WIDTH + 2 * SWA_KV_WIDTH
N_ATTN_HEADS = DIFF_HEADS + SWA_Q_HEADS
RMS_EPS = 1e-6


def rms_norm_2(x, gain):
    xf = x.astype(jnp.float32)
    y = xf * lax.rsqrt(jnp.mean(xf * xf, axis=-1, keepdims=True) + RMS_EPS)
    return (y * gain.astype(jnp.float32)).astype(x.dtype)

def alibi_slopes():
    i = jnp.arange(1, N_ATTN_HEADS + 1, dtype=jnp.float32)
    return jnp.exp2(-i * (8.0 / N_ATTN_HEADS))

def split_cols(proj):
    sizes = [SSM_WIDTH, SSM_WIDTH,
             DIFF_WIDTH, DIFF_WIDTH, DIFF_WIDTH, DIFF_WIDTH,
             SWA_WIDTH, SWA_KV_WIDTH, SWA_KV_WIDTH, SWA_WIDTH]
    out, start = [], 0
    for n in sizes:
        out.append(proj[..., start:start + n])
        start += n
    return out

def s5_mixer(u, lam_re, lam_im, log_step, b_re, b_im, c_re, c_im, d_skip, w_glu, b_glu):
    bsz, seq, _ = u.shape
    ug = u.reshape(bsz, seq, SSM_GROUPS, SSM_GROUP).astype(jnp.float32)
    step = jnp.exp(log_step.astype(jnp.float32))[:, None]
    lr = lam_re.astype(jnp.float32)
    li = lam_im.astype(jnp.float32)
    mag = jnp.exp(lr * step)
    ang = li * step
    ab_re = mag * jnp.cos(ang)
    ab_im = mag * jnp.sin(ang)
    den = lr * lr + li * li
    f_re = ((ab_re - 1.0) * lr + ab_im * li) / den
    f_im = (ab_im * lr - (ab_re - 1.0) * li) / den
    br = b_re.astype(jnp.float32)
    bi = b_im.astype(jnp.float32)
    bb_re = f_re[..., None] * br - f_im[..., None] * bi
    bb_im = f_re[..., None] * bi + f_im[..., None] * br
    bu_re = jnp.einsum('bsgh,gph->bsgp', ug, bb_re)
    bu_im = jnp.einsum('bsgh,gph->bsgp', ug, bb_im)
    a_re = jnp.broadcast_to(ab_re, bu_re.shape)
    a_im = jnp.broadcast_to(ab_im, bu_im.shape)

    def combine(e1, e2):
        a1r, a1i, b1r, b1i = e1
        a2r, a2i, b2r, b2i = e2
        return (a2r * a1r - a2i * a1i,
                a2r * a1i + a2i * a1r,
                a2r * b1r - a2i * b1i + b2r,
                a2r * b1i + a2i * b1r + b2i)

    _, _, st_re, st_im = lax.associative_scan(combine, (a_re, a_im, bu_re, bu_im), axis=1)
    y = (jnp.einsum('bsgp,ghp->bsgh', st_re, c_re.astype(jnp.float32))
         - jnp.einsum('bsgp,ghp->bsgh', st_im, c_im.astype(jnp.float32))
         + d_skip.astype(jnp.float32).reshape(SSM_GROUPS, SSM_GROUP) * ug)
    y = jax.nn.gelu(y.reshape(bsz, seq, SSM_WIDTH))
    y = y * jax.nn.sigmoid(y @ w_glu.astype(jnp.float32) + b_glu.astype(jnp.float32))
    return y.astype(u.dtype)

def diff_attention(q, k, v, slopes, lam, subln_gain, lam_init):
    bsz, seq = q.shape[0], q.shape[1]
    nb = seq // Q_BLOCK
    scale = DIFF_HEAD_DIM ** -0.5
    k1, k2 = k[:, :, :, 0], k[:, :, :, 1]

    def to_blocks(t):
        return t.reshape(bsz, nb, Q_BLOCK, DIFF_HEADS, DIFF_HEAD_DIM).transpose(1, 0, 2, 3, 4)

    q1b, q2b = to_blocks(q[:, :, :, 0]), to_blocks(q[:, :, :, 1])
    key_pos = jnp.arange(seq)

    def block(args):
        q1_blk, q2_blk, blk = args
        t = blk * Q_BLOCK + jnp.arange(Q_BLOCK)
        dist = t[:, None] - key_pos[None, :]
        mask = dist >= 0
        bias = -slopes[:, None, None] * dist.astype(jnp.float32)[None]

        def probs(qb, kk):
            s = jnp.einsum('bqhd,bkhd->bhqk', qb, kk).astype(jnp.float32) * scale + bias
            return jax.nn.softmax(jnp.where(mask, s, -jnp.inf), axis=-1)

        p = probs(q1_blk, k1) - lam * probs(q2_blk, k2)
        return jnp.einsum('bhqk,bkhd->bqhd', p.astype(v.dtype), v)

    o = lax.map(block, (q1b, q2b, jnp.arange(nb)))
    o = o.transpose(1, 0, 2, 3, 4).reshape(bsz, seq, DIFF_HEADS, 2 * DIFF_HEAD_DIM)
    o = rms_norm_2(o, subln_gain) * (1.0 - lam_init)
    return o.reshape(bsz, seq, DIFF_WIDTH)

def sliding_window_attention(q, k, v, slopes, sinks):
    bsz, seq = q.shape[0], q.shape[1]
    nb = seq // WINDOW
    scale = SWA_HEAD_DIM ** -0.5
    qb = q.reshape(bsz, nb, WINDOW, SWA_KV_HEADS, SWA_GROUP, SWA_HEAD_DIM)

    def band(t):
        cur = t.reshape(bsz, nb, WINDOW, SWA_KV_HEADS, SWA_HEAD_DIM)
        prev = jnp.concatenate([jnp.zeros_like(cur[:, :1]), cur[:, :-1]], axis=1)
        return jnp.concatenate([prev, cur], axis=2)

    kk, vv = band(k), band(v)
    t_loc = WINDOW + jnp.arange(WINDOW)
    s_loc = jnp.arange(2 * WINDOW)
    dist = t_loc[:, None] - s_loc[None, :]
    valid = (jnp.arange(nb)[:, None] * WINDOW - WINDOW + s_loc[None, :]) >= 0
    mask = ((dist >= 0) & (dist < WINDOW))[None] & valid[:, None, :]
    sl = slopes.reshape(SWA_KV_HEADS, SWA_GROUP)
    bias = -sl[:, :, None, None] * dist.astype(jnp.float32)
    s = jnp.einsum('bnqkgd,bnskd->bnkgqs', qb, kk).astype(jnp.float32) * scale + bias[None, None]
    s = jnp.where(mask[None, :, None, None], s, -jnp.inf)
    sink = sinks.astype(jnp.float32).reshape(SWA_KV_HEADS, SWA_GROUP)[None, None, :, :, None, None]
    m = jnp.maximum(jnp.max(s, axis=-1, keepdims=True), sink)
    e = jnp.exp(s - m)
    p = e / (jnp.sum(e, axis=-1, keepdims=True) + jnp.exp(sink - m))
    o = jnp.einsum('bnkgqs,bnskd->bnqkgd', p.astype(v.dtype), vv)
    return o.reshape(bsz, seq, SWA_WIDTH)

def hybrid_layer(x, cond, layer_idx, norm_gain, ada_w, ada_b, w_in, w_out,
                 ssm_lam_re, ssm_lam_im, ssm_log_step, ssm_b_re, ssm_b_im,
                 ssm_c_re, ssm_c_im, ssm_d, glu_w, glu_b,
                 diff_lq1, diff_lk1, diff_lq2, diff_lk2, diff_subln, swa_sinks):
    bsz, seq, _ = x.shape
    mod = cond @ ada_w + ada_b
    shift, scl, gate = jnp.split(mod, 3, axis=-1)
    h = rms_norm_2(x, norm_gain) * (1.0 + scl[:, None, :]) + shift[:, None, :]
    proj = h @ w_in
    (u, z_ssm, qd, kd, vd, z_diff, qs, ks, vs, z_swa) = split_cols(proj)

    slopes = alibi_slopes()
    swa_slopes = slopes[:SWA_Q_HEADS]
    diff_slopes = slopes[SWA_Q_HEADS:]

    y_ssm = s5_mixer(u, ssm_lam_re, ssm_lam_im, ssm_log_step, ssm_b_re, ssm_b_im,
                     ssm_c_re, ssm_c_im, ssm_d, glu_w, glu_b) * jax.nn.silu(z_ssm)

    lam_init = 0.8 - 0.6 * math.exp(-0.3 * layer_idx)
    lam = (jnp.exp(jnp.sum(diff_lq1.astype(jnp.float32) * diff_lk1.astype(jnp.float32)))
           - jnp.exp(jnp.sum(diff_lq2.astype(jnp.float32) * diff_lk2.astype(jnp.float32)))
           + lam_init)
    qd = qd.reshape(bsz, seq, DIFF_HEADS, 2, DIFF_HEAD_DIM)
    kd = kd.reshape(bsz, seq, DIFF_HEADS, 2, DIFF_HEAD_DIM)
    vd = vd.reshape(bsz, seq, DIFF_HEADS, 2 * DIFF_HEAD_DIM)
    y_diff = diff_attention(qd, kd, vd, diff_slopes, lam, diff_subln, lam_init) * jax.nn.silu(z_diff)

    qs = qs.reshape(bsz, seq, SWA_Q_HEADS, SWA_HEAD_DIM)
    ks = ks.reshape(bsz, seq, SWA_KV_HEADS, SWA_HEAD_DIM)
    vs = vs.reshape(bsz, seq, SWA_KV_HEADS, SWA_HEAD_DIM)
    y_swa = sliding_window_attention(qs, ks, vs, swa_slopes, swa_sinks) * jax.nn.silu(z_swa)

    y = jnp.concatenate([y_ssm, y_diff.astype(x.dtype), y_swa.astype(x.dtype)], axis=-1) @ w_out
    return x + gate[:, None, :] * y

def second_inputs(seed: int = 0) -> dict:
    key = jax.random.key(seed)
    ks = jax.random.split(key, 26)
    f32 = jnp.float32

    def nrm(k, shape, scale):
        return jax.random.normal(k, shape, f32) * scale

    L, G, P, H = DEPTH, SSM_GROUPS, SSM_STATE, SSM_GROUP
    ada_b = nrm(ks[4], (L, 3 * D_MODEL), 0.01)
    ada_b = ada_b.at[:, 2 * D_MODEL:].add(1.0)
    lam_im = jnp.broadcast_to(jnp.pi * jnp.arange(P, dtype=f32), (L, G, P)) + nrm(ks[8], (L, G, P), 0.01)
    return {
        "x": nrm(ks[0], (BATCH, SEQ, D_MODEL), 1.0),
        "c": nrm(ks[1], (BATCH, D_MODEL), 1.0),
        "norm_gain": 1.0 + nrm(ks[2], (L, D_MODEL), 0.02),
        "ada_w": nrm(ks[3], (L, D_MODEL, 3 * D_MODEL), 0.1 * D_MODEL ** -0.5),
        "ada_b": ada_b,
        "w_in": nrm(ks[5], (L, D_MODEL, IN_COLS), D_MODEL ** -0.5),
        "w_out": nrm(ks[6], (L, D_MIX, D_MODEL), D_MIX ** -0.5),
        "ssm_lam_re": -0.5 + nrm(ks[7], (L, G, P), 0.01),
        "ssm_lam_im": lam_im,
        "ssm_log_step": jax.random.uniform(ks[9], (L, G), f32, math.log(1e-3), math.log(1e-1)),
        "ssm_b_re": nrm(ks[10], (L, G, P, H), (2 * H) ** -0.5),
        "ssm_b_im": nrm(ks[11], (L, G, P, H), (2 * H) ** -0.5),
        "ssm_c_re": nrm(ks[12], (L, G, H, P), 0.5),
        "ssm_c_im": nrm(ks[13], (L, G, H, P), 0.5),
        "ssm_d": nrm(ks[14], (L, SSM_WIDTH), 1.0),
        "glu_w": nrm(ks[15], (L, SSM_WIDTH, SSM_WIDTH), SSM_WIDTH ** -0.5),
        "glu_b": nrm(ks[16], (L, SSM_WIDTH), 0.01),
        "diff_lq1": nrm(ks[17], (L, DIFF_HEAD_DIM), 0.1),
        "diff_lk1": nrm(ks[18], (L, DIFF_HEAD_DIM), 0.1),
        "diff_lq2": nrm(ks[19], (L, DIFF_HEAD_DIM), 0.1),
        "diff_lk2": nrm(ks[20], (L, DIFF_HEAD_DIM), 0.1),
        "diff_subln": 1.0 + nrm(ks[21], (L, 2 * DIFF_HEAD_DIM), 0.02),
        "swa_sinks": nrm(ks[22], (L, SWA_Q_HEADS), 1.0),
        "final_gain": 1.0 + nrm(ks[23], (D_MODEL,), 0.02),
    }

def second_block(x, c, norm_gain, ada_w, ada_b, w_in, w_out, ssm_lam_re, ssm_lam_im,
              ssm_log_step, ssm_b_re, ssm_b_im, ssm_c_re, ssm_c_im, ssm_d, glu_w, glu_b,
              diff_lq1, diff_lk1, diff_lq2, diff_lk2, diff_subln, swa_sinks, final_gain):
    cond = jax.nn.silu(c)
    for l in range(DEPTH):
        x = hybrid_layer(x, cond, l, norm_gain[l], ada_w[l], ada_b[l], w_in[l], w_out[l],
                         ssm_lam_re[l], ssm_lam_im[l], ssm_log_step[l], ssm_b_re[l], ssm_b_im[l],
                         ssm_c_re[l], ssm_c_im[l], ssm_d[l], glu_w[l], glu_b[l],
                         diff_lq1[l], diff_lk1[l], diff_lq2[l], diff_lk2[l], diff_subln[l],
                         swa_sinks[l])
    return rms_norm_2(x, final_gain)


_first_inputs_2 = second_inputs


def second_inputs(seed=0):
    import zlib

    import numpy as np

    out = dict(_first_inputs_2(seed))
    spreads = {}
    factors = {'norm_gain': 4.286,
     'ssm_lam_re': 8.0,
     'glu_b': 8.0,
     'diff_lq1': 3.401,
     'diff_lk1': 7.004,
     'diff_lq2': 7.815,
     'diff_lk2': 8.0,
     'diff_subln': 8.0,
     'final_gain': 2.906}
    for name, (base, spread) in spreads.items():
        noise = np.random.default_rng([zlib.crc32(name.encode()), seed]).standard_normal(out[name].shape)
        drawn = base * np.exp(spread * noise) if base else spread * noise
        out[name] = __import__('jax').numpy.asarray(drawn.astype(out[name].dtype))
    for name, factor in factors.items():
        out[name] = (out[name] * factor).astype(out[name].dtype)
    return out


_narrow_inputs_2 = second_inputs


def second_inputs(seed=0):
    out = dict(_narrow_inputs_2(seed))
    wider = {'ssm_lam_re': 12.0,
     'ssm_b_re': 3.08,
     'ssm_c_re': 3.01,
     'glu_b': 12.0,
     'diff_subln': 3.55,
     'swa_sinks': 12.0,
     'final_gain': 3.26}
    for name, times in wider.items():
        mean = out[name].mean()
        out[name] = (mean + times * (out[name] - mean)).astype(out[name].dtype)
    return out


def setup_inputs(seed=0):
    out = dict(first_inputs(seed))
    for name, value in second_inputs(seed + 1).items():
        if name != "x":
            out[name + "_2"] = value
    return out


def reference(
    x, mem, norm_w, w_in, gate_b, a_v_norm_w, a_v_norm_b, a_spatial_w, a_spatial_b, b_q_norm_w,
    b_k_norm_w, rel_bias, mem_norm_w, m_w_kv, m_q_norm_w, m_k_norm_w, proj_a, proj_b, proj_m,
    w_out, c_2, norm_gain_2, ada_w_2, ada_b_2, w_in_2, w_out_2, ssm_lam_re_2, ssm_lam_im_2,
    ssm_log_step_2, ssm_b_re_2, ssm_b_im_2, ssm_c_re_2, ssm_c_im_2, ssm_d_2, glu_w_2, glu_b_2,
    diff_lq1_2, diff_lk1_2, diff_lq2_2, diff_lk2_2, diff_subln_2, swa_sinks_2, final_gain_2,
):
    x = first_block(
        x, mem, norm_w, w_in, gate_b, a_v_norm_w, a_v_norm_b, a_spatial_w, a_spatial_b,
        b_q_norm_w, b_k_norm_w, rel_bias, mem_norm_w, m_w_kv, m_q_norm_w, m_k_norm_w, proj_a,
        proj_b, proj_m, w_out,
    )
    return second_block(
        x, c_2, norm_gain_2, ada_w_2, ada_b_2, w_in_2, w_out_2, ssm_lam_re_2, ssm_lam_im_2,
        ssm_log_step_2, ssm_b_re_2, ssm_b_im_2, ssm_c_re_2, ssm_c_im_2, ssm_d_2, glu_w_2,
        glu_b_2, diff_lq1_2, diff_lk1_2, diff_lq2_2, diff_lk2_2, diff_subln_2, swa_sinks_2,
        final_gain_2,
    )


_drawn_inputs = setup_inputs


def setup_inputs(seed=0):
    import zlib

    import numpy as np

    out = dict(_drawn_inputs(seed))
    spreads = {}
    factors = {'norm_gain_2': 4.228,
     'ssm_lam_re_2': 64.0,
     'ssm_lam_im_2': 13.908,
     'ssm_log_step_2': 4.008,
     'ssm_b_re_2': 3.707,
     'ssm_b_im_2': 34.595,
     'ssm_c_re_2': 3.7,
     'ssm_c_im_2': 30.508,
     'ssm_d_2': 3.159,
     'glu_w_2': 3.814,
     'glu_b_2': 8.0,
     'diff_subln_2': 8.0,
     'swa_sinks_2': 64.0}
    for name, (base, spread) in spreads.items():
        noise = np.random.default_rng([zlib.crc32(name.encode()), seed]).standard_normal(out[name].shape)
        drawn = base * np.exp(spread * noise) if base else spread * noise
        out[name] = __import__('jax').numpy.asarray(drawn.astype(out[name].dtype))
    for name, factor in factors.items():
        out[name] = (out[name] * factor).astype(out[name].dtype)
    return out
```

```python
import math
from contextlib import ExitStack

import numpy as np

import concourse.bass as bass
from concourse import mybir

ALU = mybir.AluOpType
ACT = mybir.ActivationFunctionType
AX_X = mybir.AxisListType.X
F32 = mybir.dt.float32
I32 = mybir.dt.int32
F32R = mybir.dt.float32r

P = 128
D = 1024
S = 1024
KT = D // P
TT = S // P
HALF = 512
EPS = 1e-6
HEAD_AT = (0, 2, 1, 3)
MEM = 256
A_WIDTH = 768
M_WIDTH = 512
SSM_GROUPS = 16
LEVELS = 7
LAM_INIT = 0.8 - 0.6 * math.exp(0.0)


class Core:

    def __init__(self, nc, stack):
        self.nc, self.stack = nc, stack
        self.psum = stack.enter_context(nc.psum_tensor("psum", [P, 8, HALF], F32))
        self.names, self.sems = 0, []

    def sb(self, stack, name, shape, dt=F32):
        self.names += 1
        return stack.enter_context(self.nc.sbuf_tensor(f"{name}_{self.names}", shape, dt))

    def sem(self, name):
        self.names += 1
        self.sems.append(self.nc.alloc_semaphore(f"{name}_{self.names}"))
        return self.sems[-1]

    def clear_semaphores(self):
        self.nc.clear_and_free_semaphores(self.sems)
        self.nc.all_engine_barrier()
        self.sems = []


def bank(core, first, count=2):
    return core.psum[:, first:first + count, :].rearrange("p a b -> p (a b)")


HI, LO = 0, 1
PASSES = ((LO, HI), (HI, LO), (HI, HI))


def product(pe, out, lhs, rhs, tiles, depth=KT):
    for k in tiles:
        for n, (a, b) in enumerate(PASSES):
            last = pe.matmul(out, lhs(a, k), rhs(b, k), start=(k == 0 and n == 0),
                             stop=(k == depth - 1 and n == 2))
    return last


def walk(engine, n, body):
    assert n % 2 == 0 or n == 1
    pairs = (n + 1) // 2
    for u in range(min(n, 2)):
        body(0, u, True, pairs == 1)
    if pairs > 2:
        with engine.Fori(1, pairs - 1) as i:
            for u in range(2):
                body(i, u, False, False)
    if pairs > 1:
        for u in range(2):
            body(pairs - 1, u, False, True)


class SplitTiles:

    def __init__(self, core, stack, n, tile, pieces=1):
        self.n, self.tile, self.pieces = n, tile, pieces
        self.raw = core.sb(stack, "w_raw", [P, KT, P])
        self.parts = core.sb(stack, "w_parts", [P, 2, 2, KT, P], F32R)
        self.loaded = core.sem("w_loaded")
        self.high = core.sem("w_high")
        self.low = core.sem("w_low")

    def load(self, sp, i, u, first, last=False):
        if not (first and u == 0):
            sp.wait_ge(self.low, 2 * i + u)
        if self.pieces == 1:
            sp.dma_start(self.raw[:, :, :], self.tile(2 * i + u)).then_inc(self.loaded, 16)
        else:
            for m, part in enumerate(self.tile(2 * i + u)):
                a = P // self.pieces
                sp.dma_start(self.raw[:, :, m * a:(m + 1) * a], part).then_inc(self.loaded, 16)

    def split_high(self, act, i, u):
        act.wait_ge(self.loaded, 16 * self.pieces * (2 * i + (u + 1)))
        act.copy(self.parts[:, u, HI, :, :], self.raw[:, :, :]).then_inc(self.high, 1)

    def split_low(self, dve, i, u):
        dve.wait_ge(self.high, 2 * i + (u + 1))
        dve.tensor_tensor(self.parts[:, u, LO, :, :], self.raw[:, :, :],
                          self.parts[:, u, HI, :, :].bitcast(F32), ALU.subtract).then_inc(self.low, 1)

    def first_high(self, act):
        for u in range(min(self.n, 2)):
            self.split_high(act, 0, u)

    def first_low(self, dve):
        for u in range(min(self.n, 2)):
            self.split_low(dve, 0, u)

    def ready(self, pe, i, u):
        pe.wait_ge(self.low, 2 * i + (u + 1))

    def lhs(self, u):
        return lambda part, k: self.parts[:, u, part, k, :]


class SplitMatrix:

    def __init__(self, core, stack, weights, ncols):
        self.weights, self.ncols = weights, ncols
        self.raw = core.sb(stack, "w_raw", [P, 2, ncols])
        self.parts = core.sb(stack, "w_parts", [P, 2, KT, ncols], F32R)
        self.loaded = [core.sem("w_loaded") for _ in range(2)]
        self.high = core.sem("w_high")
        self.low = core.sem("w_low")

    def load(self, sp):
        for k in range(KT):
            if k >= 2:
                sp.wait_ge(self.low, k - 1)
            sp.dma_start(self.raw[:, k % 2, :], self.weights[:, k, :]).then_inc(self.loaded[k % 2], 16)

    def split_high(self, act):
        for k in range(KT):
            act.wait_ge(self.loaded[k % 2], 16 * (k // 2 + 1))
            act.copy(self.parts[:, HI, k, :], self.raw[:, k % 2, :]).then_inc(self.high, 1)

    def split_low(self, dve):
        for k in range(KT):
            dve.wait_ge(self.high, k + 1)
            dve.tensor_tensor(self.parts[:, LO, k, :], self.raw[:, k % 2, :],
                              self.parts[:, HI, k, :].bitcast(F32), ALU.subtract).then_inc(self.low, 1)

    def products(self, pe, first, outs, lhs, c0s, width):
        for k in range(KT):
            if first:
                pe.wait_ge(self.low, k + 1)
            for out, c0 in zip(outs, c0s):
                last = product(pe, out, lhs, lambda part, j: self.parts[:, part, j, c0:c0 + width], [k])
        return last


def tile_of(ap, j):
    return ap[:, bass.ds(j, 1), :].rearrange("p j t -> p (j t)")


def stage_constants(core, const_dram, cols_dram, const, cols):
    nc = core.nc
    loaded = core.sem("const_loaded")
    with nc.Block(no_gpsimd_drain=True) as block:

        @block.sync
        def _(sp):
            sp.dma_start(const[:, :], const_dram).then_inc(loaded, 16)
            sp.dma_start(cols[:, :], cols_dram).then_inc(loaded, 16)
            sp.wait_ge(loaded, 32)

        @block.vector
        def _(dve):
            dve.wait_ge(loaded, 32)
            for name, factor in (("bqk", 64 ** -0.5), ("mq", 128 ** -0.5)):
                a, b = COL[name][0], COL[name][0] + (6 if name == "bqk" else 4)
                dve.tensor_scalar(cols[:, a:b], cols[:, a:b], factor, None, ALU.mult)


def stage_norm_transpose(core, tiles, src, gain, shift, dst, ident, eps, from_sbuf=False):
    nc = core.nc
    with ExitStack() as stack:
        xin = None if from_sbuf else core.sb(stack, "xin", [P, 2, D])
        sq = core.sb(stack, "sq", [P, D])
        xn = core.sb(stack, "xn", [P, 2, D])
        whole = core.sb(stack, "xn_turned", [P, 2, KT, P])
        ssq = core.sb(stack, "ssq", [P, tiles])
        std = core.sb(stack, "std", [P, tiles])
        rstd = core.sb(stack, "rstd", [P, tiles])
        x_loaded = [core.sem("x_loaded") for _ in range(2)]
        summed = core.sem("norm_summed")
        rooted = core.sem("norm_rooted")
        inverted = core.sem("norm_inverted")
        scaled = core.sem("norm_scaled")
        turned = core.sem("norm_turned")
        moved = core.sem("norm_moved")
        shifted = core.sem("norm_shifted")
        high = core.sem("norm_high")
        low = core.sem("norm_low")
        rows = [(src[:, t, :] if from_sbuf else xin[:, t % 2, :]) for t in range(tiles)]

        with nc.Block(no_gpsimd_drain=True) as block:

            @block.sync
            def _(sp):
                if from_sbuf:
                    return
                for t in range(tiles):
                    if t >= 2:
                        sp.wait_ge(scaled, t - 1)
                        sp.wait_ge(summed, t - 1)
                    sp.dma_start(rows[t], src[t]).then_inc(x_loaded[t % 2], 16)

            def split(act, t):
                act.wait_ge(moved if shift is None else shifted, t + 1)
                act.copy(dst[:, HI, :, t * P:(t + 1) * P], whole[:, t % 2, :, :]).then_inc(high, 1)

            @block.scalar
            def _(act):
                for t in range(tiles):
                    if not from_sbuf:
                        act.wait_ge(x_loaded[t % 2], 16 * (t // 2 + 1))
                    if t >= 1:
                        act.wait_ge(summed, t)
                    act.activation(sq[:, :], rows[t], ACT.Square,
                                   accum_out=ssq[:, t:t + 1]).then_inc(summed, 1)
                    act.wait_ge(summed, t + 1)
                    act.activation(std[:, t:t + 1], ssq[:, t:t + 1], ACT.Sqrt,
                                   bias=eps[:, 0:1], scale=1.0 / D).then_inc(rooted, 1)
                    if t >= 2:
                        split(act, t - 2)
                split(act, tiles - 2)
                split(act, tiles - 1)

            def lower(dve, t):
                dve.wait_ge(high, t + 1)
                dve.tensor_tensor(dst[:, LO, :, t * P:(t + 1) * P], whole[:, t % 2, :, :],
                                  dst[:, HI, :, t * P:(t + 1) * P].bitcast(F32), ALU.subtract).then_inc(low, 1)
                dve.wait_ge(low, t + 1)

            def move(dve, t):
                dve.wait_ge(turned, t + 1)
                part = whole[:, t % 2, :, :]
                if t >= 2:
                    lower(dve, t - 2)
                dve.tensor_tensor(part, bank(core, 2 * (t % 2)).rearrange("p (k s) -> p k s", k=KT),
                                  gain.unsqueeze(2).to_broadcast([P, KT, P]), ALU.mult).then_inc(moved, 1)
                if shift is not None:
                    dve.wait_ge(moved, t + 1)
                    dve.tensor_tensor(part, part, shift.unsqueeze(2).to_broadcast([P, KT, P]),
                                      ALU.add).then_inc(shifted, 1)

            @block.vector
            def _(dve):
                for t in range(tiles):
                    dve.wait_ge(rooted, t + 1)
                    dve.reciprocal(rstd[:, t:t + 1], std[:, t:t + 1]).then_inc(inverted, 1)
                    dve.wait_ge(inverted, t + 1)
                    if t >= 2:
                        dve.wait_ge(turned, t - 1)
                    dve.tensor_scalar(xn[:, t % 2, :], rows[t], rstd[:, t:t + 1], None,
                                      ALU.mult).then_inc(scaled, 1)
                    if t >= 1:
                        move(dve, t - 1)
                move(dve, tiles - 1)
                lower(dve, tiles - 2)
                lower(dve, tiles - 1)

            @block.tensor
            def _(pe):
                for t in range(tiles):
                    pe.wait_ge(scaled, t + 1)
                    if t >= 2:
                        pe.wait_ge(moved, t - 1)
                    for k in range(KT):
                        last = pe.transpose(bank(core, 2 * (t % 2))[:, k * P:(k + 1) * P],
                                            xn[:, t % 2, k * P:(k + 1) * P], ident)
                    last.then_inc(turned, 1)


def stage_heads(core, n, src, tokens, weight_tile, same, scale, norm_col, dst, eps, room=None):
    nc = core.nc
    width = min(tokens, HALF)
    halves = [slice(h * width, (h + 1) * width) for h in range(tokens // width)]
    early = 4
    with ExitStack() as stack:
        w = SplitTiles(core, stack, n, weight_tile)
        if room is None:
            room = core.sb(stack, "squares_roots", [P, 2, tokens])
        sq, rs = room[:, 0, :], room[:, 1, :]
        projected = core.sem("projected")
        squared = core.sem("squared")
        summed = core.sem("summed")
        rooted = core.sem("rooted")
        inverted = core.sem("inverted")
        normed = core.sem("normed")

        def dense(u):
            return bank(core, 2 * u)[:, 0:tokens]

        sums = bank(core, 4)[:, 0:tokens]

        with nc.Block(no_gpsimd_drain=True) as block:

            @block.sync
            def _(sp):
                walk(sp, n, lambda *at: w.load(sp, *at))

            @block.tensor
            def _(pe):
                def sum_squares(i, u, second):
                    pe.wait_ge(squared, 2 * i + u)
                    if not second:
                        pe.wait_ge(rooted, 2 * i + (u - 1))
                    for h in halves:
                        last = pe.matmul(sums[:, h], same, sq[:, h], start=True, stop=True)
                    last.then_inc(summed, 1)

                def tile(i, u, first, last):
                    w.ready(pe, i, u)
                    if not first:
                        pe.wait_ge(normed, 2 * i + (u - 1))
                    for m, h in enumerate(halves):
                        for tiles in (range(early), range(early, KT)):
                            done = product(pe, dense(u)[:, h], w.lhs(u), lambda part, k: src[:, part, k, h], tiles)
                            if m == 0 and tiles[0] == 0 and not (first and u == 0):
                                sum_squares(i, u, first)
                    done.then_inc(projected, 1)

                walk(pe, n, tile)
                sum_squares(n // 2, 0, False)

            @block.scalar
            def _(act):
                def tile(i, u, first, last):
                    act.wait_ge(projected, 2 * i + (u + 1))
                    if not (first and u == 0):
                        act.wait_ge(summed, 2 * i + u)
                    act.activation(sq[:, :], dense(u), ACT.Square).then_inc(squared, 1)
                    if not last:
                        w.split_high(act, i + 1, u)
                    act.wait_ge(summed, 2 * i + (u + 1))
                    if not (first and u == 0):
                        act.wait_ge(normed, 2 * i + u)
                    act.activation(rs[:, :], sums, ACT.Sqrt, bias=eps[:, 0:1],
                                   scale=scale).then_inc(rooted, 1)

                w.first_high(act)
                walk(act, n, tile)

            @block.vector
            def _(dve):
                def tile(i, u, first, last):
                    if not last:
                        w.split_low(dve, i + 1, u)
                    dve.wait_ge(rooted, 2 * i + (u + 1))
                    dve.reciprocal(rs[:, :], rs[:, :]).then_inc(inverted, 1)
                    dve.wait_ge(inverted, 2 * i + (u + 1))
                    dve.scalar_tensor_tensor(out=tile_of(dst, 2 * i + u),
                                             in0=dense(u), scalar=norm_col(2 * i + u),
                                             in1=rs[:, :], op0=ALU.mult, op1=ALU.mult).then_inc(normed, 1)

                w.first_low(dve)
                walk(dve, n, tile)


def stage_rows(core, src_units, weights, ncols):
    nc = core.nc
    with ExitStack() as stack:
        w = SplitMatrix(core, stack, weights, ncols)
        made = core.sem("rows_made")
        kept = [core.sem("rows_kept_dve"), core.sem("rows_kept_act")]

        with nc.Block(no_gpsimd_drain=True) as block:

            @block.sync
            def _(sp):
                w.load(sp)

            @block.tensor
            def _(pe):
                for n, (lhs, c0, width, _) in enumerate(src_units):
                    if n >= 4:
                        pe.wait_ge(kept[n % 2], n // 2 - 1)
                    w.products(pe, n == 0, [bank(core, n % 4, 1)[:, 0:width]], lhs, [c0],
                               width).then_inc(made, 1)

            @block.vector
            def _(dve):
                w.split_low(dve)
                for n, (_, _, width, dst) in enumerate(src_units):
                    if n % 2 == 0:
                        dve.wait_ge(made, n + 1)
                        dve.tensor_copy(dst, bank(core, n % 4, 1)[:, 0:width]).then_inc(kept[0], 1)

            @block.scalar
            def _(act):
                w.split_high(act)
                for n, (_, _, width, dst) in enumerate(src_units):
                    if n % 2 == 1:
                        act.wait_ge(made, n + 1)
                        act.copy(dst, bank(core, n % 4, 1)[:, 0:width]).then_inc(kept[1], 1)


def stage_features(core, n, src, weight_tile, func, dst_tile, scale=1.0, times=None, pieces=1, order=None, save=None):
    nc = core.nc
    order = order or (lambda a: a)
    with ExitStack() as stack:
        w = SplitTiles(core, stack, n, weight_tile, pieces)
        held = core.sb(stack, "held", [P, 2, S]) if times else None
        projected = core.sem("projected")
        mapped = core.sem("mapped")
        gated = core.sem("gated")
        saved = core.sem("features_saved") if save else None

        with nc.Block(no_gpsimd_drain=True) as block:

            @block.sync
            def _(sp):
                walk(sp, n, lambda *at: w.load(sp, *at))
                if save:
                    sp.wait_ge(mapped, n)
                    for there, made in save:
                        sp.dma_start(there, made).then_inc(saved, 16)
                    sp.wait_ge(saved, 16 * len(save))

            @block.tensor
            def _(pe):
                def project(i, u, first, last):
                    w.ready(pe, i, u)
                    if not first:
                        pe.wait_ge(mapped, 2 * i + (u - 1))
                    for h in range(2):
                        done = product(pe, bank(core, 2 * u + h, 1), w.lhs(u),
                                       lambda part, k: src[:, part, k, h * HALF:(h + 1) * HALF], range(KT))
                    done.then_inc(projected, 1)

                walk(pe, n, project)

            @block.scalar
            def _(act):
                def apply(i, u, first, last):
                    j = 2 * i + u
                    act.wait_ge(projected, j + 1)
                    if not last:
                        w.split_high(act, i + 1, u)
                    if times and not first:
                        act.wait_ge(gated, j - 1)
                    act.activation(held[:, u, :] if times else dst_tile(j), order(bank(core, 2 * u)), func,
                                   scale=scale).then_inc(mapped, 1)

                w.first_high(act)
                walk(act, n, apply)

            @block.vector
            def _(dve):
                def gate(i, u, first, last):
                    if not last:
                        w.split_low(dve, i + 1, u)
                    if times:
                        j = 2 * i + u
                        dve.wait_ge(mapped, j + 1)
                        dve.tensor_tensor(dst_tile(j), times(j), held[:, u, :], ALU.mult).then_inc(gated, 1)

                w.first_low(dve)
                walk(dve, n, gate)


def stage_bias_tables(core, rel, onehot_dram, scratch, back, table, table16):
    nc = core.nc
    with ExitStack() as stack:
        hot = core.sb(stack, "onehot", [33, 3, 384])
        rb = core.sb(stack, "rel", [33, 12])
        rows = core.sb(stack, "bias_rows", [4, 3, 384])
        loaded = core.sem("onehot_loaded")
        made = core.sem("bias_made")
        copied = core.sem("bias_copied")
        saved = core.sem("bias_saved")
        spread = core.sem("bias_spread")
        with nc.Block(no_gpsimd_drain=True) as block:

            @block.sync
            def _(sp):
                sp.dma_start(hot[:, :, :], onehot_dram).then_inc(loaded, 16)
                sp.dma_start(rb[:, :], rel).then_inc(loaded, 16)
                sp.wait_ge(copied, 3)
                sp.dma_start(scratch.rearrange("g h x -> h g x"), rows[:, :, :]).then_inc(saved, 16)
                sp.wait_ge(saved, 16)
                for g in range(3):
                    width = 256 if g < 2 else P
                    src = bass.AP(scratch.tensor, g * 4 * 384, [[1, P], [384, 4], [1, width]])
                    sp.dma_start(back[:, 4 * g:4 * g + 4, 0:width], src).then_inc(spread, 16)

            @block.tensor
            def _(pe):
                pe.wait_ge(loaded, 32)
                for g in range(3):
                    pe.matmul(bank(core, g, 1)[0:4, 0:384], rb[:, 4 * g:4 * g + 4], hot[:, g, :],
                              start=True, stop=True).then_inc(made, 1)

            @block.vector
            def _(dve):
                for g in range(3):
                    dve.wait_ge(made, g + 1)
                    dve.tensor_copy(rows[:, g, :], bank(core, g, 1)[0:4, 0:384]).then_inc(copied, 1)
                dve.wait_ge(spread, 48)
                dve.tensor_copy(table, back[:, 0:8, ::-1])
                dve.tensor_copy(table16, back[:, 8:12, 127::-1])


def stage_attention(core, units, ident, width_max=256):
    nc = core.nc
    n = len(units)
    with ExitStack() as stack:
        p = core.sb(stack, "p", [P, 2, 4, 256])
        pT = core.sb(stack, "pT", [P, 2, 1024])
        top = core.sb(stack, "top", [P, 2, 4])
        low = core.sb(stack, "low", [P, 2, 4])
        total = core.sb(stack, "total", [P, 2, 4])
        inv = core.sb(stack, "inv", [P, 2, 4])
        extra = core.sb(stack, "extra", [P, 2, 4])
        scored = core.sem("scored")
        maxed = core.sem("maxed")
        small = core.sem("small_steps")
        exped = core.sem("exped")
        weighted = core.sem("weighted")
        turned = core.sem("turned")
        moved_act = core.sem("moved_act")
        moved_dve = core.sem("moved_dve")
        mixed = core.sem("mixed")
        stored = core.sem("stored")
        sinked = core.sem("sinked")
        steps = [0]

        def S_(u):
            return bank(core, 2 * (u % 2)).rearrange("p (h w) -> p h w", h=4)

        def T_():
            return bank(core, 4)

        def O_(u):
            return bank(core, 6 + u % 2, 1)

        with nc.Block(no_gpsimd_drain=True) as block:

            @block.tensor
            def _(pe):
                def scores(u):
                    d = units[u]
                    if u >= 2:
                        pe.wait_ge(maxed, u - 1)
                        pe.wait_ge(exped, u - 1)
                    for h in range(4):
                        last = pe.matmul(S_(u)[:, h, 0:d["width"]], d["q"][h], d["k"][h],
                                         start=True, stop=True)
                    last.then_inc(scored, 1)

                def turn(u):
                    d = units[u]
                    blocks = d["width"] // P
                    pe.wait_ge(weighted, u + 1) if d["keep"] is None else pe.wait_ge(exped, u + 1)
                    if u >= 1:
                        pe.wait_ge(moved_act, u)
                        pe.wait_ge(moved_dve, u)
                    for h in range(4):
                        for b in range(blocks):
                            last = pe.transpose(T_()[:, (2 * h + b) * P:(2 * h + b + 1) * P],
                                                p[:, u % 2, h, b * P:(b + 1) * P], ident)
                    last.then_inc(turned, 1)

                def mix(u):
                    d = units[u]
                    blocks = d["width"] // P
                    pe.wait_ge(moved_act, u + 1)
                    pe.wait_ge(moved_dve, u + 1)
                    if u >= 2:
                        pe.wait_ge(stored, u - 1)
                    for h in range(4):
                        for b in range(blocks):
                            last = pe.matmul(d["out"](h, O_(u)), d["values"](h, b),
                                             pT[:, u % 2, (2 * h + b) * P:(2 * h + b + 1) * P],
                                             start=(b == 0), stop=(b == blocks - 1))
                    last.then_inc(mixed, 1)

                for u in range(n + 2):
                    if u < n:
                        scores(u)
                    if 1 <= u <= n:
                        turn(u - 1)
                    if u >= 2:
                        mix(u - 2)

            @block.vector
            def _(dve):
                def step(ins):
                    steps[0] += 1
                    ins.then_inc(small, 1)
                    dve.wait_ge(small, steps[0])

                def maxima(u):
                    d = units[u]
                    s = u % 2
                    m = d["keep"][0] if d["keep"] else top[:, s, :]
                    dve.wait_ge(scored, u + 1)
                    if u >= 2:
                        dve.wait_ge(turned, u - 1)
                    if d["bias"] is None:
                        step(dve.tensor_reduce(m, S_(u)[:, :, 0:d["width"]], AX_X, ALU.max))
                    else:
                        for h in range(4):
                            last = dve.tensor_tensor_reduce(
                                p[:, s, h, 0:d["width"]], S_(u)[:, h, 0:d["width"]], d["bias"][h],
                                1.0, -3e38, ALU.add, ALU.max, m[:, h:h + 1])
                        step(last)
                    if d["sink"] is not None:
                        step(dve.tensor_tensor(m, m, d["sink"], ALU.max))
                        step(dve.tensor_tensor(extra[:, s, :], d["sink"], m, ALU.subtract))
                    dve.tensor_scalar(low[:, s, :], m, -1.0, None, ALU.mult).then_inc(maxed, 1)

                def weights(u):
                    d = units[u]
                    s = u % 2
                    if d["keep"]:
                        return
                    dve.wait_ge(exped, u + 1)
                    if d["sink"] is not None:
                        step(dve.tensor_tensor(total[:, s, :], total[:, s, :], extra[:, s, :], ALU.add))
                    step(dve.reciprocal(inv[:, s, :], total[:, s, :]))
                    for h in range(4):
                        w = p[:, s, h, 0:d["width"]]
                        last = dve.tensor_scalar(w, w, inv[:, s, h:h + 1], None, ALU.mult)
                    last.then_inc(weighted, 1)

                def move(u):
                    d = units[u]
                    dve.wait_ge(turned, u + 1)
                    if u >= 2:
                        dve.wait_ge(mixed, u - 1)
                    view = lambda a: a[:, 512:1024].rearrange("p (h w) -> p h w", h=2)[:, :, 0:d["width"]]
                    dve.tensor_copy(view(pT[:, u % 2, :]), view(T_())).then_inc(moved_dve, 1)

                def store(u):
                    dve.wait_ge(mixed, u + 1)
                    dst, view = units[u]["store"]
                    if units[u]["keep"]:
                        dve.tensor_copy(dst, view(O_(u))).then_inc(stored, 1)
                    else:
                        dve.tensor_tensor(dst, view(O_(u)), dst, ALU.mult).then_inc(stored, 1)

                for u in range(n + 3):
                    if 2 <= u < n + 2:
                        move(u - 2)
                    if 1 <= u <= n:
                        weights(u - 1)
                    if u < n:
                        maxima(u)
                    if u >= 3:
                        store(u - 3)

            @block.scalar
            def _(act):
                def move(u):
                    d = units[u]
                    act.wait_ge(turned, u + 1)
                    if u >= 2:
                        act.wait_ge(mixed, u - 1)
                    view = lambda a: a[:, 0:512].rearrange("p (h w) -> p h w", h=2)[:, :, 0:d["width"]]
                    act.copy(view(pT[:, u % 2, :]), view(T_())).then_inc(moved_act, 1)

                def exps(u):
                    d = units[u]
                    s = u % 2
                    sums = d["keep"][1] if d["keep"] else total[:, s, :]
                    act.wait_ge(maxed, u + 1)
                    if u >= 2 and not d["keep"]:
                        act.wait_ge(weighted, u - 1)
                    if d["sink"] is not None:
                        act.activation(extra[:, s, :], extra[:, s, :], ACT.Exp)
                    for h in range(4):
                        into = p[:, s, h, 0:d["width"]]
                        src = S_(u)[:, h, 0:d["width"]] if d["bias"] is None else into
                        last = act.activation(into, src, ACT.Exp, bias=low[:, s, h:h + 1],
                                              accum_out=sums[:, h:h + 1])
                    last.then_inc(exped, 1)

                for u in range(n + 2):
                    if u >= 2:
                        move(u - 2)
                    if u < n:
                        exps(u)


def in_order(ap, g, t):
    if g == 0:
        return ap[:, t * P:(t + 1) * P]
    if g == 1:
        return ap.rearrange("p (l r) -> p r l", r=4)[:, t // 2, (t % 2) * P:(t % 2 + 1) * P]
    return ap.rearrange("p (l r) -> p r l", r=8)[:, t, :]


def window_units(qkT, v, oT, table, table16, maxima, sums):
    units = []
    for g in range(3):
        for t in range(TT):
            before = (g == 0 and t > 0) or (g == 1 and t % 2 == 1)
            width = 256 if before else 128
            q, k, bias = [], [], []
            for h in HEAD_AT:
                rows = slice(64 * (h % 2), 64 * (h % 2) + 64)
                q.append(in_order(qkT[rows, 2 * g + h // 2, :], g, t))
                kk = qkT[rows, 6 + 2 * g + h // 2, :]
                if not before:
                    k.append(in_order(kk, g, t))
                elif g == 0:
                    k.append(kk[:, (t - 1) * P:(t + 1) * P])
                else:
                    k.append(kk.rearrange("p (l r) -> p r l", r=4)[:, t // 2, :])
                bias.append(table16[:, h, :] if g == 2 else table[:, 4 * g + h, 256 - width:256])
            at = 4 * (g * TT + t)

            def values(n, b, g=g, t=t, before=before):
                h = HEAD_AT[n]
                return v[:, t - 1 + b if before else t, g, 64 * h:64 * h + 64]

            def out(n, o):
                h = HEAD_AT[n]
                return o[64 * (h % 2):64 * (h % 2) + 64, (h // 2) * P:(h // 2 + 1) * P]

            o = oT[:, g, :, :]
            if g == 0:
                dst = o[:, :, t * P:(t + 1) * P]
                view = lambda b: b[:, 0:256].rearrange("p (h q) -> p h q", h=2)
            elif g == 1:
                dst = o.rearrange("p h (l r) -> p h r l", r=4)[:, :, t // 2, (t % 2) * P:(t % 2 + 1) * P]
                view = lambda b: b[:, 0:256].rearrange("p (h q) -> p h q", h=2)
            else:
                dst = o.rearrange("p h (l r) -> p h r l", r=8)[:, :, t, :]
                view = lambda b: b[:, 0:256].rearrange("p (h q) -> p h q", h=2)
            units.append(dict(width=width, q=q, k=k, bias=bias, sink=None, values=values, out=out,
                              store=(dst, view), keep=(maxima[:, at:at + 4], sums[:, at:at + 4])))
    return units


def stage_combine(core, maxima, sums, oT, ybT, ident, sel):
    nc = core.nc
    with ExitStack() as stack:
        rows = core.sb(stack, "lse_rows", [4, 2, 3, S])
        top = core.sb(stack, "lse_top", [4, S])
        prod = core.sb(stack, "prod", [P, S])
        acc = core.sb(stack, "weighed_sum", [P, S])
        turned = core.sem("lse_turned")
        moved = core.sem("lse_moved")
        chain = core.sem("lse_chain")
        topped = core.sem("lse_topped")
        exped = core.sem("lse_exped")
        ready = core.sem("lse_ready")
        spread = core.sem("lse_spread")
        used = core.sem("lse_used")
        m = rows[:, 0, :, :]
        l = rows[:, 1, :, :]
        with nc.Block(no_gpsimd_drain=True) as block:

            @block.tensor
            def _(pe):
                for n in range(6):
                    w, g = n // 3, n % 3
                    if n >= 2:
                        pe.wait_ge(moved, n - 1)
                    for t in range(TT):
                        src = (maxima, sums)[w][:, 4 * (g * TT + t):4 * (g * TT + t) + 4]
                        last = pe.transpose(bank(core, 2 * (n % 2))[0:4, t * P:(t + 1) * P], src, ident)
                    last.then_inc(turned, 1)
                pe.wait_ge(ready, 1)
                for n in range(6):
                    pair, g = n // 3, n % 3
                    if n >= 2:
                        pe.wait_ge(used, n - 1)
                    for h in range(2):
                        last = pe.matmul(bank(core, 4 + 2 * (n % 2) + h, 1), sel[0:4, pair * P:(pair + 1) * P],
                                         m[:, g, h * HALF:(h + 1) * HALF], start=True, stop=True)
                    last.then_inc(spread, 1)

            @block.vector
            def _(dve):
                done = [0]

                def step(ins):
                    done[0] += 1
                    ins.then_inc(chain, 1)
                    dve.wait_ge(chain, done[0])

                for n in range(6):
                    w, g = n // 3, n % 3
                    dve.wait_ge(turned, n + 1)
                    r = (1, 4, 8)[g]
                    dst = rows[:, w, g, :].rearrange("p (l r) -> p r l", r=r)
                    dve.tensor_copy(dst, bank(core, 2 * (n % 2))[0:4, :].rearrange("p (r l) -> p r l", r=r))\
                       .then_inc(moved, 1)
                dve.wait_ge(moved, 6)
                step(dve.tensor_tensor(top[:, :], m[:, 0, :], m[:, 1, :], ALU.max))
                step(dve.tensor_tensor(top[:, :], top[:, :], m[:, 2, :], ALU.max))
                for g in range(3):
                    last = dve.tensor_tensor(m[:, g, :], m[:, g, :], top[:, :], ALU.subtract)
                last.then_inc(topped, 1)
                dve.wait_ge(exped, 1)
                step(dve.tensor_tensor(l, l, m, ALU.mult))
                step(dve.tensor_tensor(top[:, :], l[:, 0, :], l[:, 1, :], ALU.add))
                step(dve.tensor_tensor(top[:, :], top[:, :], l[:, 2, :], ALU.add))
                step(dve.reciprocal(top[:, :], top[:, :]))
                for g in range(3):
                    last = dve.tensor_tensor(m[:, g, :], m[:, g, :], top[:, :], ALU.mult)
                last.then_inc(ready, 1)
                for n in range(6):
                    pair, g = n // 3, n % 3
                    dve.wait_ge(spread, n + 1)
                    y = acc[:, :]
                    dst = y if g == 0 else prod[:, :]
                    dve.tensor_tensor(dst, bank(core, 4 + 2 * (n % 2)), oT[:, g, pair, :],
                                      ALU.mult).then_inc(used, 1)
                    if g > 0:
                        dve.wait_ge(used, n + 1)
                        step(dve.tensor_tensor(y, y, prod[:, :], ALU.add))
                    if g == 2:
                        step(dve.tensor_tensor(ybT[:, pair, :], ybT[:, pair, :], y, ALU.mult))

            @block.scalar
            def _(act):
                act.wait_ge(topped, 1)
                act.activation(m, m, ACT.Exp).then_inc(exped, 1)


def stage_gated_values(core, src, weights, wide_dram, wide, vv, eps):
    nc = core.nc
    width = A_WIDTH // 2
    with ExitStack() as stack:
        w = SplitMatrix(core, stack, weights, A_WIDTH)
        act_v = w.raw
        sq = bank(core, 4)[:, 0:A_WIDTH]
        part = core.sb(stack, "ln_part", [P, 2, 2])
        mean = core.sb(stack, "ln_mean", [P, 2])
        ssq = core.sb(stack, "ln_ssq", [P, 2])
        rstd = core.sb(stack, "ln_rstd", [P, 2])
        wide_loaded = core.sem("ln_rows_loaded")
        made = core.sem("values_made")
        mapped = core.sem("values_mapped")
        squared = core.sem("values_squared")
        rooted = core.sem("values_rooted")
        done = core.sem("values_done")
        chain = core.sem("values_chain")

        with nc.Block(no_gpsimd_drain=True) as block:

            @block.sync
            def _(sp):
                sp.dma_start(wide[:, :, :], wide_dram).then_inc(wide_loaded, 16)
                w.load(sp)

            @block.tensor
            def _(pe):
                for t in range(TT):
                    if t >= 2:
                        pe.wait_ge(mapped, t - 1)
                    w.products(pe, t == 0, [bank(core, 2 * (t % 2) + h, 1)[:, 0:width] for h in range(2)],
                               lambda part, k: src[:, part, k, t * P:(t + 1) * P], [0, width],
                               width).then_inc(made, 1)

            @block.scalar
            def _(act):
                def gelu(t):
                    act.wait_ge(made, t + 1)
                    if t >= 2:
                        act.wait_ge(done, t - 1)
                    for h in range(2):
                        last = act.activation(act_v[:, t % 2, h * width:(h + 1) * width],
                                              bank(core, 2 * (t % 2) + h, 1)[:, 0:width], ACT.Gelu,
                                              accum_out=part[:, t % 2, h:h + 1])
                    last.then_inc(mapped, 1)

                def root(t):
                    act.wait_ge(squared, t + 1)
                    act.activation(rstd[:, t % 2:t % 2 + 1], ssq[:, t % 2:t % 2 + 1], ACT.Sqrt,
                                   bias=eps[:, 0:1], scale=1 / A_WIDTH).then_inc(rooted, 1)

                w.split_high(act)
                act.wait_ge(w.low, KT)
                for t in range(TT + 1):
                    if t < TT:
                        gelu(t)
                    if t >= 1:
                        root(t - 1)

            @block.vector
            def _(dve):
                steps = [0]

                def step(ins):
                    steps[0] += 1
                    ins.then_inc(chain, 1)
                    dve.wait_ge(chain, steps[0])

                w.split_low(dve)
                for t in range(TT):
                    s = t % 2
                    dve.wait_ge(mapped, t + 1)
                    dve.wait_ge(wide_loaded, 16)
                    step(dve.tensor_tensor(mean[:, s:s + 1], part[:, s, 0:1], part[:, s, 1:2], ALU.add))
                    step(dve.tensor_scalar(mean[:, s:s + 1], mean[:, s:s + 1], 1 / A_WIDTH, None, ALU.mult))
                    x = act_v[:, s, :]
                    step(dve.tensor_scalar(x, x, mean[:, s:s + 1], None, ALU.subtract))
                    dve.tensor_tensor_reduce(sq[:, :], x, x, 1.0, 0.0, ALU.mult, ALU.add,
                                             ssq[:, s:s + 1]).then_inc(squared, 1)
                    dve.wait_ge(rooted, t + 1)
                    step(dve.reciprocal(rstd[:, s:s + 1], rstd[:, s:s + 1]))
                    step(dve.scalar_tensor_tensor(out=vv[:, t, :], in0=x, scalar=rstd[:, s:s + 1],
                                                  in1=wide[:, 0, :], op0=ALU.mult, op1=ALU.mult))
                    dve.tensor_tensor(vv[:, t, :], vv[:, t, :], wide[:, 1, :], ALU.add).then_inc(done, 1)


def stage_merge(core, hT, ys, gate_tile, proj_tiles, gate_b, mergedT):
    nc = core.nc
    depth = [y[1] for y in ys]
    with ExitStack() as stack:
        w = SplitTiles(core, stack, 24, None)
        wp = core.sb(stack, "w_proj", [P, 2, 6, P])
        gate = core.sb(stack, "gate", [P, 2, S])
        prod = core.sb(stack, "gated", [P, 2, S])
        loaded = [core.sem("merge_loaded") for _ in range(2)]
        made = core.sem("merge_made")
        opened = core.sem("merge_opened")
        used = core.sem("merge_used")
        summed = core.sem("merge_summed")

        def unit(i, n):
            return 2 * i + n // 3, n % 3, n % 2, 6 * i + n

        def sixes(engine, body):
            for n in range(6):
                body(0, n, n < 2, False)
            with engine.Fori(1, 3) as i:
                for n in range(6):
                    body(i, n, False, False)
            for n in range(6):
                body(3, n, False, n >= 4)

        def next_split(split, engine, i, n):
            split(engine, 3 * i + (n // 2 + 1), n % 2)

        with nc.Block(no_gpsimd_drain=True) as block:

            @block.sync
            def _(sp):
                def load_projection(i, n):
                    j, b, s, u = unit(i, n)
                    sp.dma_start(wp[:, s, 0:depth[b], :], proj_tiles[b](j)).then_inc(loaded[s], 16)

                def load(i, n, first, last):
                    j, b, s, u = unit(i, n)
                    if not (first and n == 0):
                        sp.wait_ge(w.low, u)
                    sp.dma_start(w.raw[:, :, :], gate_tile(b, j)).then_inc(w.loaded, 16)
                    if not (first and n == 0):
                        load_projection(i if n else i - 1, n - 1 if n else 5)

                sixes(sp, load)
                sp.wait_ge(w.low, 24)
                load_projection(3, 5)

            @block.tensor
            def _(pe):
                def products(i, n, first, last):
                    j, b, s, u = unit(i, n)
                    w.ready(pe, 3 * i + n // 2, s)
                    if not first:
                        pe.wait_ge(used, u - 1)
                    for h in range(2):
                        product(pe, bank(core, 4 * s + h, 1), w.lhs(s),
                                lambda part, k: hT[:, part, k, h * HALF:(h + 1) * HALF], range(KT))
                    pe.wait_ge(loaded[s], 48 * i + 16 * (n // 2) + 16)
                    for h in range(2):
                        for k in range(depth[b]):
                            last = pe.matmul(bank(core, 4 * s + 2 + h, 1), wp[:, s, k, :],
                                             ys[b][0][:, k, h * HALF:(h + 1) * HALF],
                                             start=(k == 0), stop=(k == depth[b] - 1))
                    last.then_inc(made, 1)

                sixes(pe, products)

            @block.scalar
            def _(act):
                def sigmoid(i, n, first, last):
                    j, b, s, u = unit(i, n)
                    act.wait_ge(made, u + 1)
                    if not last:
                        next_split(w.split_high, act, i, n)
                    if not first:
                        act.wait_ge(used, u - 1)
                    act.activation(gate[:, s, :], bank(core, 4 * s), ACT.Sigmoid,
                                   bias=gate_b(b, j)).then_inc(opened, 1)

                w.first_high(act)
                sixes(act, sigmoid)

            @block.vector
            def _(dve):
                def gated_sum(i, n, first, last):
                    j, b, s, u = unit(i, n)
                    if not last:
                        next_split(w.split_low, dve, i, n)
                    dve.wait_ge(opened, u + 1)
                    dst = mergedT[:, j, :] if b == 0 else prod[:, s, :]
                    if b == 1 and not first:
                        dve.wait_ge(summed, 4 * i + 2 * (n // 3))
                    dve.tensor_tensor(dst, bank(core, 4 * s + 2), gate[:, s, :], ALU.mult).then_inc(used, 1)
                    if b > 0:
                        dve.wait_ge(used, u + 1)
                        if b == 2:
                            dve.wait_ge(summed, 4 * i + 2 * (n // 3) + 1)
                        dve.tensor_tensor(mergedT[:, j, :], mergedT[:, j, :], prod[:, s, :],
                                          ALU.add).then_inc(summed, 1)

                w.first_low(dve)
                sixes(dve, gated_sum)


def stage_mix_chunks(core, vv, spatial_dram, spatial_b_dram, yaT):
    nc = core.nc
    with ExitStack() as stack:
        wT = core.sb(stack, "spatial_w", [P, 4, P])
        bias = core.sb(stack, "spatial_b", [P, 6, P])
        held = core.sb(stack, "spatial_sum", [P, 2, S])
        loaded = core.sem("spatial_loaded")
        masked = core.sem("spatial_masked")
        made = core.sem("spatial_made")
        added = core.sem("spatial_added")
        with nc.Block(no_gpsimd_drain=True) as block:

            @block.sync
            def _(sp):
                sp.dma_start(wT[:, :, :], spatial_dram).then_inc(loaded, 16)
                sp.dma_start(bias[:, :, :], spatial_b_dram).then_inc(loaded, 16)

            @block.gpsimd
            def _(pool):
                pool.wait_ge(loaded, 32)
                pool.affine_select(out=wT[:, :, :], in_=wT[:, :, :], compare_op=ALU.is_ge, fill=0.0, base=0,
                                   pattern=[[0, 4], [1, P]], channel_multiplier=-1).then_inc(masked, 1)

            @block.tensor
            def _(pe):
                pe.wait_ge(masked, 1)
                for c in range(6):
                    if c >= 2:
                        pe.wait_ge(added, c - 1)
                    for t in range(TT):
                        for rows in ([slice(0, 64), slice(64, 128)] if c in (1, 4) else [slice(0, 128)]):
                            first = c * P + rows.start
                            last = pe.matmul(bank(core, 2 * (c % 2))[rows, t * P:(t + 1) * P],
                                             vv[:, t, first:first + rows.stop - rows.start],
                                             wT[:, first // 192, :], start=True, stop=True)
                    last.then_inc(made, 1)

            @block.vector
            def _(dve):
                for c in range(6):
                    s = c % 2
                    dve.wait_ge(made, c + 1)
                    split = lambda a: a.rearrange("p (n t) -> p n t", t=P)
                    dve.tensor_tensor(split(held[:, s, :]), split(bank(core, 2 * s)),
                                      bias[:, c, :].unsqueeze(1).to_broadcast([P, TT, P]),
                                      ALU.add).then_inc(added, 1)
                    dve.wait_ge(added, c + 1)
                    dve.tensor_tensor(yaT[:, c, :], yaT[:, c, :], held[:, s, :], ALU.mult)


def stage_output(core, yT, weights, base_tile, gate, dst):
    nc = core.nc
    with ExitStack() as stack:
        w = SplitMatrix(core, stack, weights, D)
        y = core.sb(stack, "y_parts", [P, 2, 2, KT, P], F32R)
        base = core.sb(stack, "base", [P, 2, D]) if base_tile else None
        base_loaded = [core.sem("base_loaded") for _ in range(2)]
        y_high = core.sem("y_high")
        y_low = core.sem("y_low")
        made = core.sem("out_made")
        gated = core.sem("out_gated")
        added = core.sem("out_added")
        tokens = lambda t: yT[:, :, t * P:(t + 1) * P]
        with nc.Block(no_gpsimd_drain=True) as block:

            @block.sync
            def _(sp):
                w.load(sp)
                if base_tile:
                    for t in range(TT):
                        if t >= 2:
                            sp.wait_ge(added, t - 1)
                        sp.dma_start(base[:, t % 2, :], base_tile(t)).then_inc(base_loaded[t % 2], 16)

            @block.tensor
            def _(pe):
                for t in range(TT):
                    pe.wait_ge(y_low, t + 1)
                    if t >= 2:
                        pe.wait_ge(added, t - 1)
                    w.products(pe, t == 0, [bank(core, 2 * (t % 2) + h, 1) for h in range(2)],
                               lambda part, k: y[:, t % 2, part, k, :], [0, HALF], HALF).then_inc(made, 1)

            @block.scalar
            def _(act):
                def split(t):
                    if t >= 2:
                        act.wait_ge(made, t - 1)
                    act.copy(y[:, t % 2, HI, :, :], tokens(t)).then_inc(y_high, 1)

                split(0)
                split(1)
                w.split_high(act)
                for t in range(2, TT):
                    split(t)

            @block.vector
            def _(dve):
                def split(t):
                    dve.wait_ge(y_high, t + 1)
                    dve.tensor_tensor(y[:, t % 2, LO, :, :], tokens(t), y[:, t % 2, HI, :, :].bitcast(F32),
                                      ALU.subtract).then_inc(y_low, 1)

                split(0)
                split(1)
                w.split_low(dve)
                for t in range(TT):
                    dve.wait_ge(made, t + 1)
                    if t + 2 < TT:
                        split(t + 2)
                    rows = bank(core, 2 * (t % 2))
                    if base_tile:
                        dve.wait_ge(base_loaded[t % 2], 16 * (t // 2) + 16)
                        dve.tensor_tensor(dst[:, t, :], rows, base[:, t % 2, :], ALU.add).then_inc(added, 1)
                    else:
                        dve.tensor_tensor(rows, rows, gate, ALU.mult).then_inc(gated, 1)
                        dve.wait_ge(gated, t + 1)
                        dve.tensor_tensor(dst[:, t, :], rows, dst[:, t, :], ALU.add).then_inc(added, 1)


def stage_modulation(core, cond_cols, ada, ada_b, gate_b, norm_gain, shift, gain, gate, beside):
    nc = core.nc
    load_beside, vector_beside, save_beside = beside
    with ExitStack() as stack:
        w = core.sb(stack, "ada_w", [P, 2, KT, D])
        wide = core.sb(stack, "cond_wide", [P, KT, P])
        cond = core.sb(stack, "cond", [P, KT])
        loaded = [core.sem("ada_loaded") for _ in range(2)]
        c_loaded = core.sem("cond_loaded")
        silued = core.sem("cond_silu")
        made = core.sem("mod_made")
        used = core.sem("mod_used")
        with nc.Block(no_gpsimd_drain=True) as block:

            @block.sync
            def _(sp):
                load_beside(sp)
                sp.dma_start(cond[:, :], cond_cols).then_inc(c_loaded, 16)
                sp.dma_start(gate[:, :], gate_b).then_inc(c_loaded, 16)
                for n in range(3):
                    if n == 2:
                        sp.wait_ge(made, 1)
                    sp.dma_start(w[:, n % 2, :, :], ada[:, :, n * D:(n + 1) * D]).then_inc(loaded[n % 2], 16)
                save_beside(sp)

            @block.scalar
            def _(act):
                act.wait_ge(c_loaded, 32)
                act.activation(cond[:, :], cond[:, :], ACT.Silu).then_inc(silued, 1)
                act.wait_ge(silued, 1)
                act.copy(wide[:, :, :], cond[:, :].unsqueeze(2).to_broadcast([P, KT, P])).then_inc(silued, 1)

            @block.tensor
            def _(pe):
                pe.wait_ge(silued, 2)
                for n in range(2):
                    pe.wait_ge(loaded[n], 16)
                    for j in range(KT):
                        for k in range(KT):
                            last = pe.matmul(bank(core, n, 1)[:, j:j + 1], w[:, n, k, j * P:(j + 1) * P],
                                             cond[:, k:k + 1], start=(k == 0), stop=(k == KT - 1))
                    last.then_inc(made, 1)
                pe.wait_ge(loaded[0], 32)
                for h in range(2):
                    for k in range(KT):
                        last = pe.matmul(bank(core, 2 + h, 1), wide[:, k, :], w[:, 0, k, h * HALF:(h + 1) * HALF],
                                         start=(k == 0), stop=(k == KT - 1))
                last.then_inc(made, 1)

            @block.vector
            def _(dve):
                vector_beside(dve)
                dve.wait_ge(made, 1)
                dve.tensor_tensor(shift[:, :], bank(core, 0, 1)[:, 0:KT], ada_b[:, 0:KT], ALU.add)
                dve.wait_ge(made, 2)
                dve.tensor_tensor(gain[:, :], bank(core, 1, 1)[:, 0:KT], ada_b[:, KT:2 * KT], ALU.add)\
                   .then_inc(used, 1)
                dve.wait_ge(used, 1)
                dve.scalar_tensor_tensor(out=gain[:, :], in0=gain[:, :], scalar=1.0, in1=norm_gain,
                                         op0=ALU.add, op1=ALU.mult)
                dve.wait_ge(made, 3)
                dve.wait_ge(c_loaded, 32)
                dve.tensor_tensor(gate[:, :], bank(core, 2), gate[:, :], ALU.add)


LN2_HI = 0.693359375
LN2_LO = -2.12194440e-4
ROUND = 1.5 * 2 ** 23
TWO_PI = (6.28125, 1.9340515e-3, 1.2556660e-6)


def ssm_matrices_beside(core, stack, prm_dram, bc_dram, const, kept, powers, d_cols):
    nc = core.nc
    N = SSM_GROUPS
    G = core.sb(stack, "ssm_G", [P, N, 2 * P])
    M_out = core.sb(stack, "ssm_M", [P, N, P])
    c_stack = core.sb(stack, "ssm_C", [P, N, N])
    prm = core.sb(stack, "ssm_prm", [P, 4, N])
    bc = core.sb(stack, "ssm_bc", [P, 4, N, N])
    tiny = core.sb(stack, "ssm_tiny", [P, 12, N])
    whole = core.sb(stack, "ssm_int", [P, N], I32)
    pre = core.sb(stack, "ssm_pw_re", [P, 9, N])
    pim = core.sb(stack, "ssm_pw_im", [P, 9, N])
    mats = core.sb(stack, "ssm_mats", [P, 4, N, N])
    tmp = core.sb(stack, "ssm_tmp", [P, N, N])
    loaded = core.sem("ssm_loaded")
    chain = core.sem("ssm_chain")
    sign = const[:, SIGN:SIGN + 1]
    finished = core.sem("ssm_finished")
    saved = core.sem("ssm_saved")

    def load(sp):
        sp.dma_start(prm[:, :, :], prm_dram).then_inc(loaded, 16)
        sp.dma_start(bc[:, :, :, :], bc_dram).then_inc(loaded, 16)

    def save(sp):
        sp.wait_ge(finished, 1)
        for there, made in zip(kept, (G, M_out, c_stack)):
            sp.dma_start(there, made[:, :, :]).then_inc(saved, 16)
        sp.wait_ge(saved, 16 * len(kept))

    def vector(dve):
        steps = [0]

        def step(ins):
            steps[0] += 1
            ins.then_inc(chain, 1)
            dve.wait_ge(chain, steps[0])

        def tt(out, a, b, op):
            step(dve.tensor_tensor(out, a, b, op))

        def ts(out, a, s1, op1, s2=None, op2=ALU.bypass):
            if s2 is None:
                step(dve.tensor_scalar(out, a, s1, None, op1))
            else:
                step(dve.tensor_scalar(out, a, s1, s2, op1, op2))

        def stt(out, a, s, b, op1, op2):
            step(dve.scalar_tensor_tensor(out=out, in0=a, scalar=s, in1=b, op0=op1, op1=op2))

        def horner(acc, x, coeffs):
            ts(acc, x, coeffs[-1], ALU.mult)
            for c in reversed(coeffs[:-1]):
                stt(acc, acc, c, x, ALU.add, ALU.mult)

        def exponential(out, x, k, r):
            ts(x, x, -87.0, ALU.max, 88.7, ALU.min)
            ts(k, x, 1 / math.log(2), ALU.mult)
            ts(k, k, ROUND, ALU.add)
            ts(k, k, ROUND, ALU.subtract)
            stt(r, k, -LN2_HI, x, ALU.mult, ALU.add)
            stt(r, k, -LN2_LO, r, ALU.mult, ALU.add)
            horner(out, r, [1 / math.factorial(i) for i in range(1, 10)])
            ts(out, out, 1.0, ALU.add)
            ts(k, k, 127.0, ALU.add)
            ts(k, k, 2.0 ** 23, ALU.mult)
            step(dve.tensor_copy(whole[:, :], k))
            tt(out, out, whole[:, :].bitcast(F32), ALU.mult)

        dve.wait_ge(loaded, 32)
        lr, li, ls, dd = (prm[:, i, :] for i in range(4))
        stepv, mag, ang, cosv, sinv, a, b, c, den, fr, fi, ai = (tiny[:, i, :] for i in range(12))
        step(dve.tensor_copy(d_cols[:, :], dd))
        exponential(stepv, ls, a, b)
        tt(c, lr, stepv, ALU.mult)
        exponential(mag, c, a, b)
        tt(ang, li, stepv, ALU.mult)
        ts(a, ang, 1 / (2 * math.pi), ALU.mult)
        ts(a, a, ROUND, ALU.add)
        ts(a, a, ROUND, ALU.subtract)
        for part in TWO_PI:
            stt(ang, a, -part, ang, ALU.mult, ALU.add)
        ts(ang, ang, 0.5, ALU.mult)
        tt(b, ang, ang, ALU.mult)
        horner(sinv, b, [(-1) ** i / math.factorial(2 * i + 1) for i in range(1, 8)])
        stt(sinv, sinv, 1.0, ang, ALU.add, ALU.mult)
        horner(cosv, b, [(-1) ** i / math.factorial(2 * i) for i in range(1, 9)])
        ts(cosv, cosv, 1.0, ALU.add)
        tt(c, sinv, cosv, ALU.mult)
        tt(cosv, sinv, sinv, ALU.mult)
        ts(cosv, cosv, -2.0, ALU.mult, 1.0, ALU.add)
        stt(pim[:, 1, :], c, 2.0, mag, ALU.mult, ALU.mult)
        tt(pre[:, 1, :], cosv, mag, ALU.mult)
        ar, ai = pre[:, 1, :], pim[:, 1, :]
        tt(a, lr, lr, ALU.mult)
        tt(den, li, li, ALU.mult)
        tt(den, den, a, ALU.add)
        step(dve.reciprocal(den, den))
        ts(c, ar, -1.0, ALU.add)
        tt(a, c, lr, ALU.mult)
        tt(b, ai, li, ALU.mult)
        tt(fr, a, b, ALU.add)
        tt(fr, fr, den, ALU.mult)
        tt(a, ai, lr, ALU.mult)
        tt(b, c, li, ALU.mult)
        tt(fi, a, b, ALU.subtract)
        tt(fi, fi, den, ALU.mult)

        def times(outr, outi, xr, xi, yr, yi):
            tt(a, xr, yr, ALU.mult)
            tt(b, xi, yi, ALU.mult)
            tt(outr, a, b, ALU.subtract)
            tt(a, xr, yi, ALU.mult)
            tt(b, xi, yr, ALU.mult)
            tt(outi, a, b, ALU.add)

        for k in range(1, 8):
            times(pre[:, k + 1, :], pim[:, k + 1, :], pre[:, k, :], pim[:, k, :], ar, ai)
        step(dve.tensor_copy(powers[:, 0, 0, :], pre[:, 8, :]))
        step(dve.tensor_copy(powers[:, 1, 0, :], pim[:, 8, :]))
        for k in range(1, LEVELS):
            r, i = powers[:, 0, k - 1, :], powers[:, 1, k - 1, :]
            times(powers[:, 0, k, :], powers[:, 1, k, :], r, i, r, i)

        wide = lambda v: v.unsqueeze(2).to_broadcast([P, N, N])
        B, iB, C, iC = (mats[:, i, :, :] for i in range(4))
        b1, b2, c1, c2 = (bc[:, i, :, :] for i in range(4))
        ts(b2, b2, sign, ALU.mult)
        tt(B, b1, wide(fr), ALU.mult)
        tt(tmp[:, :, :], b2, wide(fi), ALU.mult)
        tt(B, B, tmp[:, :, :], ALU.add)
        tt(iB, b2, wide(fr), ALU.mult)
        tt(tmp[:, :, :], b1, wide(fi), ALU.mult)
        tt(iB, iB, tmp[:, :, :], ALU.subtract)
        ts(C, c1, sign, ALU.mult, -1.0, ALU.mult)
        ts(iC, c2, -1.0, ALU.mult)
        step(dve.memset(G[:, :, P:2 * P], 0.0))

        def mix(out, r, i, x, y):
            tt(out, x, wide(r), ALU.mult)
            tt(tmp[:, :, :], y, wide(i), ALU.mult)
            tt(out, out, tmp[:, :, :], ALU.add)

        step(dve.tensor_copy(G[:, :, 7 * N:8 * N], B))
        for k in range(1, 8):
            mix(G[:, :, (7 - k) * N:(8 - k) * N], pre[:, k, :], pim[:, k, :], B, iB)
        for t in range(8):
            mix(M_out[:, :, t * N:(t + 1) * N], pre[:, t + 1, :], pim[:, t + 1, :], C, iC)
        dve.tensor_copy(c_stack[:, :, :], C).then_inc(finished, 1)

    return load, vector, save


def stage_ssm_scan(core, matrices, scratch_u, const, ident, G, M_out, c_stack, powers, d_cols, Y):
    nc = core.nc
    N = SSM_GROUPS
    with ExitStack() as stack:
        U = core.sb(stack, "ssm_U", [P, N, P])
        Gt = core.sb(stack, "ssm_Gt", [P, N, P])
        T = core.sb(stack, "ssm_T", [P, N, P])
        X = core.sb(stack, "ssm_X", [P, N, P])
        L = core.sb(stack, "ssm_L", [P, 2, N, P])
        matrices_loaded = core.sem("ssm_matrices_loaded")
        spread = core.sem("u_spread")
        turned = core.sem("g_turned")
        g_kept = core.sem("g_kept")
        t_made = core.sem("t_made")
        t_kept = core.sem("t_kept")
        v_made = core.sem("v_made")
        x_new = core.sem("x_new")
        diag = core.sem("level_diag")
        level = core.sem("level_ready")
        carried = core.sem("carried")
        y_made = core.sem("y_made")
        swap = const[:, SWAP:SWAP + P]

        with nc.Block(no_gpsimd_drain=True) as block:

            @block.sync
            def _(sp):
                for there, into in matrices:
                    sp.dma_start(into, there).then_inc(matrices_loaded, 16)
                for t in range(8):
                    sp.dma_start(U[N * t:N * t + N, :, :],
                                 scratch_u[:, :, t, :].rearrange("g h c -> h g c")).then_inc(spread, 16)

            @block.tensor
            def _(pe):
                pe.wait_ge(matrices_loaded, 16 * len(matrices))
                for a in range(4):
                    for g in range(4 * a, 4 * a + 4):
                        last = pe.transpose(bank(core, a, 1)[:, (g % 4) * P:(g % 4 + 1) * P],
                                            G[:, g, 0:P], ident)
                    last.then_inc(turned, 1)
                for a in range(4):
                    for g in range(4 * a, 4 * a + 4):
                        for t in range(8):
                            at = (g % 4) * P + t * N
                            last = pe.matmul(bank(core, 4 + a, 1)[:, at:at + N],
                                             G[:, g, (7 - t) * N:(7 - t) * N + P], c_stack[:, g, :],
                                             start=True, stop=True)
                    last.then_inc(t_made, 1)
                pe.wait_ge(spread, 128)
                for a in range(4):
                    pe.wait_ge(g_kept, a + 1)
                    for g in range(4 * a, 4 * a + 4):
                        last = pe.matmul(bank(core, a, 1)[:, (g % 4) * P:(g % 4 + 1) * P],
                                         Gt[:, g, :], U[:, g, :], start=True, stop=True)
                    last.then_inc(v_made, 1)
                for k in range(LEVELS):
                    pe.wait_ge(level, k + 1)
                    for a in range(4):
                        pe.wait_ge(x_new, 4 * k + a + 1)
                        for g in range(4 * a, 4 * a + 4):
                            width = P - 2 ** k
                            last = pe.matmul(bank(core, a, 1)[:, (g % 4) * P:(g % 4) * P + width],
                                             L[:, k % 2, g, :], X[:, g, 0:width], start=True, stop=True)
                        last.then_inc(carried, 1)
                pe.wait_ge(t_kept, 1)
                for a in range(4):
                    pe.wait_ge(x_new, 4 * LEVELS + a + 1)
                    for g in range(4 * a, 4 * a + 4):
                        at = (g % 4) * P
                        pe.matmul(bank(core, 4 + a, 1)[:, at:at + P], T[:, g, :], U[:, g, :],
                                  start=True, stop=False)
                        last = pe.matmul(bank(core, 4 + a, 1)[:, at + 1:at + P], M_out[:, g, :],
                                         X[:, g, 0:P - 1], start=False, stop=True)
                    last.then_inc(y_made, 1)

            @block.scalar
            def _(act):
                for a in range(4):
                    act.wait_ge(turned, a + 1)
                    act.copy(Gt[:, 4 * a:4 * a + 4, :].rearrange("p g s -> p (g s)"),
                             bank(core, a, 1)).then_inc(g_kept, 1)
                for k in range(LEVELS):
                    if k >= 2:
                        act.wait_ge(carried, 4 * (k - 1))
                    for g in range(N):
                        last = act.activation(L[:, k % 2, g, :], ident, ACT.Copy,
                                              scale=powers[:, 0, k, g:g + 1])
                    last.then_inc(diag, 1)
                for a in range(4):
                    act.wait_ge(y_made, a + 1)
                    act.copy(Y[:, 4 * a:4 * a + 4, :].rearrange("p g s -> p (g s)"), bank(core, 4 + a, 1))

            @block.vector
            def _(dve):
                def level_matrices(k):
                    dve.wait_ge(diag, k + 1)
                    for g in range(N):
                        m = L[:, k % 2, g, :]
                        last = dve.scalar_tensor_tensor(out=m, in0=swap, scalar=powers[:, 1, k, g:g + 1],
                                                        in1=m, op0=ALU.mult, op1=ALU.add)
                    last.then_inc(level, 1)

                for a in range(4):
                    dve.wait_ge(t_made, a + 1)
                    for g in range(4 * a, 4 * a + 4):
                        last = dve.scalar_tensor_tensor(
                            out=T[:, g, :], in0=ident, scalar=d_cols[:, g:g + 1],
                            in1=bank(core, 4 + a, 1)[:, (g % 4) * P:(g % 4 + 1) * P],
                            op0=ALU.mult, op1=ALU.add)
                last.then_inc(t_kept, 1)
                level_matrices(0)
                for a in range(4):
                    dve.wait_ge(v_made, a + 1)
                    dve.tensor_copy(X[:, 4 * a:4 * a + 4, :].rearrange("p g s -> p (g s)"),
                                    bank(core, a, 1)).then_inc(x_new, 1)
                for k in range(LEVELS):
                    if k + 1 < LEVELS:
                        level_matrices(k + 1)
                    for a in range(4):
                        dve.wait_ge(carried, 4 * k + a + 1)
                        later = X[:, 4 * a:4 * a + 4, 2 ** k:P]
                        dve.tensor_tensor(later, later,
                                          bank(core, a, 1).rearrange("p (g s) -> p g s", g=4)[:, :, 0:P - 2 ** k],
                                          ALU.add).then_inc(x_new, 1)


def stage_ssm_output(core, Y, scratch_y, glu_dram, glu_b, yT):
    nc = core.nc
    N = SSM_GROUPS
    with ExitStack() as stack:
        ys = core.sb(stack, "ssm_ys", [P, 2, S])
        sig = core.sb(stack, "ssm_sig", [P, 2, S])
        w = core.sb(stack, "glu_w", [P, 2, 2 * P])
        saved = core.sem("y_saved")
        loaded = core.sem("y_loaded")
        mapped = core.sem("y_mapped")
        made = core.sem("glu_made")
        opened = core.sem("glu_opened")
        gated = core.sem("glu_gated")
        with nc.Block(no_gpsimd_drain=True) as block:

            @block.sync
            def _(sp):
                sp.dma_start(w[:, :, :], glu_dram).then_inc(loaded, 16)
                for t in range(8):
                    sp.dma_start(scratch_y[:, :, t, :].rearrange("g h c -> h g c"),
                                 Y[N * t:N * t + N, :, :]).then_inc(saved, 16)
                sp.wait_ge(saved, 128)
                for j in range(2):
                    sp.dma_start(ys[:, j, :], scratch_y[8 * j:8 * j + 8].rearrange("g h t c -> (g h) (t c)"))\
                      .then_inc(loaded, 16)

            @block.scalar
            def _(act):
                act.wait_ge(loaded, 48)
                act.activation(ys[:, :, :], ys[:, :, :], ACT.Gelu_apprx_tanh).then_inc(mapped, 1)
                for m in range(2):
                    act.wait_ge(made, m + 1)
                    act.activation(sig[:, m, :], bank(core, 2 * m), ACT.Sigmoid,
                                   bias=glu_b[:, m:m + 1]).then_inc(opened, 1)

            @block.tensor
            def _(pe):
                pe.wait_ge(mapped, 1)
                for m in range(2):
                    for h in range(2):
                        for k in range(2):
                            last = pe.matmul(bank(core, 2 * m + h, 1), w[:, k, m * P:(m + 1) * P],
                                             ys[:, k, h * HALF:(h + 1) * HALF], start=(k == 0), stop=(k == 1))
                    last.then_inc(made, 1)

            @block.vector
            def _(dve):
                for m in range(2):
                    dve.wait_ge(opened, m + 1)
                    dve.tensor_tensor(sig[:, m, :], ys[:, m, :], sig[:, m, :], ALU.mult).then_inc(gated, 1)
                    dve.wait_ge(gated, m + 1)
                    by_chunk = yT[:, m, :].rearrange("p (c t) -> p c t", t=8)
                    dve.tensor_tensor(by_chunk, by_chunk, sig[:, m, :].rearrange("p (t c) -> p c t", t=8),
                                      ALU.mult)


def stage_diff_tables(core, lam_dram, neg_lam):
    nc = core.nc
    with ExitStack() as stack:
        rows = core.sb(stack, "lam_rows", [P, 4, 64])
        prod = core.sb(stack, "lam_prod", [P, 64])
        dots = core.sb(stack, "lam_dots", [P, 2])
        loaded = core.sem("lam_loaded")
        dotted = core.sem("lam_dotted")
        exped = core.sem("lam_exped")
        with nc.Block(no_gpsimd_drain=True) as block:

            @block.sync
            def _(sp):
                sp.dma_start(rows[:, :, :], lam_dram).then_inc(loaded, 16)

            @block.vector
            def _(dve):
                dve.wait_ge(loaded, 16)
                for i in range(2):
                    dve.tensor_tensor_reduce(prod[:, :], rows[:, 2 * i, :], rows[:, 2 * i + 1, :], 1.0, 0.0,
                                             ALU.mult, ALU.add, dots[:, i:i + 1]).then_inc(dotted, 1)
                    dve.wait_ge(dotted, i + 1)
                dve.wait_ge(exped, 1)
                dve.tensor_tensor(neg_lam[:, :], dots[:, 1:2], dots[:, 0:1], ALU.subtract).then_inc(dotted, 1)
                dve.wait_ge(dotted, 3)
                dve.tensor_scalar(neg_lam[:, :], neg_lam[:, :], -LAM_INIT, None, ALU.add)

            @block.scalar
            def _(act):
                act.wait_ge(dotted, 2)
                act.activation(dots[:, :], dots[:, :], ACT.Exp).then_inc(exped, 1)


def stage_diff_attention(core, qT, kT, v, far_dram, neg_lam, ident, out):
    nc = core.nc
    units = [(h, t) for h in range(4) for t in range(TT)]
    n = len(units)
    with ExitStack() as stack:
        far = core.sb(stack, "far", [P, D])
        bias = core.sb(stack, "alibi", [P, 2, D])
        p = core.sb(stack, "diff_p", [P, 3, 2, D])
        pT = core.sb(stack, "diff_pT", [P, 2, D])
        top = core.sb(stack, "diff_top", [P, 2, 2])
        low = core.sb(stack, "diff_low", [P, 2, 2])
        total = core.sb(stack, "diff_total", [P, 2, 2])
        inv = core.sb(stack, "diff_inv", [P, 2, 2])
        far_loaded = core.sem("far_loaded")
        scored = core.sem("diff_scored")
        maxed = core.sem("diff_maxed")
        small = core.sem("diff_small")
        exped = core.sem("diff_exped")
        weighted = core.sem("diff_weighted")
        turned = core.sem("diff_turned")
        moved_act = core.sem("diff_moved_act")
        moved_dve = core.sem("diff_moved_dve")
        mixed = core.sem("diff_mixed")
        stored = core.sem("diff_stored")

        def place(b):
            return HALF * (b % 2) + P * (b // 2)

        with nc.Block(no_gpsimd_drain=True) as block:

            @block.sync
            def _(sp):
                sp.dma_start(far[:, :], far_dram).then_inc(far_loaded, 16)

            @block.tensor
            def _(pe):
                def scores(u):
                    h, t = units[u]
                    width = (t + 1) * P
                    if u >= 1:
                        pe.wait_ge(maxed, u)
                    for c0 in range(0, width, HALF):
                        cw = min(HALF, width - c0)
                        for m in range(2):
                            rows = slice(64 * m, 64 * m + 64)
                            last = pe.matmul(bank(core, 2 * m)[:, c0:c0 + cw], qT[rows, h, t * P:(t + 1) * P],
                                             kT[rows, h, c0:c0 + cw], start=True, stop=True)
                    last.then_inc(scored, 1)

                def turn(u):
                    h, t = units[u]
                    pe.wait_ge(weighted, u + 1)
                    if u >= 1:
                        pe.wait_ge(moved_act, u)
                        pe.wait_ge(moved_dve, u)
                    for b in range(t + 1):
                        last = pe.transpose(bank(core, 4)[:, place(b):place(b) + P],
                                            p[:, u % 3, 0, b * P:(b + 1) * P], ident)
                    last.then_inc(turned, 1)

                def mix(u):
                    h, t = units[u]
                    pe.wait_ge(moved_act, u + 1)
                    pe.wait_ge(moved_dve, u + 1)
                    if u >= 2:
                        pe.wait_ge(stored, u - 1)
                    for b in range(t + 1):
                        last = pe.matmul(bank(core, 6 + u % 2, 1)[:, 0:P], pT[:, u % 2, place(b):place(b) + P],
                                         v[:, b, h * P:(h + 1) * P], start=(b == 0), stop=(b == t))
                    last.then_inc(mixed, 1)

                for u in range(n + 3):
                    if u < n:
                        scores(u)
                    if 2 <= u < n + 2:
                        turn(u - 2)
                    if u >= 3:
                        mix(u - 3)

            @block.vector
            def _(dve):
                steps = [0]

                def step(ins):
                    steps[0] += 1
                    ins.then_inc(small, 1)
                    dve.wait_ge(small, steps[0])

                def slopes(h):
                    step(dve.tensor_scalar(bias[:, h % 2, :], far[:, :], 2.0 ** -(5 + h), None, ALU.mult))

                def maxima(u):
                    h, t = units[u]
                    s = u % 2
                    width = (t + 1) * P
                    if t == 0:
                        slopes(h)
                    dve.wait_ge(scored, u + 1)
                    if u >= 3:
                        dve.wait_ge(turned, u - 2)
                    for m in range(2):
                        last = dve.tensor_tensor_reduce(
                            p[:, u % 3, m, 0:width], bank(core, 2 * m)[:, 0:width], bias[:, h % 2, D - width:D],
                            1.0, -3e38, ALU.add, ALU.max, top[:, s, m:m + 1])
                    step(last)
                    dve.tensor_scalar(low[:, s, :], top[:, s, :], -1.0, None, ALU.mult).then_inc(maxed, 1)

                def weights(u):
                    h, t = units[u]
                    s = u % 2
                    width = (t + 1) * P
                    dve.wait_ge(exped, u + 1)
                    step(dve.reciprocal(inv[:, s, :], total[:, s, :]))
                    step(dve.tensor_scalar(inv[:, s, 1:2], inv[:, s, 1:2], neg_lam, None, ALU.mult))
                    p1, p2 = p[:, u % 3, 0, 0:width], p[:, u % 3, 1, 0:width]
                    step(dve.tensor_scalar(p2, p2, inv[:, s, 1:2], None, ALU.mult))
                    dve.scalar_tensor_tensor(out=p1, in0=p1, scalar=inv[:, s, 0:1], in1=p2, op0=ALU.mult,
                                             op1=ALU.add).then_inc(weighted, 1)

                def move(u):
                    h, t = units[u]
                    dve.wait_ge(turned, u + 1)
                    if u >= 2:
                        dve.wait_ge(mixed, u - 1)
                    if t == 0:
                        dve.sem_inc(moved_dve, 1)
                        return
                    odd = (t + 1) // 2 * P
                    dve.tensor_copy(pT[:, u % 2, HALF:HALF + odd],
                                    bank(core, 5, 1)[:, 0:odd]).then_inc(moved_dve, 1)

                def store(u):
                    h, t = units[u]
                    dve.wait_ge(mixed, u + 1)
                    dve.tensor_copy(out[:, t, h * P:(h + 1) * P], bank(core, 6 + u % 2, 1)[:, 0:P])\
                       .then_inc(stored, 1)

                dve.wait_ge(far_loaded, 16)
                for u in range(n + 4):
                    if 1 <= u <= n:
                        weights(u - 1)
                    if u < n:
                        maxima(u)
                    if 2 <= u < n + 2:
                        move(u - 2)
                    if u >= 4:
                        store(u - 4)

            @block.scalar
            def _(act):
                def move(u):
                    h, t = units[u]
                    act.wait_ge(turned, u + 1)
                    if u >= 2:
                        act.wait_ge(mixed, u - 1)
                    even = (t + 2) // 2 * P
                    act.copy(pT[:, u % 2, 0:even], bank(core, 4, 1)[:, 0:even]).then_inc(moved_act, 1)

                def exps(u):
                    h, t = units[u]
                    s = u % 2
                    width = (t + 1) * P
                    act.wait_ge(maxed, u + 1)
                    if u >= 2:
                        act.wait_ge(weighted, u - 1)
                    for m in range(2):
                        last = act.activation(p[:, u % 3, m, 0:width], p[:, u % 3, m, 0:width], ACT.Exp,
                                              bias=low[:, s, m:m + 1], accum_out=total[:, s, m:m + 1])
                    last.then_inc(exped, 1)

                for u in range(n + 2):
                    if u < n:
                        exps(u)
                    if u >= 2:
                        move(u - 2)


def stage_diff_norm(core, o, subln, ident, eps, yT):
    nc = core.nc
    with ExitStack() as stack:
        sq = core.sb(stack, "dn_sq", [P, TT * 512])
        r = core.sb(stack, "dn_r", [P, 4 * TT])
        sub = core.sb(stack, "dn_sub", [P, 1])
        squared = core.sem("dn_squared")
        rooted = core.sem("dn_rooted")
        chain = core.sem("dn_chain")
        scaled = core.sem("dn_scaled")
        turned = core.sem("dn_turned")
        moved = core.sem("dn_moved")
        heads = lambda a: a.rearrange("p (h d) -> p h d", d=P)
        with nc.Block(no_gpsimd_drain=True) as block:

            @block.vector
            def _(dve):
                dve.tensor_scalar(sub[:, :], subln, 1.0 - LAM_INIT, None, ALU.mult).then_inc(chain, 1)
                flat = o.rearrange("p t d -> p (t d)")
                dve.tensor_tensor(sq[:, :], flat, flat, ALU.mult).then_inc(chain, 1)
                dve.wait_ge(chain, 2)
                dve.tensor_reduce(r[:, :], heads(sq[:, :]), AX_X, ALU.add).then_inc(squared, 1)
                dve.wait_ge(rooted, 1)
                dve.reciprocal(r[:, :], r[:, :]).then_inc(chain, 1)
                dve.wait_ge(chain, 3)
                for t in range(TT):
                    dve.tensor_tensor(heads(o[:, t, :]), heads(o[:, t, :]),
                                      r[:, 4 * t:4 * t + 4].unsqueeze(2).to_broadcast([P, 4, P]),
                                      ALU.mult).then_inc(scaled, 1)
                for t in range(TT):
                    dve.wait_ge(turned, t + 1)
                    y = yT[:, 2:6, t * P:(t + 1) * P]
                    dve.scalar_tensor_tensor(out=y, in0=heads(bank(core, t % 4, 1)), scalar=sub[:, 0:1], in1=y,
                                             op0=ALU.mult, op1=ALU.mult).then_inc(moved, 1)

            @block.scalar
            def _(act):
                act.wait_ge(squared, 1)
                act.activation(r[:, :], r[:, :], ACT.Sqrt, bias=eps[:, 0:1], scale=1 / P).then_inc(rooted, 1)

            @block.tensor
            def _(pe):
                for t in range(TT):
                    pe.wait_ge(scaled, t + 1)
                    if t >= 4:
                        pe.wait_ge(moved, t - 3)
                    for h in range(4):
                        last = pe.transpose(bank(core, t % 4, 1)[:, h * P:(h + 1) * P],
                                            o[:, t, h * P:(h + 1) * P], ident)
                    last.then_inc(turned, 1)


def stage_swa_tables(core, far_dram, table):
    nc = core.nc
    with ExitStack() as stack:
        far = core.sb(stack, "swa_far", [P, 256])
        loaded = core.sem("swa_far_loaded")
        with nc.Block(no_gpsimd_drain=True) as block:

            @block.sync
            def _(sp):
                sp.dma_start(far[:, :], far_dram).then_inc(loaded, 16)

            @block.vector
            def _(dve):
                dve.wait_ge(loaded, 16)
                for h in range(4):
                    dve.tensor_scalar(table[:, h, :], far[:, :], 2.0 ** -(1 + h), None, ALU.mult)


def stage_final_norm(core, x, gain_dram, eps, out_tiles):
    nc = core.nc
    with ExitStack() as stack:
        gain = core.sb(stack, "final_gain", [P, D])
        sq = core.sb(stack, "final_sq", [P, D])
        y = core.sb(stack, "final_y", [P, 2, D])
        r = core.sb(stack, "final_r", [P, 2, TT])
        loaded = core.sem("final_loaded")
        summed = core.sem("final_summed")
        rooted = core.sem("final_rooted")
        inverted = core.sem("final_inverted")
        scaled = core.sem("final_scaled")
        stored = [core.sem("final_stored") for _ in range(2)]
        with nc.Block(no_gpsimd_drain=True) as block:

            @block.sync
            def _(sp):
                sp.dma_start(gain[:, :], gain_dram).then_inc(loaded, 16)
                for t in range(TT):
                    sp.wait_ge(scaled, t + 1)
                    sp.dma_start(out_tiles[t], y[:, t % 2, :]).then_inc(stored[t % 2], 16)
                for s in stored:
                    sp.wait_ge(s, 16 * TT // 2)

            @block.scalar
            def _(act):
                for t in range(TT):
                    if t >= 1:
                        act.wait_ge(summed, t)
                    act.activation(sq[:, :], x[:, t, :], ACT.Square,
                                   accum_out=r[:, 0, t:t + 1]).then_inc(summed, 1)
                    act.wait_ge(summed, t + 1)
                    act.activation(r[:, 1, t:t + 1], r[:, 0, t:t + 1], ACT.Sqrt, bias=eps[:, 0:1],
                                   scale=1 / D).then_inc(rooted, 1)

            @block.vector
            def _(dve):
                dve.wait_ge(loaded, 16)
                for t in range(TT):
                    dve.wait_ge(rooted, t + 1)
                    dve.reciprocal(r[:, 1, t:t + 1], r[:, 1, t:t + 1]).then_inc(inverted, 1)
                    dve.wait_ge(inverted, t + 1)
                    if t >= 2:
                        dve.wait_ge(stored[t % 2], 16 * (t // 2))
                    dve.scalar_tensor_tensor(out=y[:, t % 2, :], in0=x[:, t, :], scalar=r[:, 1, t:t + 1],
                                             in1=gain[:, :], op0=ALU.mult, op1=ALU.mult).then_inc(scaled, 1)


def first_block(core, A, const, cols, x1):
    nc = core.nc
    ident, same64, ones, eps = const[:, 0:128], const[:, 128:256], const[:, 256:384], const[:, 384:385]
    col = lambda n: cols[:, COL[n][0]:COL[n][1]]
    by_rows = lambda name: A[name].rearrange("(k p) n -> p k n", p=P)
    with ExitStack() as out_stack:
        mergedT = core.sb(out_stack, "mergedT", [P, KT, S])
        stack = out_stack.enter_context(ExitStack())
        hT = core.sb(stack, "hT", [P, 2, KT, S], F32R)
        x_rows = A["x"].rearrange("b (t p) d -> (b t) p d", p=P)
        stage_norm_transpose(core, TT, x_rows, col("norm_w"), None, hT, ident, eps)
        w_in = A["w_in"].rearrange("(k p) n -> p k n", p=P)
        ybT = x1[:, 6:8, :]

        def columns(first):
            return lambda j: w_in[:, :, bass.ds(j * P + first, P)]

        stage_features(core, 2, hT, columns(4608), ACT.Silu, lambda j: tile_of(ybT, j))
        with ExitStack() as b_stack:
            oT = x1[:, 0:6, :].rearrange("p (g c) s -> p g c s", g=3)
            maxima = core.sb(b_stack, "maxima", [P, 96])
            sums = core.sb(b_stack, "sums", [P, 96])
            with ExitStack() as qkv_stack:
                v = mergedT[:, 0:6, :].rearrange("p a b -> p (a b)").rearrange("p (t g d) -> p t g d", t=TT, g=3)
                stage_rows(core, [(lambda part, k, g=g, t=t: in_order(hT[:, part, k, :], g, t), 256 * g, 256,
                                   v[:, t, g, :]) for g in range(3) for t in range(TT)], w_in[:, :, 3840:4608], 768)
                qkT = core.sb(qkv_stack, "qkT", [P, 12, S])
                stage_heads(core, 12, hT, S, columns(2304), same64, 1 / 64,
                            lambda j: cols[:, bass.ds(j + COL["bqk"][0], 1)], qkT, eps, room=mergedT[:, 6:8, :])
                table = core.sb(qkv_stack, "bias_table", [P, 8, 256])
                table16 = core.sb(qkv_stack, "bias_table16", [P, 4, 128])
                scratch = nc.dram_tensor("bias_scratch", (3, 4, 384), F32, kind="Internal").ap()
                stage_bias_tables(core, A["rel"], A["onehot"], scratch,
                                  x1[:, 0:3, :].rearrange("p a (b c) -> p (a b) c", b=4), table[:, :, :], table16[:, :, :])
                stage_attention(core, window_units(qkT, v, oT, table, table16, maxima, sums), ident)
            stage_combine(core, maxima, sums, oT, ybT, ident, const[:, SEL:SEL + 256])

        core.clear_semaphores()
        ymT = core.sb(stack, "ymT", [P, 4, S])
        stage_features(core, 4, hT, columns(5376), ACT.Silu, lambda j: tile_of(ymT, j))
        with ExitStack() as m_stack:
            memT = core.sb(m_stack, "memT", [P, 2, KT, MEM], F32R)
            stage_norm_transpose(core, 2, A["mem"].rearrange("b (t p) d -> (b t) p d", p=P),
                                 col("mem_norm_w"), None, memT, ident, eps)
            w_kv = A["m_w_kv"].rearrange("(k p) n -> p k n", p=P)
            mkT = mergedT[:, 0, :].rearrange("p (h t) -> p h t", h=4)
            stage_heads(core, 4, memT, MEM, lambda j: w_kv[:, :, bass.ds(j * P, P)], ones, 1 / 128,
                        lambda j: cols[:, bass.ds(j + COL["mk"][0], 1)], mkT, eps)
            mv = mergedT[:, 1, :].rearrange("p (t d) -> p t d", t=2)
            stage_rows(core, [(lambda part, k, t=t: memT[:, part, k, t * P:(t + 1) * P], 0, M_WIDTH, mv[:, t, :])
                              for t in range(2)], w_kv[:, :, M_WIDTH:2 * M_WIDTH], M_WIDTH)
            mqT = mergedT[:, 2:6, :]
            stage_heads(core, 4, hT, S, columns(4864), ones, 1 / 128,
                        lambda j: cols[:, bass.ds(j + COL["mq"][0], 1)], mqT, eps)
            units = [dict(width=MEM, q=[mqT[:, h, t * P:(t + 1) * P] for h in range(4)],
                          k=[mkT[:, h, :] for h in range(4)], bias=None, sink=None, keep=None,
                          values=lambda h, b: mv[:, b, h * P:(h + 1) * P],
                          out=lambda h, o: o[:, h * P:(h + 1) * P],
                          store=(ymT[:, :, t * P:(t + 1) * P], lambda b: b.rearrange("p (h q) -> p h q", h=4)))
                     for t in range(TT)]
            stage_attention(core, units, ident)

        yaT = x1[:, 0:6, :]
        stage_features(core, 6, hT, columns(0), ACT.Gelu, lambda j: tile_of(yaT, j))
        stage_features(core, 6, hT, columns(2 * A_WIDTH), ACT.Silu, lambda j: tile_of(yaT, j),
                       times=lambda j: tile_of(yaT, j))
        with ExitStack() as a_stack:
            vv = mergedT[:, 0:6, :].rearrange("p a b -> p (a b)").rearrange("p (t d) -> p t d", t=TT)
            wide = mergedT[:, 6:8, 0:A_WIDTH]
            stage_gated_values(core, hT, w_in[:, :, A_WIDTH:2 * A_WIDTH], A["ln_rows"], wide, vv, eps)
            stage_mix_chunks(core, vv, A["spatial_w"], A["spatial_b"], yaT)

        core.clear_semaphores()
        projs = [lambda j, w=by_rows(n): w[:, :, bass.ds(j * P, P)] for n in ("proj_a", "proj_b", "proj_m")]
        gate0 = COL["gate_b"][0]
        stage_merge(core, hT, [(yaT, 6), (ybT, 2), (ymT, 4)],
                    lambda b, j: w_in[:, :, bass.ds(j * P + 5888 + D * b, P)], projs,
                    lambda b, j: cols[:, bass.ds(j + gate0 + KT * b, 1)], mergedT)
        stack.close()
        stage_output(core, mergedT, by_rows("w_out"), lambda t: x_rows[t], None, x1)


def second_block(core, A, const, cols, x1, out):
    nc = core.nc
    ident, eps = const[:, 0:128], const[:, 384:385]
    col = lambda n: cols[:, COL[n][0]:COL[n][1]]
    by_rows = lambda name: A[name].rearrange("(k p) n -> p k n", p=P)
    N = SSM_GROUPS
    with ExitStack() as stack:
        gate = core.sb(stack, "x_gate", [P, D])
        yT = core.sb(stack, "yT", [P, KT, S])
        powers = core.sb(stack, "ssm_powers", [P, 2, LEVELS, N])
        d_cols = core.sb(stack, "ssm_d", [P, N])
        shift = core.sb(stack, "shift", [P, KT])
        gain = core.sb(stack, "gain", [P, KT])
        shapes = ((P, N, 2 * P), (P, N, P), (P, N, N))
        kept = [nc.dram_tensor(f"ssm_kept_{n}", s, F32, kind="Internal").ap() for n, s in enumerate(shapes)]
        with ExitStack() as m_stack:
            stage_modulation(core, A["c"], by_rows("ada_w"), col("ada_b"), A["ada_gate_b"],
                             col("norm_gain"), shift, gain, gate,
                             ssm_matrices_beside(core, m_stack, A["ssm_prm"], A["ssm_bc"], const, kept,
                                                 powers, d_cols))
        room_stack = stack.enter_context(ExitStack())
        room = core.sb(room_stack, "room", [P, 12, S])
        scratch_u = nc.dram_tensor("u_scratch", (N, N, 8, P), F32, kind="Internal").ap()
        scratch_y = nc.dram_tensor("y_scratch", (N, N, 8, P), F32, kind="Internal").ap()
        qT, kT = room[:, 0:4, :], room[:, 4:8, :]
        v = room[:, 8:12, :].rearrange("p a b -> p (a b)").rearrange("p (t d) -> p t d", t=TT)
        with ExitStack() as h_stack:
            h2T = core.sb(h_stack, "h2T", [P, 2, KT, S], F32R)
            stage_norm_transpose(core, TT, x1, gain[:, :], shift[:, :], h2T, ident, eps, from_sbuf=True)
            w_in = by_rows("w_in_2")

            def columns(first):
                return lambda j: w_in[:, :, bass.ds(j * P + first, P)]

            stage_features(core, 2, h2T, columns(256), ACT.Silu, lambda j: tile_of(yT, j))
            stage_features(core, 4, h2T, columns(2048), ACT.Silu, lambda j: tile_of(yT, j + 2))
            stage_features(core, 2, h2T, columns(3072), ACT.Silu, lambda j: tile_of(yT, j + 6))

            stage_features(core, 2, h2T, columns(0), ACT.Copy,
                           lambda j: room[:, j, :].rearrange("p (t c) -> p c t", t=8),
                           order=lambda a: a.rearrange("p (c t) -> p c t", t=8),
                           save=[(scratch_u[8 * j:8 * j + 8].rearrange("g h t c -> (g h) (t c)"), room[:, j, :])
                                 for j in range(2)])

            table = room[:, 0, :].rearrange("p (h w) -> p h w", h=4)
            wqT, wkT = room[:, 1:3, :], room[:, 3:4, :]
            wv = room[:, 4, :].rearrange("p (t d) -> p t d", t=TT)
            stage_swa_tables(core, A["far_window"], table)
            stage_features(core, 2, h2T, lambda j: [w_in[:, :, 2560 + P * n + 64 * j:][:, :, 0:64] for n in range(2)],
                           ACT.Copy, lambda j: tile_of(wqT, j), scale=64 ** -0.5, pieces=2)
            stage_features(core, 1, h2T, columns(2816), ACT.Copy, lambda j: tile_of(wkT, j))
            stage_rows(core, [(lambda part, k, t=t: h2T[:, part, k, t * P:(t + 1) * P], 0, P, wv[:, t, :])
                              for t in range(TT)], w_in[:, :, 2944:3072], P)
            units = []
            for t in range(TT):
                width = 256 if t else P
                rows = [slice(64 * (n // 2), 64 * (n // 2) + 64) for n in range(4)]
                units.append(dict(
                    width=width, keep=None, sink=col("sinks"),
                    q=[wqT[rows[n], n % 2, t * P:(t + 1) * P] for n in range(4)],
                    k=[wkT[rows[n], 0, (t + 1) * P - width:(t + 1) * P] for n in range(4)],
                    bias=[table[:, n, 256 - width:256] for n in range(4)],
                    values=lambda n, b, t=t: wv[:, t - 1 + b if t else 0, 64 * (n // 2):64 * (n // 2) + 64],
                    out=lambda n, o: o[64 * (n % 2):64 * (n % 2) + 64, (n // 2) * P:(n // 2 + 1) * P],
                    store=(yT[:, 6:8, t * P:(t + 1) * P],
                           lambda b: b[:, 0:256].rearrange("p (h q) -> p h q", h=2))))
            core.clear_semaphores()
            stage_attention(core, units, ident)

            stage_features(core, 4, h2T, columns(512), ACT.Copy, lambda j: tile_of(qT, j), scale=64 ** -0.5)
            stage_features(core, 4, h2T, columns(1024), ACT.Copy, lambda j: tile_of(kT, j))
            for c in (0, 256):
                stage_rows(core, [(lambda part, k, t=t: h2T[:, part, k, t * P:(t + 1) * P], 0, 256, v[:, t, c:c + 256])
                                  for t in range(TT)], w_in[:, :, 1536 + c:1792 + c], 256)

        with ExitStack() as d_stack:
            neg_lam = core.sb(d_stack, "neg_lam", [P, 1])
            stage_diff_tables(core, A["lam"], neg_lam)
            o = core.sb(d_stack, "diff_o", [P, TT, 512])
            stage_diff_attention(core, qT, kT, v, A["far"], neg_lam[:, 0:1], ident, o)
            stage_diff_norm(core, o, col("subln"), ident, eps, yT)

        core.clear_semaphores()
        with ExitStack() as s_stack:
            G = core.sb(s_stack, "ssm_G", [P, N, 2 * P])
            M_out = core.sb(s_stack, "ssm_M", [P, N, P])
            c_stack = core.sb(s_stack, "ssm_C", [P, N, N])
            Y = room[:, 0:2, :].rearrange("p a (g c) -> p (a g) c", c=P)
            matrices = [(there, made[:, :, :]) for there, made in zip(kept, (G, M_out, c_stack))]
            stage_ssm_scan(core, matrices, scratch_u, const, ident,
                           G, M_out, c_stack, powers, d_cols, Y)
            stage_ssm_output(core, Y, scratch_y, A["glu_w"].rearrange("(k p) n -> p k n", p=P),
                             col("glu_b"), yT)
        room_stack.close()
        stage_output(core, yT, by_rows("w_out_2"), None, gate[:, :], x1)
        stage_final_norm(core, x1, A["final_gain"], eps, out.rearrange("b (t p) d -> (b t) p d", p=P))


def layers(nc, A, out):
    with ExitStack() as stack:
        core = Core(nc, stack)
        const = core.sb(stack, "const", [P, CONST_COLS])
        cols = core.sb(stack, "cols", [P, COLS])
        x1 = core.sb(stack, "x1", [P, TT, D])
        stage_constants(core, A["const"], A["cols"], const, cols)
        first_block(core, A, const, cols, x1)
        core.clear_semaphores()
        second_block(core, A, const, cols, x1, out)


def pack_columns():
    sizes = [("norm_w", 8), ("mem_norm_w", 8), ("gate_b", 24), ("bqk", 12), ("mq", 4), ("mk", 4),
             ("norm_gain", 8), ("ada_b", 24), ("subln", 1), ("glu_b", 2), ("sinks", 4)]
    at, where = 0, {}
    for name, n in sizes:
        where[name] = (at, at + n)
        at += n
    return where, at


COL, COLS = pack_columns()
SEL, SWAP, SIGN = 512, 768, 385
CONST_COLS = 896


def bucket_rows():
    rows = np.zeros((33, 3, 384), np.float32)
    rows[32] = -1e30
    for g, dilation in enumerate((1, 4, 16)):
        for apart in range(129):
            if g == 2 and (apart % 2 or apart == 128):
                continue
            dist = (apart // 2 if g == 2 else apart) * dilation
            large = 16 + int(np.float32(np.log(np.float32(max(dist, 1)) / np.float32(16))
                                        / np.float32(math.log(2048 / 16))) * np.float32(16))
            rows[dist if dist < 16 else min(large, 31), g, 127 + apart] = 1.0
            rows[32, g, 127 + apart] = 0.0
    return rows


def distances(rows, width, at, limit):
    away = at + np.arange(rows)[:, None] - np.arange(width)[None, :]
    return np.where((away >= 0) & (away < limit), -away.astype(np.float32), np.float32(-1e30)).astype(np.float32)


def ssm_columns(I):
    twice = lambda v: np.concatenate([v, v])
    G = SSM_GROUPS
    return np.ascontiguousarray(np.stack([
        twice(I["ssm_lam_re_2"][0].T), twice(I["ssm_lam_im_2"][0].T),
        np.broadcast_to(I["ssm_log_step_2"][0][None], (P, G)),
        np.concatenate([I["ssm_d_2"][0].reshape(G, G).T] * 8)], axis=1))


def ssm_matrices(I):
    br, bi = (I[n][0].transpose(1, 0, 2) for n in ("ssm_b_re_2", "ssm_b_im_2"))
    cr, ci = (I[n][0].transpose(2, 0, 1) for n in ("ssm_c_re_2", "ssm_c_im_2"))
    stacks = [np.concatenate(pair) for pair in ((br, bi), (bi, br), (cr, ci), (ci, cr))]
    return np.ascontiguousarray(np.stack(stacks, axis=1))


def kernel(**inputs):
    import concourse.bacc as bacc
    from concourse.bass_utils import run_bass_kernel_spmd

    I = {k: np.asarray(v) for k, v in inputs.items()}
    const = np.zeros((P, CONST_COLS), np.float32)
    const[:, 0:128] = np.eye(P)
    const[:, 128:256] = np.kron(np.eye(2), np.ones((64, 64)))
    const[:, 256:384] = 1.0
    const[:, 384] = EPS
    for n, h in enumerate(HEAD_AT):
        at = SEL + P * (h // 2) + 64 * (h % 2)
        const[n, at:at + 64] = 1.0
    for p in range(P):
        const[p, SWAP + (p + 64) % P] = 1.0 if p < 64 else -1.0
    const[:, SIGN] = np.where(np.arange(P) < 64, -1.0, 1.0)

    def by_tile(v):
        return v.reshape(-1, P).T

    def over_partitions(v):
        return np.ascontiguousarray(np.broadcast_to(v[None], (P,) + v.shape))

    two = lambda v: np.concatenate([v, v])[:, None]
    parts = {
        "norm_w": by_tile(I["norm_w"]), "mem_norm_w": by_tile(I["mem_norm_w"]),
        "gate_b": by_tile(I["gate_b"]),
        "bqk": np.concatenate([two(I["b_q_norm_w"])] * 6 + [two(I["b_k_norm_w"])] * 6, 1),
        "mq": np.repeat(I["m_q_norm_w"][:, None], 4, 1), "mk": np.repeat(I["m_k_norm_w"][:, None], 4, 1),
        "norm_gain": by_tile(I["norm_gain_2"]), "ada_b": by_tile(I["ada_b_2"]),
        "subln": I["diff_subln_2"].reshape(P, 1), "glu_b": by_tile(I["glu_b_2"]),
        "sinks": over_partitions(I["swa_sinks_2"].reshape(4)),
    }
    arrays = {
        "const": const,
        "cols": np.ascontiguousarray(np.concatenate([parts[n] for n in COL], axis=1)),
        "x": I["x"], "w_in": I["w_in"], "mem": I["mem"], "m_w_kv": I["m_w_kv"],
        "proj_a": I["proj_a"], "proj_b": I["proj_b"], "proj_m": I["proj_m"], "w_out": I["w_out"],
        "c": by_tile(I["c_2"]), "ada_w": I["ada_w_2"][0], "ada_gate_b": over_partitions(I["ada_b_2"][0, 2 * D:]),
        "w_in_2": I["w_in_2"][0], "w_out_2": I["w_out_2"][0], "glu_w": I["glu_w_2"][0],
        "final_gain": over_partitions(I["final_gain_2"]),
        "lam": over_partitions(np.concatenate([I[n] for n in ("diff_lq1_2", "diff_lk1_2", "diff_lq2_2",
                                                              "diff_lk2_2")])),
        "ssm_prm": ssm_columns(I), "ssm_bc": ssm_matrices(I),
        "far": distances(P, D, 7 * P, D), "far_window": distances(P, 2 * P, P, P),
        "ln_rows": over_partitions(np.stack([I["a_v_norm_w"], I["a_v_norm_b"]])),
        "spatial_w": np.ascontiguousarray(I["a_spatial_w"].transpose(2, 0, 1)),
        "spatial_b": np.ascontiguousarray(np.repeat(I["a_spatial_b"], A_WIDTH // 4, axis=0)
                                          .reshape(6, P, P).transpose(1, 0, 2)), "onehot": bucket_rows(),
        "rel": np.concatenate([I["rel_bias"], np.ones((1, 12), np.float32)]),
    }
    nc = bacc.Bacc("TRN2", target_bir_lowering=False, num_devices=1)
    dram = {n: nc.dram_tensor(n, a.shape, mybir.dt.from_np(a.dtype), kind="ExternalInput").ap()
            for n, a in arrays.items()}
    out = nc.dram_tensor("out", (1, S, D), F32, kind="ExternalOutput").ap()
    layers(nc, dram, out)
    r = run_bass_kernel_spmd(nc, [arrays], core_ids=[0])
    return r.results[0]["out"]
```

```python
import math
from contextlib import ExitStack

import numpy as np

import concourse.bass as bass
from concourse import mybir

ALU = mybir.AluOpType
ACT = mybir.ActivationFunctionType
AX_X = mybir.AxisListType.X
F32 = mybir.dt.float32
I32 = mybir.dt.int32
F32R = mybir.dt.float32r

P = 128
D = 1024
S = 1024
KT = D // P
TT = S // P
HALF = 512
EPS = 1e-6
HEAD_AT = (0, 2, 1, 3)
MEM = 256
A_WIDTH = 768
M_WIDTH = 512
SSM_GROUPS = 16
LEVELS = 7
LAM_INIT = 0.8 - 0.6 * math.exp(0.0)


class Core:

    def __init__(self, nc, stack):
        self.nc, self.stack = nc, stack
        self.psum = stack.enter_context(nc.psum_tensor("psum", [P, 8, HALF], F32))
        self.names, self.sems = 0, []

    def sb(self, stack, name, shape, dt=F32):
        self.names += 1
        return stack.enter_context(self.nc.sbuf_tensor(f"{name}_{self.names}", shape, dt))

    def sem(self, name):
        self.names += 1
        self.sems.append(self.nc.alloc_semaphore(f"{name}_{self.names}"))
        return self.sems[-1]

    def clear_semaphores(self):
        self.nc.clear_and_free_semaphores(self.sems)
        self.nc.all_engine_barrier()
        self.sems = []


def bank(core, first, count=2):
    return core.psum[:, first:first + count, :].rearrange("p a b -> p (a b)")


HI, LO = 0, 1
PASSES = ((LO, HI), (HI, LO), (HI, HI))


def product(pe, out, lhs, rhs, tiles, depth=KT):
    for k in tiles:
        for n, (a, b) in enumerate(PASSES):
            last = pe.matmul(out, lhs(a, k), rhs(b, k), start=(k == 0 and n == 0),
                             stop=(k == depth - 1 and n == 2))
    return last


def walk(engine, n, body, base=0):
    assert base % 2 == 0 and (n % 2 == 0 or n == 1)
    pairs, start = (n + 1) // 2, base // 2
    for u in range(min(n, 2)):
        body(start, u, start == 0, pairs == 1)
    if pairs > 2:
        with engine.Fori(start + 1, start + pairs - 1) as i:
            for u in range(2):
                body(i, u, False, False)
    if pairs > 1:
        for u in range(2):
            body(start + pairs - 1, u, False, True)


class SplitTiles:

    def __init__(self, core, stack, tiles, double=()):
        self.tiles, self.double = tiles, double
        self.n = sum(n for n, _ in tiles)
        self.raw = core.sb(stack, "w_raw", [P, KT, P])
        self.parts = core.sb(stack, "w_parts", [P, 2, 2, KT, P], F32R)
        self.loaded = core.sem("w_loaded")
        self.high = core.sem("w_high")
        self.low = core.sem("w_low")
        self.ahead = False

    def load_tile(self, sp, view):
        if isinstance(view, list):
            for m, part in enumerate(view):
                sp.dma_start(self.raw[:, :, 64 * m:64 * m + 64], part).then_inc(self.loaded, 16)
        else:
            sp.dma_start(self.raw[:, :, :], view).then_inc(self.loaded, 16)

    def fetch(self, sp, group=0):
        n, tile = self.tiles[group]
        base = sum(m for m, _ in self.tiles[:group])

        def one(i, u, first, last):
            if first and u == 0:
                if self.ahead:
                    return
            else:
                sp.wait_ge(self.low, 2 * i + u)
            self.load_tile(sp, tile(2 * i + (u - base)))

        walk(sp, n, one, base)

    def split_high(self, act, i, u):
        extra = 0
        if isinstance(i, int):
            extra = sum(1 for j in range(2 * i + u + 1) if j in self.double)
        act.wait_ge(self.loaded, 16 * (2 * i + (u + 1 + extra)))
        act.copy(self.parts[:, u, HI, :, :], self.raw[:, :, :]).then_inc(self.high, 1)

    def split_low(self, dve, i, u):
        dve.wait_ge(self.high, 2 * i + (u + 1))
        dve.tensor_tensor(self.parts[:, u, LO, :, :], self.raw[:, :, :],
                          self.parts[:, u, HI, :, :].bitcast(F32), ALU.subtract).then_inc(self.low, 1)

    def more(self, i, u, last):
        return not last or 2 * i + u + 2 < self.n

    def first_high(self, act):
        for u in range(1 if self.ahead else 0, min(self.n, 2)):
            self.split_high(act, 0, u)

    def first_low(self, dve):
        for u in range(1 if self.ahead else 0, min(self.n, 2)):
            self.split_low(dve, 0, u)

    def ahead_load(self, sp):
        self.ahead = True
        self.load_tile(sp, self.tiles[0][1](0))

    def ahead_high(self, act):
        self.split_high(act, 0, 0)

    def ahead_low(self, dve):
        self.split_low(dve, 0, 0)

    def ready(self, pe, i, u):
        pe.wait_ge(self.low, 2 * i + (u + 1))

    def lhs(self, u):
        return lambda part, k: self.parts[:, u, part, k, :]


class SplitMatrix:

    def __init__(self, core, stack, weights, ncols):
        self.weights, self.ncols = weights, ncols
        self.raw = core.sb(stack, "w_raw", [P, 2, ncols])
        self.parts = core.sb(stack, "w_parts", [P, 2, KT, ncols], F32R)
        self.loaded = [core.sem("w_loaded") for _ in range(2)]
        self.high = core.sem("w_high")
        self.low = core.sem("w_low")
        self.ahead = False

    def ahead_load(self, sp):
        self.fetch(sp)
        self.ahead = True

    def ahead_high(self, act):
        self.split_high(act, True)

    def ahead_low(self, dve):
        self.split_low(dve, True)

    def fetch(self, sp):
        if self.ahead:
            return
        for k in range(KT):
            if k >= 2:
                sp.wait_ge(self.low, k - 1)
            sp.dma_start(self.raw[:, k % 2, :], self.weights[:, k, :]).then_inc(self.loaded[k % 2], 16)

    def split_high(self, act, ahead=False):
        if self.ahead and not ahead:
            return
        for k in range(KT):
            act.wait_ge(self.loaded[k % 2], 16 * (k // 2 + 1))
            act.copy(self.parts[:, HI, k, :], self.raw[:, k % 2, :]).then_inc(self.high, 1)

    def split_low(self, dve, ahead=False):
        if self.ahead and not ahead:
            return
        for k in range(KT):
            dve.wait_ge(self.high, k + 1)
            dve.tensor_tensor(self.parts[:, LO, k, :], self.raw[:, k % 2, :],
                              self.parts[:, HI, k, :].bitcast(F32), ALU.subtract).then_inc(self.low, 1)

    def products(self, pe, first, outs, lhs, c0s, width):
        for k in range(KT):
            if first:
                pe.wait_ge(self.low, k + 1)
            for out, c0 in zip(outs, c0s):
                last = product(pe, out, lhs, lambda part, j: self.parts[:, part, j, c0:c0 + width], [k])
        return last


def tile_of(ap, j):
    return ap[:, bass.ds(j, 1), :].rearrange("p j t -> p (j t)")


def stage_constants(core, const_dram, cols_dram, const, cols):
    nc = core.nc
    loaded = core.sem("const_loaded")
    with nc.Block(no_gpsimd_drain=True) as block:

        @block.sync
        def _(sp):
            sp.dma_start(const[:, :], const_dram).then_inc(loaded, 16)
            sp.dma_start(cols[:, :], cols_dram).then_inc(loaded, 16)
            sp.wait_ge(loaded, 32)

        @block.vector
        def _(dve):
            dve.wait_ge(loaded, 32)
            for name, factor in (("bqk", 64 ** -0.5), ("mq", 128 ** -0.5)):
                a, b = COL[name][0], COL[name][0] + (6 if name == "bqk" else 4)
                dve.tensor_scalar(cols[:, a:b], cols[:, a:b], factor, None, ALU.mult)


def stage_norm_transpose(core, tiles, src, gain, shift, dst, ident, eps, from_sbuf=False, ahead=None, room=None):
    nc = core.nc
    with ExitStack() as stack:
        xin = None if from_sbuf else core.sb(stack, "xin", [P, 2, D])
        sq = bank(core, 4)
        if room is None:
            room = core.sb(stack, "xn", [P, 4, D])
        xn = room[:, 0:2, :]
        whole = room[:, 2:4, :].rearrange("p s (k t) -> p s k t", k=KT)
        ssq = core.sb(stack, "ssq", [P, tiles])
        std = core.sb(stack, "std", [P, tiles])
        rstd = core.sb(stack, "rstd", [P, tiles])
        x_loaded = [core.sem("x_loaded") for _ in range(2)]
        summed = core.sem("norm_summed")
        rooted = core.sem("norm_rooted")
        inverted = core.sem("norm_inverted")
        scaled = core.sem("norm_scaled")
        turned = core.sem("norm_turned")
        moved = core.sem("norm_moved")
        shifted = core.sem("norm_shifted")
        high = core.sem("norm_high")
        low = core.sem("norm_low")
        rows = [(src[:, t, :] if from_sbuf else xin[:, t % 2, :]) for t in range(tiles)]

        with nc.Block(no_gpsimd_drain=True) as block:

            @block.sync
            def _(sp):
                if from_sbuf:
                    if ahead:
                        ahead.ahead_load(sp)
                    return
                for t in range(tiles):
                    if t >= 2:
                        sp.wait_ge(scaled, t - 1)
                        sp.wait_ge(summed, t - 1)
                    sp.dma_start(rows[t], src[t]).then_inc(x_loaded[t % 2], 16)
                    if ahead and t == 1:
                        ahead.ahead_load(sp)

            def split(act, t):
                act.wait_ge(moved if shift is None else shifted, t + 1)
                act.copy(dst[:, HI, :, t * P:(t + 1) * P], whole[:, t % 2, :, :]).then_inc(high, 1)

            @block.scalar
            def _(act):
                for t in range(tiles):
                    if not from_sbuf:
                        act.wait_ge(x_loaded[t % 2], 16 * (t // 2 + 1))
                    if t >= 1:
                        act.wait_ge(summed, t)
                    act.activation(sq, rows[t], ACT.Square,
                                   accum_out=ssq[:, t:t + 1]).then_inc(summed, 1)
                    act.wait_ge(summed, t + 1)
                    act.activation(std[:, t:t + 1], ssq[:, t:t + 1], ACT.Sqrt,
                                   bias=eps[:, 0:1], scale=1.0 / D).then_inc(rooted, 1)
                    if t >= 2:
                        split(act, t - 2)
                    if ahead and t == 3:
                        ahead.ahead_high(act)
                split(act, tiles - 2)
                split(act, tiles - 1)

            @block.gpsimd
            def _(pool):
                for t in range(tiles):
                    pool.wait_ge(high, t + 1)
                    pool.tensor_tensor(dst[:, LO, :, t * P:(t + 1) * P], whole[:, t % 2, :, :],
                                       dst[:, HI, :, t * P:(t + 1) * P].bitcast(F32), ALU.subtract).then_inc(low, 1)

            def move(dve, t):
                dve.wait_ge(turned, t + 1)
                part = whole[:, t % 2, :, :]
                if t >= 2:
                    dve.wait_ge(high, t - 1)
                    dve.wait_ge(low, t - 1)
                dve.tensor_tensor(part, bank(core, 2 * (t % 2)).rearrange("p (k s) -> p k s", k=KT),
                                  gain.unsqueeze(2).to_broadcast([P, KT, P]), ALU.mult).then_inc(moved, 1)
                if shift is not None:
                    dve.wait_ge(moved, t + 1)
                    dve.tensor_tensor(part, part, shift.unsqueeze(2).to_broadcast([P, KT, P]),
                                      ALU.add).then_inc(shifted, 1)

            @block.vector
            def _(dve):
                for t in range(tiles):
                    dve.wait_ge(rooted, t + 1)
                    dve.reciprocal(rstd[:, t:t + 1], std[:, t:t + 1]).then_inc(inverted, 1)
                    dve.wait_ge(inverted, t + 1)
                    if t >= 2:
                        dve.wait_ge(turned, t - 1)
                    dve.tensor_scalar(xn[:, t % 2, :], rows[t], rstd[:, t:t + 1], None,
                                      ALU.mult).then_inc(scaled, 1)
                    if t >= 1:
                        move(dve, t - 1)
                    if ahead and t == 4:
                        ahead.ahead_low(dve)
                move(dve, tiles - 1)
                dve.wait_ge(low, tiles)

            @block.tensor
            def _(pe):
                for t in range(tiles):
                    pe.wait_ge(scaled, t + 1)
                    if t >= 2:
                        pe.wait_ge(moved, t - 1)
                    for k in range(KT):
                        last = pe.transpose(bank(core, 2 * (t % 2))[:, k * P:(k + 1) * P],
                                            xn[:, t % 2, k * P:(k + 1) * P], ident)
                    last.then_inc(turned, 1)


def stage_heads(core, n, src, tokens, w, same, scale, norm_col, dst, eps, room=None):
    nc = core.nc
    width = min(tokens, HALF)
    halves = [slice(h * width, (h + 1) * width) for h in range(tokens // width)]
    early = 4
    with ExitStack() as stack:
        if not isinstance(w, SplitTiles):
            w = SplitTiles(core, stack, [(n, w)])
        if room is None:
            room = core.sb(stack, "squares_roots", [P, 2, tokens])
        sq, rs = room[:, 0, :], room[:, 1, :]
        projected = core.sem("projected")
        squared = core.sem("squared")
        summed = core.sem("summed")
        rooted = core.sem("rooted")
        inverted = core.sem("inverted")
        normed = core.sem("normed")

        def dense(u):
            return bank(core, 2 * u)[:, 0:tokens]

        sums = bank(core, 4)[:, 0:tokens]

        with nc.Block(no_gpsimd_drain=True) as block:

            @block.sync
            def _(sp):
                w.fetch(sp)

            @block.tensor
            def _(pe):
                def sum_squares(i, u, second):
                    pe.wait_ge(squared, 2 * i + u)
                    if not second:
                        pe.wait_ge(rooted, 2 * i + (u - 1))
                    for h in halves:
                        last = pe.matmul(sums[:, h], same, sq[:, h], start=True, stop=True)
                    last.then_inc(summed, 1)

                def tile(i, u, first, last):
                    w.ready(pe, i, u)
                    if not first:
                        pe.wait_ge(normed, 2 * i + (u - 1))
                    for m, h in enumerate(halves):
                        for tiles in (range(early), range(early, KT)):
                            done = product(pe, dense(u)[:, h], w.lhs(u), lambda part, k: src[:, part, k, h], tiles)
                            if m == 0 and tiles[0] == 0 and not (first and u == 0):
                                sum_squares(i, u, first)
                    done.then_inc(projected, 1)

                walk(pe, n, tile)
                sum_squares(n // 2, 0, False)

            @block.scalar
            def _(act):
                def tile(i, u, first, last):
                    act.wait_ge(projected, 2 * i + (u + 1))
                    if not (first and u == 0):
                        act.wait_ge(summed, 2 * i + u)
                    act.activation(sq[:, :], dense(u), ACT.Square).then_inc(squared, 1)
                    if not last:
                        w.split_high(act, i + 1, u)
                    act.wait_ge(summed, 2 * i + (u + 1))
                    if not (first and u == 0):
                        act.wait_ge(normed, 2 * i + u)
                    act.activation(rs[:, :], sums, ACT.Sqrt, bias=eps[:, 0:1],
                                   scale=scale).then_inc(rooted, 1)

                w.first_high(act)
                walk(act, n, tile)

            @block.vector
            def _(dve):
                def tile(i, u, first, last):
                    if not last:
                        w.split_low(dve, i + 1, u)
                    dve.wait_ge(rooted, 2 * i + (u + 1))
                    dve.reciprocal(rs[:, :], rs[:, :]).then_inc(inverted, 1)
                    dve.wait_ge(inverted, 2 * i + (u + 1))
                    dve.scalar_tensor_tensor(out=tile_of(dst, 2 * i + u),
                                             in0=dense(u), scalar=norm_col(2 * i + u),
                                             in1=rs[:, :], op0=ALU.mult, op1=ALU.mult).then_inc(normed, 1)

                w.first_low(dve)
                walk(dve, n, tile)


def stage_rows(core, src_units, weights, ncols, ahead=None):
    nc = core.nc
    with ExitStack() as stack:
        w = weights if isinstance(weights, SplitMatrix) else SplitMatrix(core, stack, weights, ncols)
        made = core.sem("rows_made")
        kept = [core.sem("rows_kept_dve"), core.sem("rows_kept_act")]

        with nc.Block(no_gpsimd_drain=True) as block:

            @block.sync
            def _(sp):
                w.fetch(sp)
                if ahead:
                    ahead.ahead_load(sp)

            @block.tensor
            def _(pe):
                for n, (lhs, c0, width, _) in enumerate(src_units):
                    if n >= 4:
                        pe.wait_ge(kept[n % 2], n // 2 - 1)
                    w.products(pe, n == 0, [bank(core, n % 4, 1)[:, 0:width]], lhs, [c0],
                               width).then_inc(made, 1)

            @block.vector
            def _(dve):
                w.split_low(dve)
                if ahead:
                    ahead.ahead_low(dve)
                for n, (_, _, width, dst) in enumerate(src_units):
                    if n % 2 == 0:
                        dve.wait_ge(made, n + 1)
                        dve.tensor_copy(dst, bank(core, n % 4, 1)[:, 0:width]).then_inc(kept[0], 1)

            @block.scalar
            def _(act):
                w.split_high(act)
                if ahead:
                    ahead.ahead_high(act)
                for n, (_, _, width, dst) in enumerate(src_units):
                    if n % 2 == 1:
                        act.wait_ge(made, n + 1)
                        act.copy(dst, bank(core, n % 4, 1)[:, 0:width]).then_inc(kept[1], 1)


class Features:

    def __init__(self, n, weights, func, dst, scale=1.0, times=None, view=None, save=(), after_save=False):
        self.n, self.weights, self.func, self.dst, self.scale = n, weights, func, dst, scale
        self.times, self.view, self.written, self.after_save = times, view or (lambda a: a), save, after_save


def feature_weights(core, stack, groups, double=()):
    return SplitTiles(core, stack, [(g.n, g.weights) for g in groups], double)


def stage_features(core, src, groups, w=None, ahead=None):
    nc = core.nc
    base = [sum(g.n for g in groups[:m]) for m in range(len(groups) + 1)]
    gates = [m for m, g in enumerate(groups) if g.times]
    with ExitStack() as stack:
        w = w or feature_weights(core, stack, groups)
        held = core.sb(stack, "held", [P, 2, S]) if gates else None
        projected = core.sem("projected")
        mapped = core.sem("mapped")
        gated = core.sem("gated")
        saved = core.sem("features_saved")
        saves = sum(len(g.written) for g in groups)

        with nc.Block(no_gpsimd_drain=True) as block:

            @block.sync
            def _(sp):
                def save(m):
                    if groups[m].written:
                        sp.wait_ge(mapped, base[m + 1])
                    for there, made in groups[m].written:
                        sp.dma_start(there, made).then_inc(saved, 16)

                for m in range(len(groups)):
                    w.fetch(sp, m)
                    if m:
                        save(m - 1)
                save(len(groups) - 1)
                if ahead:
                    ahead.ahead_load(sp)
                if saves:
                    sp.wait_ge(saved, 16 * saves)

            @block.tensor
            def _(pe):
                def project(i, u, first, last):
                    w.ready(pe, i, u)
                    if not first:
                        pe.wait_ge(mapped, 2 * i + (u - 1))
                    for h in range(2):
                        done = product(pe, bank(core, 2 * u + h, 1), w.lhs(u),
                                       lambda part, k: src[:, part, k, h * HALF:(h + 1) * HALF], range(KT))
                    done.then_inc(projected, 1)

                for m, g in enumerate(groups):
                    walk(pe, g.n, project, base[m])

            @block.scalar
            def _(act):
                w.first_high(act)
                if ahead:
                    ahead.ahead_high(act)
                for m, g in enumerate(groups):
                    if g.after_save:
                        act.wait_ge(saved, 16 * saves)

                    def apply(i, u, first, last):
                        act.wait_ge(projected, 2 * i + (u + 1))
                        if w.more(i, u, last):
                            w.split_high(act, i + 1, u)
                        if g.times and not (last and g.n == 2 or first):
                            act.wait_ge(gated, 2 * i + (u - base[m] - 1))
                        act.activation(held[:, u, :] if g.times else g.dst(2 * i + (u - base[m])),
                                       g.view(bank(core, 2 * u)), g.func, scale=g.scale).then_inc(mapped, 1)

                    def peeled(i, u, first, last):
                        start = base[m] // 2
                        apply(i, u, not last and isinstance(i, int) and i == start, last)

                    walk(act, g.n, peeled, base[m])

            @block.vector
            def _(dve):
                w.first_low(dve)
                if ahead:
                    ahead.ahead_low(dve)
                for m, g in enumerate(groups):

                    def gate(i, u, first, last):
                        if w.more(i, u, last):
                            w.split_low(dve, i + 1, u)
                        if g.times:
                            j = 2 * i + (u - base[m])
                            dve.wait_ge(mapped, 2 * i + (u + 1))
                            dve.tensor_tensor(g.dst(j), g.times(j), held[:, u, :], ALU.mult).then_inc(gated, 1)

                    walk(dve, g.n, gate, base[m])


def stage_bias_tables(core, rel, onehot_dram, scratch, back, table, table16):
    nc = core.nc
    with ExitStack() as stack:
        hot = core.sb(stack, "onehot", [33, 3, 384])
        rb = core.sb(stack, "rel", [33, 12])
        rows = core.sb(stack, "bias_rows", [4, 3, 384])
        loaded = core.sem("onehot_loaded")
        made = core.sem("bias_made")
        copied = core.sem("bias_copied")
        saved = core.sem("bias_saved")
        spread = core.sem("bias_spread")
        with nc.Block(no_gpsimd_drain=True) as block:

            @block.sync
            def _(sp):
                sp.dma_start(hot[:, :, :], onehot_dram).then_inc(loaded, 16)
                sp.dma_start(rb[:, :], rel).then_inc(loaded, 16)
                sp.wait_ge(copied, 3)
                sp.dma_start(scratch.rearrange("g h x -> h g x"), rows[:, :, :]).then_inc(saved, 16)
                sp.wait_ge(saved, 16)
                for g in range(3):
                    width = 256 if g < 2 else P
                    src = bass.AP(scratch.tensor, g * 4 * 384, [[1, P], [384, 4], [1, width]])
                    sp.dma_start(back[:, 4 * g:4 * g + 4, 0:width], src).then_inc(spread, 16)

            @block.tensor
            def _(pe):
                pe.wait_ge(loaded, 32)
                for g in range(3):
                    pe.matmul(bank(core, g, 1)[0:4, 0:384], rb[:, 4 * g:4 * g + 4], hot[:, g, :],
                              start=True, stop=True).then_inc(made, 1)

            @block.vector
            def _(dve):
                for g in range(3):
                    dve.wait_ge(made, g + 1)
                    dve.tensor_copy(rows[:, g, :], bank(core, g, 1)[0:4, 0:384]).then_inc(copied, 1)
                dve.wait_ge(spread, 48)
                dve.tensor_copy(table, back[:, 0:8, ::-1])
                dve.tensor_copy(table16, back[:, 8:12, 127::-1])


def stage_attention(core, units, ident, width_max=256):
    nc = core.nc
    n = len(units)
    with ExitStack() as stack:
        p = core.sb(stack, "p", [P, 2, 4, 256])
        pT = core.sb(stack, "pT", [P, 2, 1024])
        top = core.sb(stack, "top", [P, 2, 4])
        low = core.sb(stack, "low", [P, 2, 4])
        total = core.sb(stack, "total", [P, 2, 4])
        inv = core.sb(stack, "inv", [P, 2, 4])
        extra = core.sb(stack, "extra", [P, 2, 4])
        scored = core.sem("scored")
        maxed = core.sem("maxed")
        small = core.sem("small_steps")
        exped = core.sem("exped")
        weighted = core.sem("weighted")
        turned = core.sem("turned")
        moved_act = core.sem("moved_act")
        moved_dve = core.sem("moved_dve")
        mixed = core.sem("mixed")
        stored = core.sem("stored")
        sinked = core.sem("sinked")
        steps = [0]

        def S_(u):
            return bank(core, 2 * (u % 2)).rearrange("p (h w) -> p h w", h=4)

        def T_():
            return bank(core, 4)

        def O_(u):
            return bank(core, 6 + u % 2, 1)

        with nc.Block(no_gpsimd_drain=True) as block:

            @block.tensor
            def _(pe):
                def scores(u):
                    d = units[u]
                    if u >= 2:
                        pe.wait_ge(maxed, u - 1)
                        pe.wait_ge(exped, u - 1)
                    for h in range(4):
                        last = pe.matmul(S_(u)[:, h, 0:d["width"]], d["q"][h], d["k"][h],
                                         start=True, stop=True)
                    last.then_inc(scored, 1)

                def turn(u):
                    d = units[u]
                    blocks = d["width"] // P
                    pe.wait_ge(weighted, u + 1) if d["keep"] is None else pe.wait_ge(exped, u + 1)
                    if u >= 1:
                        pe.wait_ge(moved_act, u)
                        pe.wait_ge(moved_dve, u)
                    for h in range(4):
                        for b in range(blocks):
                            last = pe.transpose(T_()[:, (2 * h + b) * P:(2 * h + b + 1) * P],
                                                p[:, u % 2, h, b * P:(b + 1) * P], ident)
                    last.then_inc(turned, 1)

                def mix(u):
                    d = units[u]
                    blocks = d["width"] // P
                    pe.wait_ge(moved_act, u + 1)
                    pe.wait_ge(moved_dve, u + 1)
                    if u >= 2:
                        pe.wait_ge(stored, u - 1)
                    for h in range(4):
                        for b in range(blocks):
                            last = pe.matmul(d["out"](h, O_(u)), d["values"](h, b),
                                             pT[:, u % 2, (2 * h + b) * P:(2 * h + b + 1) * P],
                                             start=(b == 0), stop=(b == blocks - 1))
                    last.then_inc(mixed, 1)

                for u in range(n + 2):
                    if u < n:
                        scores(u)
                    if 1 <= u <= n:
                        turn(u - 1)
                    if u >= 2:
                        mix(u - 2)

            @block.vector
            def _(dve):
                def step(ins):
                    steps[0] += 1
                    ins.then_inc(small, 1)
                    dve.wait_ge(small, steps[0])

                def maxima(u):
                    d = units[u]
                    s = u % 2
                    m = d["keep"][0] if d["keep"] else top[:, s, :]
                    dve.wait_ge(scored, u + 1)
                    if u >= 2:
                        dve.wait_ge(turned, u - 1)
                    if d["bias"] is None:
                        step(dve.tensor_reduce(m, S_(u)[:, :, 0:d["width"]], AX_X, ALU.max))
                    else:
                        for h in range(4):
                            last = dve.tensor_tensor_reduce(
                                p[:, s, h, 0:d["width"]], S_(u)[:, h, 0:d["width"]], d["bias"][h],
                                1.0, -3e38, ALU.add, ALU.max, m[:, h:h + 1])
                        step(last)
                    if d["sink"] is not None:
                        step(dve.tensor_tensor(m, m, d["sink"], ALU.max))
                        step(dve.tensor_tensor(extra[:, s, :], d["sink"], m, ALU.subtract))
                    dve.tensor_scalar(low[:, s, :], m, -1.0, None, ALU.mult).then_inc(maxed, 1)

                def weights(u):
                    d = units[u]
                    s = u % 2
                    if d["keep"]:
                        return
                    dve.wait_ge(exped, u + 1)
                    if d["sink"] is not None:
                        step(dve.tensor_tensor(total[:, s, :], total[:, s, :], extra[:, s, :], ALU.add))
                    step(dve.reciprocal(inv[:, s, :], total[:, s, :]))
                    for h in range(4):
                        w = p[:, s, h, 0:d["width"]]
                        last = dve.tensor_scalar(w, w, inv[:, s, h:h + 1], None, ALU.mult)
                    last.then_inc(weighted, 1)

                def move(u):
                    d = units[u]
                    dve.wait_ge(turned, u + 1)
                    if u >= 2:
                        dve.wait_ge(mixed, u - 1)
                    view = lambda a: a[:, 512:1024].rearrange("p (h w) -> p h w", h=2)[:, :, 0:d["width"]]
                    dve.tensor_copy(view(pT[:, u % 2, :]), view(T_())).then_inc(moved_dve, 1)

                def store(u):
                    dve.wait_ge(mixed, u + 1)
                    dst, view = units[u]["store"]
                    if units[u]["keep"]:
                        dve.tensor_copy(dst, view(O_(u))).then_inc(stored, 1)
                    else:
                        dve.tensor_tensor(dst, view(O_(u)), dst, ALU.mult).then_inc(stored, 1)

                for u in range(n + 3):
                    if 2 <= u < n + 2:
                        move(u - 2)
                    if 1 <= u <= n:
                        weights(u - 1)
                    if u < n:
                        maxima(u)
                    if u >= 3:
                        store(u - 3)

            @block.scalar
            def _(act):
                def move(u):
                    d = units[u]
                    act.wait_ge(turned, u + 1)
                    if u >= 2:
                        act.wait_ge(mixed, u - 1)
                    view = lambda a: a[:, 0:512].rearrange("p (h w) -> p h w", h=2)[:, :, 0:d["width"]]
                    act.copy(view(pT[:, u % 2, :]), view(T_())).then_inc(moved_act, 1)

                def exps(u):
                    d = units[u]
                    s = u % 2
                    sums = d["keep"][1] if d["keep"] else total[:, s, :]
                    act.wait_ge(maxed, u + 1)
                    if u >= 2 and not d["keep"]:
                        act.wait_ge(weighted, u - 1)
                    if d["sink"] is not None:
                        act.activation(extra[:, s, :], extra[:, s, :], ACT.Exp)
                    for h in range(4):
                        into = p[:, s, h, 0:d["width"]]
                        src = S_(u)[:, h, 0:d["width"]] if d["bias"] is None else into
                        last = act.activation(into, src, ACT.Exp, bias=low[:, s, h:h + 1],
                                              accum_out=sums[:, h:h + 1])
                    last.then_inc(exped, 1)

                for u in range(n + 2):
                    if u >= 2:
                        move(u - 2)
                    if u < n:
                        exps(u)


def in_order(ap, g, t):
    if g == 0:
        return ap[:, t * P:(t + 1) * P]
    if g == 1:
        return ap.rearrange("p (l r) -> p r l", r=4)[:, t // 2, (t % 2) * P:(t % 2 + 1) * P]
    return ap.rearrange("p (l r) -> p r l", r=8)[:, t, :]


def window_units(qkT, v, oT, table, table16, maxima, sums):
    units = []
    for g in range(3):
        for t in range(TT):
            before = (g == 0 and t > 0) or (g == 1 and t % 2 == 1)
            width = 256 if before else 128
            q, k, bias = [], [], []
            for h in HEAD_AT:
                rows = slice(64 * (h % 2), 64 * (h % 2) + 64)
                q.append(in_order(qkT[rows, 2 * g + h // 2, :], g, t))
                kk = qkT[rows, 6 + 2 * g + h // 2, :]
                if not before:
                    k.append(in_order(kk, g, t))
                elif g == 0:
                    k.append(kk[:, (t - 1) * P:(t + 1) * P])
                else:
                    k.append(kk.rearrange("p (l r) -> p r l", r=4)[:, t // 2, :])
                bias.append(table16[:, h, :] if g == 2 else table[:, 4 * g + h, 256 - width:256])
            at = 4 * (g * TT + t)

            def values(n, b, g=g, t=t, before=before):
                h = HEAD_AT[n]
                return v[:, t - 1 + b if before else t, g, 64 * h:64 * h + 64]

            def out(n, o):
                h = HEAD_AT[n]
                return o[64 * (h % 2):64 * (h % 2) + 64, (h // 2) * P:(h // 2 + 1) * P]

            o = oT[:, g, :, :]
            if g == 0:
                dst = o[:, :, t * P:(t + 1) * P]
                view = lambda b: b[:, 0:256].rearrange("p (h q) -> p h q", h=2)
            elif g == 1:
                dst = o.rearrange("p h (l r) -> p h r l", r=4)[:, :, t // 2, (t % 2) * P:(t % 2 + 1) * P]
                view = lambda b: b[:, 0:256].rearrange("p (h q) -> p h q", h=2)
            else:
                dst = o.rearrange("p h (l r) -> p h r l", r=8)[:, :, t, :]
                view = lambda b: b[:, 0:256].rearrange("p (h q) -> p h q", h=2)
            units.append(dict(width=width, q=q, k=k, bias=bias, sink=None, values=values, out=out,
                              store=(dst, view), keep=(maxima[:, at:at + 4], sums[:, at:at + 4])))
    return units


def stage_combine(core, maxima, sums, oT, ybT, ident, sel):
    nc = core.nc
    with ExitStack() as stack:
        rows = core.sb(stack, "lse_rows", [4, 2, 3, S])
        top = core.sb(stack, "lse_top", [4, S])
        prod = core.sb(stack, "prod", [P, S])
        acc = core.sb(stack, "weighed_sum", [P, S])
        turned = core.sem("lse_turned")
        moved = core.sem("lse_moved")
        chain = core.sem("lse_chain")
        topped = core.sem("lse_topped")
        exped = core.sem("lse_exped")
        ready = core.sem("lse_ready")
        spread = core.sem("lse_spread")
        used = core.sem("lse_used")
        m = rows[:, 0, :, :]
        l = rows[:, 1, :, :]
        with nc.Block(no_gpsimd_drain=True) as block:

            @block.tensor
            def _(pe):
                for n in range(6):
                    w, g = n // 3, n % 3
                    if n >= 2:
                        pe.wait_ge(moved, n - 1)
                    for t in range(TT):
                        src = (maxima, sums)[w][:, 4 * (g * TT + t):4 * (g * TT + t) + 4]
                        last = pe.transpose(bank(core, 2 * (n % 2))[0:4, t * P:(t + 1) * P], src, ident)
                    last.then_inc(turned, 1)
                pe.wait_ge(ready, 1)
                for n in range(6):
                    pair, g = n // 3, n % 3
                    if n >= 2:
                        pe.wait_ge(used, n - 1)
                    for h in range(2):
                        last = pe.matmul(bank(core, 4 + 2 * (n % 2) + h, 1), sel[0:4, pair * P:(pair + 1) * P],
                                         m[:, g, h * HALF:(h + 1) * HALF], start=True, stop=True)
                    last.then_inc(spread, 1)

            @block.vector
            def _(dve):
                done = [0]

                def step(ins):
                    done[0] += 1
                    ins.then_inc(chain, 1)
                    dve.wait_ge(chain, done[0])

                for n in range(6):
                    w, g = n // 3, n % 3
                    dve.wait_ge(turned, n + 1)
                    r = (1, 4, 8)[g]
                    dst = rows[:, w, g, :].rearrange("p (l r) -> p r l", r=r)
                    dve.tensor_copy(dst, bank(core, 2 * (n % 2))[0:4, :].rearrange("p (r l) -> p r l", r=r))\
                       .then_inc(moved, 1)
                dve.wait_ge(moved, 6)
                step(dve.tensor_tensor(top[:, :], m[:, 0, :], m[:, 1, :], ALU.max))
                step(dve.tensor_tensor(top[:, :], top[:, :], m[:, 2, :], ALU.max))
                for g in range(3):
                    last = dve.tensor_tensor(m[:, g, :], m[:, g, :], top[:, :], ALU.subtract)
                last.then_inc(topped, 1)
                dve.wait_ge(exped, 1)
                step(dve.tensor_tensor(l, l, m, ALU.mult))
                step(dve.tensor_tensor(top[:, :], l[:, 0, :], l[:, 1, :], ALU.add))
                step(dve.tensor_tensor(top[:, :], top[:, :], l[:, 2, :], ALU.add))
                step(dve.reciprocal(top[:, :], top[:, :]))
                for g in range(3):
                    last = dve.tensor_tensor(m[:, g, :], m[:, g, :], top[:, :], ALU.mult)
                last.then_inc(ready, 1)
                for n in range(6):
                    pair, g = n // 3, n % 3
                    dve.wait_ge(spread, n + 1)
                    y = acc[:, :]
                    dst = y if g == 0 else prod[:, :]
                    dve.tensor_tensor(dst, bank(core, 4 + 2 * (n % 2)), oT[:, g, pair, :],
                                      ALU.mult).then_inc(used, 1)
                    if g > 0:
                        dve.wait_ge(used, n + 1)
                        step(dve.tensor_tensor(y, y, prod[:, :], ALU.add))
                    if g == 2:
                        step(dve.tensor_tensor(ybT[:, pair, :], ybT[:, pair, :], y, ALU.mult))

            @block.scalar
            def _(act):
                act.wait_ge(topped, 1)
                act.activation(m, m, ACT.Exp).then_inc(exped, 1)


def stage_gated_values(core, src, weights, wide_dram, wide, vv, eps):
    nc = core.nc
    width = A_WIDTH // 2
    with ExitStack() as stack:
        w = SplitMatrix(core, stack, weights, A_WIDTH)
        act_v = w.raw
        sq = bank(core, 4)[:, 0:A_WIDTH]
        part = core.sb(stack, "ln_part", [P, 2, 2])
        mean = core.sb(stack, "ln_mean", [P, 2])
        ssq = core.sb(stack, "ln_ssq", [P, 2])
        rstd = core.sb(stack, "ln_rstd", [P, 2])
        wide_loaded = core.sem("ln_rows_loaded")
        made = core.sem("values_made")
        mapped = core.sem("values_mapped")
        squared = core.sem("values_squared")
        rooted = core.sem("values_rooted")
        done = core.sem("values_done")
        chain = core.sem("values_chain")

        with nc.Block(no_gpsimd_drain=True) as block:

            @block.sync
            def _(sp):
                sp.dma_start(wide[:, :, :], wide_dram).then_inc(wide_loaded, 16)
                w.fetch(sp)

            @block.tensor
            def _(pe):
                for t in range(TT):
                    if t >= 2:
                        pe.wait_ge(mapped, t - 1)
                    w.products(pe, t == 0, [bank(core, 2 * (t % 2) + h, 1)[:, 0:width] for h in range(2)],
                               lambda part, k: src[:, part, k, t * P:(t + 1) * P], [0, width],
                               width).then_inc(made, 1)

            @block.scalar
            def _(act):
                def gelu(t):
                    act.wait_ge(made, t + 1)
                    if t >= 2:
                        act.wait_ge(done, t - 1)
                    for h in range(2):
                        last = act.activation(act_v[:, t % 2, h * width:(h + 1) * width],
                                              bank(core, 2 * (t % 2) + h, 1)[:, 0:width], ACT.Gelu,
                                              accum_out=part[:, t % 2, h:h + 1])
                    last.then_inc(mapped, 1)

                def root(t):
                    act.wait_ge(squared, t + 1)
                    act.activation(rstd[:, t % 2:t % 2 + 1], ssq[:, t % 2:t % 2 + 1], ACT.Sqrt,
                                   bias=eps[:, 0:1], scale=1 / A_WIDTH).then_inc(rooted, 1)

                w.split_high(act)
                act.wait_ge(w.low, KT)
                for t in range(TT + 1):
                    if t < TT:
                        gelu(t)
                    if t >= 1:
                        root(t - 1)

            @block.vector
            def _(dve):
                steps = [0]

                def step(ins):
                    steps[0] += 1
                    ins.then_inc(chain, 1)
                    dve.wait_ge(chain, steps[0])

                w.split_low(dve)
                for t in range(TT):
                    s = t % 2
                    dve.wait_ge(mapped, t + 1)
                    dve.wait_ge(wide_loaded, 16)
                    step(dve.tensor_tensor(mean[:, s:s + 1], part[:, s, 0:1], part[:, s, 1:2], ALU.add))
                    step(dve.tensor_scalar(mean[:, s:s + 1], mean[:, s:s + 1], 1 / A_WIDTH, None, ALU.mult))
                    x = act_v[:, s, :]
                    step(dve.tensor_scalar(x, x, mean[:, s:s + 1], None, ALU.subtract))
                    dve.tensor_tensor_reduce(sq[:, :], x, x, 1.0, 0.0, ALU.mult, ALU.add,
                                             ssq[:, s:s + 1]).then_inc(squared, 1)
                    dve.wait_ge(rooted, t + 1)
                    step(dve.reciprocal(rstd[:, s:s + 1], rstd[:, s:s + 1]))
                    step(dve.scalar_tensor_tensor(out=vv[:, t, :], in0=x, scalar=rstd[:, s:s + 1],
                                                  in1=wide[:, 0, :], op0=ALU.mult, op1=ALU.mult))
                    dve.tensor_tensor(vv[:, t, :], vv[:, t, :], wide[:, 1, :], ALU.add).then_inc(done, 1)


def stage_merge(core, hT, ys, w, gate_tile, proj_tiles, gate_b, mergedT):
    nc = core.nc
    depth = [y[1] for y in ys]
    with ExitStack() as stack:
        wp = core.sb(stack, "w_proj", [P, 2, 6, P])
        gate = core.sb(stack, "gate", [P, 2, S])
        prod = core.sb(stack, "gated", [P, 2, S])
        loaded = [core.sem("merge_loaded") for _ in range(2)]
        made = core.sem("merge_made")
        opened = core.sem("merge_opened")
        used = core.sem("merge_used")
        summed = core.sem("merge_summed")

        def unit(i, n):
            return 2 * i + n // 3, n % 3, n % 2, 6 * i + n

        def sixes(engine, body):
            for n in range(6):
                body(0, n, n < 2, False)
            with engine.Fori(1, 3) as i:
                for n in range(6):
                    body(i, n, False, False)
            for n in range(6):
                body(3, n, False, n >= 4)

        def next_split(split, engine, i, n):
            split(engine, 3 * i + (n // 2 + 1), n % 2)

        with nc.Block(no_gpsimd_drain=True) as block:

            @block.sync
            def _(sp):
                def load_projection(i, n):
                    j, b, s, u = unit(i, n)
                    sp.dma_start(wp[:, s, 0:depth[b], :], proj_tiles[b](j)).then_inc(loaded[s], 16)

                def load(i, n, first, last):
                    j, b, s, u = unit(i, n)
                    if not (first and n == 0):
                        sp.wait_ge(w.low, u)
                        w.load_tile(sp, gate_tile(b, j))
                    if not (first and n == 0):
                        load_projection(i if n else i - 1, n - 1 if n else 5)

                sixes(sp, load)
                sp.wait_ge(w.low, 24)
                load_projection(3, 5)

            @block.tensor
            def _(pe):
                def products(i, n, first, last):
                    j, b, s, u = unit(i, n)
                    w.ready(pe, 3 * i + n // 2, s)
                    if not first:
                        pe.wait_ge(used, u - 1)
                    for h in range(2):
                        product(pe, bank(core, 4 * s + h, 1), w.lhs(s),
                                lambda part, k: hT[:, part, k, h * HALF:(h + 1) * HALF], range(KT))
                    pe.wait_ge(loaded[s], 48 * i + 16 * (n // 2) + 16)
                    for h in range(2):
                        for k in range(depth[b]):
                            last = pe.matmul(bank(core, 4 * s + 2 + h, 1), wp[:, s, k, :],
                                             ys[b][0][:, k, h * HALF:(h + 1) * HALF],
                                             start=(k == 0), stop=(k == depth[b] - 1))
                    last.then_inc(made, 1)

                sixes(pe, products)

            @block.scalar
            def _(act):
                def sigmoid(i, n, first, last):
                    j, b, s, u = unit(i, n)
                    act.wait_ge(made, u + 1)
                    if not last:
                        next_split(w.split_high, act, i, n)
                    if not first:
                        act.wait_ge(used, u - 1)
                    act.activation(gate[:, s, :], bank(core, 4 * s), ACT.Sigmoid,
                                   bias=gate_b(b, j)).then_inc(opened, 1)

                w.first_high(act)
                sixes(act, sigmoid)

            @block.vector
            def _(dve):
                def gated_sum(i, n, first, last):
                    j, b, s, u = unit(i, n)
                    if not last:
                        next_split(w.split_low, dve, i, n)
                    dve.wait_ge(opened, u + 1)
                    dst = mergedT[:, j, :] if b == 0 else prod[:, s, :]
                    if b == 1 and not first:
                        dve.wait_ge(summed, 4 * i + 2 * (n // 3))
                    dve.tensor_tensor(dst, bank(core, 4 * s + 2), gate[:, s, :], ALU.mult).then_inc(used, 1)
                    if b > 0:
                        dve.wait_ge(used, u + 1)
                        if b == 2:
                            dve.wait_ge(summed, 4 * i + 2 * (n // 3) + 1)
                        dve.tensor_tensor(mergedT[:, j, :], mergedT[:, j, :], prod[:, s, :],
                                          ALU.add).then_inc(summed, 1)

                w.first_low(dve)
                sixes(dve, gated_sum)


def stage_mix_chunks(core, vv, spatial_dram, spatial_b_dram, yaT, ahead):
    nc = core.nc
    with ExitStack() as stack:
        wT = core.sb(stack, "spatial_w", [P, 4, P])
        bias = core.sb(stack, "spatial_b", [P, 6, P])
        held = core.sb(stack, "spatial_sum", [P, 2, S])
        loaded = core.sem("spatial_loaded")
        masked = core.sem("spatial_masked")
        made = core.sem("spatial_made")
        added = core.sem("spatial_added")
        with nc.Block(no_gpsimd_drain=True) as block:

            @block.sync
            def _(sp):
                sp.dma_start(wT[:, :, :], spatial_dram).then_inc(loaded, 16)
                sp.dma_start(bias[:, :, :], spatial_b_dram).then_inc(loaded, 16)
                ahead.ahead_load(sp)

            @block.scalar
            def _(act):
                ahead.ahead_high(act)

            @block.gpsimd
            def _(pool):
                pool.wait_ge(loaded, 32)
                pool.affine_select(out=wT[:, :, :], in_=wT[:, :, :], compare_op=ALU.is_ge, fill=0.0, base=0,
                                   pattern=[[0, 4], [1, P]], channel_multiplier=-1).then_inc(masked, 1)

            @block.tensor
            def _(pe):
                pe.wait_ge(masked, 1)
                for c in range(6):
                    if c >= 2:
                        pe.wait_ge(added, c - 1)
                    for t in range(TT):
                        for rows in ([slice(0, 64), slice(64, 128)] if c in (1, 4) else [slice(0, 128)]):
                            first = c * P + rows.start
                            last = pe.matmul(bank(core, 2 * (c % 2))[rows, t * P:(t + 1) * P],
                                             vv[:, t, first:first + rows.stop - rows.start],
                                             wT[:, first // 192, :], start=True, stop=True)
                    last.then_inc(made, 1)

            @block.vector
            def _(dve):
                for c in range(6):
                    s = c % 2
                    dve.wait_ge(made, c + 1)
                    split = lambda a: a.rearrange("p (n t) -> p n t", t=P)
                    dve.tensor_tensor(split(held[:, s, :]), split(bank(core, 2 * s)),
                                      bias[:, c, :].unsqueeze(1).to_broadcast([P, TT, P]),
                                      ALU.add).then_inc(added, 1)
                    dve.wait_ge(added, c + 1)
                    if c == 1:
                        ahead.ahead_low(dve)
                    dve.tensor_tensor(yaT[:, c, :], yaT[:, c, :], held[:, s, :], ALU.mult)


def stage_output(core, yT, weights, base_tile, gate, dst, final=None):
    nc = core.nc
    with ExitStack() as stack:
        w = SplitMatrix(core, stack, weights, D)
        y = core.sb(stack, "y_parts", [P, 2, 2, KT, P], F32R)
        base = core.sb(stack, "base", [P, 2, D]) if base_tile else None
        base_loaded = [core.sem("base_loaded") for _ in range(2)]
        y_high = core.sem("y_high")
        y_low = core.sem("y_low")
        made = core.sem("out_made")
        gated = core.sem("out_gated")
        added = core.sem("out_added")
        if final:
            final_gain, eps, out_tiles = final
            gain = core.sb(stack, "final_gain", [P, D])
            sq = core.sb(stack, "final_sq", [P, D])
            rows_out = core.sb(stack, "final_y", [P, 2, D])
            stat = core.sb(stack, "final_stat", [P, 2, TT])
            gain_loaded = core.sem("final_gain_loaded")
            summed = core.sem("final_summed")
            rooted = core.sem("final_rooted")
            inverted = core.sem("final_inverted")
            scaled = core.sem("final_scaled")
            stored = [core.sem("final_stored") for _ in range(2)]
        tokens = lambda t: yT[:, :, t * P:(t + 1) * P]
        with nc.Block(no_gpsimd_drain=True) as block:

            @block.sync
            def _(sp):
                w.fetch(sp)
                if base_tile:
                    for t in range(TT):
                        if t >= 2:
                            sp.wait_ge(added, t - 1)
                        sp.dma_start(base[:, t % 2, :], base_tile(t)).then_inc(base_loaded[t % 2], 16)
                if final:
                    sp.dma_start(gain[:, :], final_gain).then_inc(gain_loaded, 16)
                    for t in range(TT):
                        sp.wait_ge(scaled, t + 1)
                        sp.dma_start(out_tiles[t], rows_out[:, t % 2, :]).then_inc(stored[t % 2], 16)
                    for s in stored:
                        sp.wait_ge(s, 16 * TT // 2)

            @block.tensor
            def _(pe):
                for t in range(TT):
                    pe.wait_ge(y_low, t + 1)
                    if t >= 2:
                        pe.wait_ge(added, t - 1)
                    w.products(pe, t == 0, [bank(core, 2 * (t % 2) + h, 1) for h in range(2)],
                               lambda part, k: y[:, t % 2, part, k, :], [0, HALF], HALF).then_inc(made, 1)

            @block.scalar
            def _(act):
                def split(t):
                    if t >= 2:
                        act.wait_ge(made, t - 1)
                    act.copy(y[:, t % 2, HI, :, :], tokens(t)).then_inc(y_high, 1)

                def root(t):
                    act.wait_ge(added, t + 1)
                    if t >= 1:
                        act.wait_ge(summed, t)
                    act.activation(sq[:, :], dst[:, t, :], ACT.Square,
                                   accum_out=stat[:, 0, t:t + 1]).then_inc(summed, 1)
                    act.wait_ge(summed, t + 1)
                    act.activation(stat[:, 1, t:t + 1], stat[:, 0, t:t + 1], ACT.Sqrt, bias=eps[:, 0:1],
                                   scale=1 / D).then_inc(rooted, 1)

                split(0)
                split(1)
                w.split_high(act)
                for t in range(2, TT):
                    split(t)
                    if final:
                        root(t - 2)
                if final:
                    root(TT - 2)
                    root(TT - 1)

            @block.vector
            def _(dve):
                def split(t):
                    dve.wait_ge(y_high, t + 1)
                    dve.tensor_tensor(y[:, t % 2, LO, :, :], tokens(t), y[:, t % 2, HI, :, :].bitcast(F32),
                                      ALU.subtract).then_inc(y_low, 1)

                def scale(t):
                    dve.wait_ge(rooted, t + 1)
                    dve.reciprocal(stat[:, 1, t:t + 1], stat[:, 1, t:t + 1]).then_inc(inverted, 1)
                    dve.wait_ge(inverted, t + 1)
                    if t >= 2:
                        dve.wait_ge(stored[t % 2], 16 * (t // 2))
                    dve.scalar_tensor_tensor(out=rows_out[:, t % 2, :], in0=dst[:, t, :],
                                             scalar=stat[:, 1, t:t + 1], in1=gain[:, :], op0=ALU.mult,
                                             op1=ALU.mult).then_inc(scaled, 1)

                split(0)
                split(1)
                w.split_low(dve)
                if final:
                    dve.wait_ge(gain_loaded, 16)
                for t in range(TT):
                    dve.wait_ge(made, t + 1)
                    if t + 2 < TT:
                        split(t + 2)
                    rows = bank(core, 2 * (t % 2))
                    if base_tile:
                        dve.wait_ge(base_loaded[t % 2], 16 * (t // 2) + 16)
                        dve.tensor_tensor(dst[:, t, :], rows, base[:, t % 2, :], ALU.add).then_inc(added, 1)
                    else:
                        dve.tensor_tensor(rows, rows, gate, ALU.mult).then_inc(gated, 1)
                        dve.wait_ge(gated, t + 1)
                        dve.tensor_tensor(dst[:, t, :], rows, dst[:, t, :], ALU.add).then_inc(added, 1)
                    if final and t >= 1:
                        scale(t - 1)
                if final:
                    scale(TT - 1)


def stage_modulation(core, cond_cols, ada, ada_b, gate_b, norm_gain, shift, gain, gate, beside):
    nc = core.nc
    load_beside, vector_beside, save_beside = beside
    with ExitStack() as stack:
        w = core.sb(stack, "ada_w", [P, 2, KT, D])
        wide = core.sb(stack, "cond_wide", [P, KT, P])
        cond = core.sb(stack, "cond", [P, KT])
        loaded = [core.sem("ada_loaded") for _ in range(2)]
        c_loaded = core.sem("cond_loaded")
        silued = core.sem("cond_silu")
        made = core.sem("mod_made")
        used = core.sem("mod_used")
        with nc.Block(no_gpsimd_drain=True) as block:

            @block.sync
            def _(sp):
                load_beside(sp)
                sp.dma_start(cond[:, :], cond_cols).then_inc(c_loaded, 16)
                sp.dma_start(gate[:, :], gate_b).then_inc(c_loaded, 16)
                for n in range(3):
                    if n == 2:
                        sp.wait_ge(made, 1)
                    sp.dma_start(w[:, n % 2, :, :], ada[:, :, n * D:(n + 1) * D]).then_inc(loaded[n % 2], 16)
                save_beside(sp)

            @block.scalar
            def _(act):
                act.wait_ge(c_loaded, 32)
                act.activation(cond[:, :], cond[:, :], ACT.Silu).then_inc(silued, 1)
                act.wait_ge(silued, 1)
                act.copy(wide[:, :, :], cond[:, :].unsqueeze(2).to_broadcast([P, KT, P])).then_inc(silued, 1)

            @block.tensor
            def _(pe):
                pe.wait_ge(silued, 2)
                for n in range(2):
                    pe.wait_ge(loaded[n], 16)
                    for j in range(KT):
                        for k in range(KT):
                            last = pe.matmul(bank(core, n, 1)[:, j:j + 1], w[:, n, k, j * P:(j + 1) * P],
                                             cond[:, k:k + 1], start=(k == 0), stop=(k == KT - 1))
                    last.then_inc(made, 1)
                pe.wait_ge(loaded[0], 32)
                for h in range(2):
                    for k in range(KT):
                        last = pe.matmul(bank(core, 2 + h, 1), wide[:, k, :], w[:, 0, k, h * HALF:(h + 1) * HALF],
                                         start=(k == 0), stop=(k == KT - 1))
                last.then_inc(made, 1)

            @block.vector
            def _(dve):
                vector_beside(dve)
                dve.wait_ge(made, 1)
                dve.tensor_tensor(shift[:, :], bank(core, 0, 1)[:, 0:KT], ada_b[:, 0:KT], ALU.add)
                dve.wait_ge(made, 2)
                dve.tensor_tensor(gain[:, :], bank(core, 1, 1)[:, 0:KT], ada_b[:, KT:2 * KT], ALU.add)\
                   .then_inc(used, 1)
                dve.wait_ge(used, 1)
                dve.scalar_tensor_tensor(out=gain[:, :], in0=gain[:, :], scalar=1.0, in1=norm_gain,
                                         op0=ALU.add, op1=ALU.mult)
                dve.wait_ge(made, 3)
                dve.wait_ge(c_loaded, 32)
                dve.tensor_tensor(gate[:, :], bank(core, 2), gate[:, :], ALU.add)


LN2_HI = 0.693359375
LN2_LO = -2.12194440e-4
ROUND = 1.5 * 2 ** 23
TWO_PI = (6.28125, 1.9340515e-3, 1.2556660e-6)


def ssm_matrices_beside(core, stack, prm_dram, bc_dram, const, kept, powers, d_cols):
    nc = core.nc
    N = SSM_GROUPS
    G = core.sb(stack, "ssm_G", [P, N, 2 * P])
    M_out = core.sb(stack, "ssm_M", [P, N, P])
    c_stack = core.sb(stack, "ssm_C", [P, N, N])
    prm = core.sb(stack, "ssm_prm", [P, 4, N])
    bc = core.sb(stack, "ssm_bc", [P, 4, N, N])
    tiny = core.sb(stack, "ssm_tiny", [P, 12, N])
    whole = core.sb(stack, "ssm_int", [P, N], I32)
    pre = core.sb(stack, "ssm_pw_re", [P, 9, N])
    pim = core.sb(stack, "ssm_pw_im", [P, 9, N])
    mats = core.sb(stack, "ssm_mats", [P, 4, N, N])
    tmp = core.sb(stack, "ssm_tmp", [P, N, N])
    loaded = core.sem("ssm_loaded")
    chain = core.sem("ssm_chain")
    sign = const[:, SIGN:SIGN + 1]
    finished = core.sem("ssm_finished")
    saved = core.sem("ssm_saved")

    def load(sp):
        sp.dma_start(prm[:, :, :], prm_dram).then_inc(loaded, 16)
        sp.dma_start(bc[:, :, :, :], bc_dram).then_inc(loaded, 16)

    def save(sp):
        sp.wait_ge(finished, 1)
        for there, made in zip(kept, (G, M_out, c_stack)):
            sp.dma_start(there, made[:, :, :]).then_inc(saved, 16)
        sp.wait_ge(saved, 16 * len(kept))

    def vector(dve):
        steps = [0]

        def step(ins):
            steps[0] += 1
            ins.then_inc(chain, 1)
            dve.wait_ge(chain, steps[0])

        def tt(out, a, b, op):
            step(dve.tensor_tensor(out, a, b, op))

        def ts(out, a, s1, op1, s2=None, op2=ALU.bypass):
            if s2 is None:
                step(dve.tensor_scalar(out, a, s1, None, op1))
            else:
                step(dve.tensor_scalar(out, a, s1, s2, op1, op2))

        def stt(out, a, s, b, op1, op2):
            step(dve.scalar_tensor_tensor(out=out, in0=a, scalar=s, in1=b, op0=op1, op1=op2))

        def horner(acc, x, coeffs):
            ts(acc, x, coeffs[-1], ALU.mult)
            for c in reversed(coeffs[:-1]):
                stt(acc, acc, c, x, ALU.add, ALU.mult)

        def exponential(out, x, k, r):
            ts(x, x, -87.0, ALU.max, 88.7, ALU.min)
            ts(k, x, 1 / math.log(2), ALU.mult)
            ts(k, k, ROUND, ALU.add)
            ts(k, k, ROUND, ALU.subtract)
            stt(r, k, -LN2_HI, x, ALU.mult, ALU.add)
            stt(r, k, -LN2_LO, r, ALU.mult, ALU.add)
            horner(out, r, [1 / math.factorial(i) for i in range(1, 10)])
            ts(out, out, 1.0, ALU.add)
            ts(k, k, 127.0, ALU.add)
            ts(k, k, 2.0 ** 23, ALU.mult)
            step(dve.tensor_copy(whole[:, :], k))
            tt(out, out, whole[:, :].bitcast(F32), ALU.mult)

        dve.wait_ge(loaded, 32)
        lr, li, ls, dd = (prm[:, i, :] for i in range(4))
        stepv, mag, ang, cosv, sinv, a, b, c, den, fr, fi, ai = (tiny[:, i, :] for i in range(12))
        step(dve.tensor_copy(d_cols[:, :], dd))
        exponential(stepv, ls, a, b)
        tt(c, lr, stepv, ALU.mult)
        exponential(mag, c, a, b)
        tt(ang, li, stepv, ALU.mult)
        ts(a, ang, 1 / (2 * math.pi), ALU.mult)
        ts(a, a, ROUND, ALU.add)
        ts(a, a, ROUND, ALU.subtract)
        for part in TWO_PI:
            stt(ang, a, -part, ang, ALU.mult, ALU.add)
        ts(ang, ang, 0.5, ALU.mult)
        tt(b, ang, ang, ALU.mult)
        horner(sinv, b, [(-1) ** i / math.factorial(2 * i + 1) for i in range(1, 8)])
        stt(sinv, sinv, 1.0, ang, ALU.add, ALU.mult)
        horner(cosv, b, [(-1) ** i / math.factorial(2 * i) for i in range(1, 9)])
        ts(cosv, cosv, 1.0, ALU.add)
        tt(c, sinv, cosv, ALU.mult)
        tt(cosv, sinv, sinv, ALU.mult)
        ts(cosv, cosv, -2.0, ALU.mult, 1.0, ALU.add)
        stt(pim[:, 1, :], c, 2.0, mag, ALU.mult, ALU.mult)
        tt(pre[:, 1, :], cosv, mag, ALU.mult)
        ar, ai = pre[:, 1, :], pim[:, 1, :]
        tt(a, lr, lr, ALU.mult)
        tt(den, li, li, ALU.mult)
        tt(den, den, a, ALU.add)
        step(dve.reciprocal(den, den))
        ts(c, ar, -1.0, ALU.add)
        tt(a, c, lr, ALU.mult)
        tt(b, ai, li, ALU.mult)
        tt(fr, a, b, ALU.add)
        tt(fr, fr, den, ALU.mult)
        tt(a, ai, lr, ALU.mult)
        tt(b, c, li, ALU.mult)
        tt(fi, a, b, ALU.subtract)
        tt(fi, fi, den, ALU.mult)

        def times(outr, outi, xr, xi, yr, yi):
            tt(a, xr, yr, ALU.mult)
            tt(b, xi, yi, ALU.mult)
            tt(outr, a, b, ALU.subtract)
            tt(a, xr, yi, ALU.mult)
            tt(b, xi, yr, ALU.mult)
            tt(outi, a, b, ALU.add)

        for k in range(1, 8):
            times(pre[:, k + 1, :], pim[:, k + 1, :], pre[:, k, :], pim[:, k, :], ar, ai)
        step(dve.tensor_copy(powers[:, 0, 0, :], pre[:, 8, :]))
        step(dve.tensor_copy(powers[:, 1, 0, :], pim[:, 8, :]))
        for k in range(1, LEVELS):
            r, i = powers[:, 0, k - 1, :], powers[:, 1, k - 1, :]
            times(powers[:, 0, k, :], powers[:, 1, k, :], r, i, r, i)

        wide = lambda v: v.unsqueeze(2).to_broadcast([P, N, N])
        B, iB, C, iC = (mats[:, i, :, :] for i in range(4))
        b1, b2, c1, c2 = (bc[:, i, :, :] for i in range(4))
        ts(b2, b2, sign, ALU.mult)
        tt(B, b1, wide(fr), ALU.mult)
        tt(tmp[:, :, :], b2, wide(fi), ALU.mult)
        tt(B, B, tmp[:, :, :], ALU.add)
        tt(iB, b2, wide(fr), ALU.mult)
        tt(tmp[:, :, :], b1, wide(fi), ALU.mult)
        tt(iB, iB, tmp[:, :, :], ALU.subtract)
        ts(C, c1, sign, ALU.mult, -1.0, ALU.mult)
        ts(iC, c2, -1.0, ALU.mult)
        step(dve.memset(G[:, :, P:2 * P], 0.0))

        def mix(out, r, i, x, y):
            tt(out, x, wide(r), ALU.mult)
            tt(tmp[:, :, :], y, wide(i), ALU.mult)
            tt(out, out, tmp[:, :, :], ALU.add)

        step(dve.tensor_copy(G[:, :, 7 * N:8 * N], B))
        for k in range(1, 8):
            mix(G[:, :, (7 - k) * N:(8 - k) * N], pre[:, k, :], pim[:, k, :], B, iB)
        for t in range(8):
            mix(M_out[:, :, t * N:(t + 1) * N], pre[:, t + 1, :], pim[:, t + 1, :], C, iC)
        dve.tensor_copy(c_stack[:, :, :], C).then_inc(finished, 1)

    return load, vector, save


def stage_ssm_scan(core, L_room, scratch_u, const, ident, G, M_out, c_stack, powers, d_cols, Y):
    nc = core.nc
    N = SSM_GROUPS
    with ExitStack() as stack:
        U = core.sb(stack, "ssm_U", [P, N, P])
        Gt = core.sb(stack, "ssm_Gt", [P, N, P])
        T = core.sb(stack, "ssm_T", [P, N, P])
        X = core.sb(stack, "ssm_X", [P, N, P])
        L_late = core.sb(stack, "ssm_L", [P, 2, N, P])
        spread = core.sem("u_spread")
        turned = core.sem("g_turned")
        g_kept = core.sem("g_kept")
        t_made = core.sem("t_made")
        t_kept = core.sem("t_kept")
        v_made = core.sem("v_made")
        x_new = core.sem("x_new")
        diag = core.sem("level_diag")
        level = core.sem("level_ready")
        carried = core.sem("carried")
        y_made = core.sem("y_made")
        swap = const[:, SWAP:SWAP + P]

        def L(k):
            return L_room[:, k, :, :] if k < LEVELS - 2 else L_late[:, k - LEVELS + 2, :, :]

        with nc.Block(no_gpsimd_drain=True) as block:

            @block.sync
            def _(sp):
                for t in range(8):
                    sp.dma_start(U[N * t:N * t + N, :, :],
                                 scratch_u[:, :, t, :].rearrange("g h c -> h g c")).then_inc(spread, 16)

            @block.tensor
            def _(pe):
                for a in range(4):
                    for g in range(4 * a, 4 * a + 4):
                        last = pe.transpose(bank(core, a, 1)[:, (g % 4) * P:(g % 4 + 1) * P],
                                            G[:, g, 0:P], ident)
                    last.then_inc(turned, 1)
                for a in range(4):
                    for g in range(4 * a, 4 * a + 4):
                        for t in range(8):
                            at = (g % 4) * P + t * N
                            last = pe.matmul(bank(core, 4 + a, 1)[:, at:at + N],
                                             G[:, g, (7 - t) * N:(7 - t) * N + P], c_stack[:, g, :],
                                             start=True, stop=True)
                    last.then_inc(t_made, 1)
                pe.wait_ge(spread, 128)
                for a in range(4):
                    pe.wait_ge(g_kept, a + 1)
                    for g in range(4 * a, 4 * a + 4):
                        last = pe.matmul(bank(core, a, 1)[:, (g % 4) * P:(g % 4 + 1) * P],
                                         Gt[:, g, :], U[:, g, :], start=True, stop=True)
                    last.then_inc(v_made, 1)
                for k in range(LEVELS):
                    pe.wait_ge(level, k + 1)
                    for a in range(4):
                        pe.wait_ge(x_new, 4 * k + a + 1)
                        for g in range(4 * a, 4 * a + 4):
                            width = P - 2 ** k
                            last = pe.matmul(bank(core, a, 1)[:, (g % 4) * P:(g % 4) * P + width],
                                             L(k)[:, g, :], X[:, g, 0:width], start=True, stop=True)
                        last.then_inc(carried, 1)
                pe.wait_ge(t_kept, 1)
                for a in range(4):
                    pe.wait_ge(x_new, 4 * LEVELS + a + 1)
                    for g in range(4 * a, 4 * a + 4):
                        at = (g % 4) * P
                        pe.matmul(bank(core, 4 + a, 1)[:, at:at + P], T[:, g, :], U[:, g, :],
                                  start=True, stop=False)
                        last = pe.matmul(bank(core, 4 + a, 1)[:, at + 1:at + P], M_out[:, g, :],
                                         X[:, g, 0:P - 1], start=False, stop=True)
                    last.then_inc(y_made, 1)

            @block.scalar
            def _(act):
                def diagonals(k):
                    for g in range(N):
                        last = act.activation(L(k)[:, g, :], ident, ACT.Copy, scale=powers[:, 0, k, g:g + 1])
                    last.then_inc(diag, 1)

                for k in range(LEVELS):
                    diagonals(k)
                    if 2 <= k < 6:
                        a = k - 2
                        act.wait_ge(turned, a + 1)
                        act.copy(Gt[:, 4 * a:4 * a + 4, :].rearrange("p g s -> p (g s)"),
                                 bank(core, a, 1)).then_inc(g_kept, 1)
                for a in range(4):
                    act.wait_ge(y_made, a + 1)
                    act.copy(Y[:, 4 * a:4 * a + 4, :].rearrange("p g s -> p (g s)"), bank(core, 4 + a, 1))

            @block.vector
            def _(dve):
                def level_matrices(k):
                    dve.wait_ge(diag, k + 1)
                    for g in range(N):
                        m = L(k)[:, g, :]
                        last = dve.scalar_tensor_tensor(out=m, in0=swap, scalar=powers[:, 1, k, g:g + 1],
                                                        in1=m, op0=ALU.mult, op1=ALU.add)
                    last.then_inc(level, 1)

                for k in range(5):
                    level_matrices(k)
                for a in range(4):
                    dve.wait_ge(t_made, a + 1)
                    for g in range(4 * a, 4 * a + 4):
                        last = dve.scalar_tensor_tensor(
                            out=T[:, g, :], in0=ident, scalar=d_cols[:, g:g + 1],
                            in1=bank(core, 4 + a, 1)[:, (g % 4) * P:(g % 4 + 1) * P],
                            op0=ALU.mult, op1=ALU.add)
                last.then_inc(t_kept, 1)
                level_matrices(5)
                level_matrices(6)
                for a in range(4):
                    dve.wait_ge(v_made, a + 1)
                    dve.tensor_copy(X[:, 4 * a:4 * a + 4, :].rearrange("p g s -> p (g s)"),
                                    bank(core, a, 1)).then_inc(x_new, 1)
                for k in range(LEVELS):
                    for a in range(4):
                        dve.wait_ge(carried, 4 * k + a + 1)
                        later = X[:, 4 * a:4 * a + 4, 2 ** k:P]
                        dve.tensor_tensor(later, later,
                                          bank(core, a, 1).rearrange("p (g s) -> p g s", g=4)[:, :, 0:P - 2 ** k],
                                          ALU.add).then_inc(x_new, 1)


def stage_ssm_output(core, Y, scratch_y, glu_dram, glu_b, yT):
    nc = core.nc
    N = SSM_GROUPS
    with ExitStack() as stack:
        ys = core.sb(stack, "ssm_ys", [P, 2, S])
        sig = core.sb(stack, "ssm_sig", [P, 2, S])
        w = core.sb(stack, "glu_w", [P, 2, 2 * P])
        saved = core.sem("y_saved")
        loaded = core.sem("y_loaded")
        mapped = core.sem("y_mapped")
        made = core.sem("glu_made")
        opened = core.sem("glu_opened")
        gated = core.sem("glu_gated")
        with nc.Block(no_gpsimd_drain=True) as block:

            @block.sync
            def _(sp):
                sp.dma_start(w[:, :, :], glu_dram).then_inc(loaded, 16)
                for t in range(8):
                    sp.dma_start(scratch_y[:, :, t, :].rearrange("g h c -> h g c"),
                                 Y[N * t:N * t + N, :, :]).then_inc(saved, 16)
                sp.wait_ge(saved, 128)
                for j in range(2):
                    sp.dma_start(ys[:, j, :], scratch_y[8 * j:8 * j + 8].rearrange("g h t c -> (g h) (t c)"))\
                      .then_inc(loaded, 16)

            @block.scalar
            def _(act):
                act.wait_ge(loaded, 48)
                act.activation(ys[:, :, :], ys[:, :, :], ACT.Gelu_apprx_tanh).then_inc(mapped, 1)
                for m in range(2):
                    act.wait_ge(made, m + 1)
                    act.activation(sig[:, m, :], bank(core, 2 * m), ACT.Sigmoid,
                                   bias=glu_b[:, m:m + 1]).then_inc(opened, 1)

            @block.tensor
            def _(pe):
                pe.wait_ge(mapped, 1)
                for m in range(2):
                    for h in range(2):
                        for k in range(2):
                            last = pe.matmul(bank(core, 2 * m + h, 1), w[:, k, m * P:(m + 1) * P],
                                             ys[:, k, h * HALF:(h + 1) * HALF], start=(k == 0), stop=(k == 1))
                    last.then_inc(made, 1)

            @block.vector
            def _(dve):
                for m in range(2):
                    dve.wait_ge(opened, m + 1)
                    dve.tensor_tensor(sig[:, m, :], ys[:, m, :], sig[:, m, :], ALU.mult).then_inc(gated, 1)
                    dve.wait_ge(gated, m + 1)
                    by_chunk = yT[:, m, :].rearrange("p (c t) -> p c t", t=8)
                    dve.tensor_tensor(by_chunk, by_chunk, sig[:, m, :].rearrange("p (t c) -> p c t", t=8),
                                      ALU.mult)


def stage_diff_tables(core, lam_dram, neg_lam):
    nc = core.nc
    with ExitStack() as stack:
        rows = core.sb(stack, "lam_rows", [P, 4, 64])
        prod = core.sb(stack, "lam_prod", [P, 64])
        dots = core.sb(stack, "lam_dots", [P, 2])
        loaded = core.sem("lam_loaded")
        dotted = core.sem("lam_dotted")
        exped = core.sem("lam_exped")
        with nc.Block(no_gpsimd_drain=True) as block:

            @block.sync
            def _(sp):
                sp.dma_start(rows[:, :, :], lam_dram).then_inc(loaded, 16)

            @block.vector
            def _(dve):
                dve.wait_ge(loaded, 16)
                for i in range(2):
                    dve.tensor_tensor_reduce(prod[:, :], rows[:, 2 * i, :], rows[:, 2 * i + 1, :], 1.0, 0.0,
                                             ALU.mult, ALU.add, dots[:, i:i + 1]).then_inc(dotted, 1)
                    dve.wait_ge(dotted, i + 1)
                dve.wait_ge(exped, 1)
                dve.tensor_tensor(neg_lam[:, :], dots[:, 1:2], dots[:, 0:1], ALU.subtract).then_inc(dotted, 1)
                dve.wait_ge(dotted, 3)
                dve.tensor_scalar(neg_lam[:, :], neg_lam[:, :], -LAM_INIT, None, ALU.add)

            @block.scalar
            def _(act):
                act.wait_ge(dotted, 2)
                act.activation(dots[:, :], dots[:, :], ACT.Exp).then_inc(exped, 1)


def stage_diff_attention(core, qT, kT, v, far_dram, neg_lam, ident, out, loads):
    nc = core.nc
    units = [(h, t) for h in range(4) for t in range(TT)]
    n = len(units)
    with ExitStack() as stack:
        far = core.sb(stack, "far", [P, D])
        bias = core.sb(stack, "alibi", [P, 2, D])
        p = core.sb(stack, "diff_p", [P, 3, 2, D])
        pT = core.sb(stack, "diff_pT", [P, 2, D])
        top = core.sb(stack, "diff_top", [P, 2, 2])
        low = core.sb(stack, "diff_low", [P, 2, 2])
        total = core.sb(stack, "diff_total", [P, 2, 2])
        inv = core.sb(stack, "diff_inv", [P, 2, 2])
        far_loaded = core.sem("far_loaded")
        loaded = core.sem("later_inputs_loaded")
        scored = core.sem("diff_scored")
        maxed = core.sem("diff_maxed")
        small = core.sem("diff_small")
        exped = core.sem("diff_exped")
        weighted = core.sem("diff_weighted")
        turned = core.sem("diff_turned")
        moved_act = core.sem("diff_moved_act")
        moved_dve = core.sem("diff_moved_dve")
        mixed = core.sem("diff_mixed")
        stored = core.sem("diff_stored")

        def place(b):
            return HALF * (b % 2) + P * (b // 2)

        with nc.Block(no_gpsimd_drain=True) as block:

            @block.sync
            def _(sp):
                sp.dma_start(far[:, :], far_dram).then_inc(far_loaded, 16)
                for there, into in loads:
                    sp.dma_start(into[:, :, :], there).then_inc(loaded, 16)
                sp.wait_ge(loaded, 16 * len(loads))

            @block.tensor
            def _(pe):
                def scores(u):
                    h, t = units[u]
                    width = (t + 1) * P
                    if u >= 1:
                        pe.wait_ge(maxed, u)
                    for c0 in range(0, width, HALF):
                        cw = min(HALF, width - c0)
                        for m in range(2):
                            rows = slice(64 * m, 64 * m + 64)
                            last = pe.matmul(bank(core, 2 * m)[:, c0:c0 + cw], qT[rows, h, t * P:(t + 1) * P],
                                             kT[rows, h, c0:c0 + cw], start=True, stop=True)
                    last.then_inc(scored, 1)

                def turn(u):
                    h, t = units[u]
                    pe.wait_ge(weighted, u + 1)
                    if u >= 1:
                        pe.wait_ge(moved_act, u)
                        pe.wait_ge(moved_dve, u)
                    for b in range(t + 1):
                        last = pe.transpose(bank(core, 4)[:, place(b):place(b) + P],
                                            p[:, u % 3, 0, b * P:(b + 1) * P], ident)
                    last.then_inc(turned, 1)

                def mix(u):
                    h, t = units[u]
                    pe.wait_ge(moved_act, u + 1)
                    pe.wait_ge(moved_dve, u + 1)
                    if u >= 2:
                        pe.wait_ge(stored, u - 1)
                    for b in range(t + 1):
                        last = pe.matmul(bank(core, 6 + u % 2, 1)[:, 0:P], pT[:, u % 2, place(b):place(b) + P],
                                         v[:, b, h * P:(h + 1) * P], start=(b == 0), stop=(b == t))
                    last.then_inc(mixed, 1)

                for u in range(n + 3):
                    if u < n:
                        scores(u)
                    if 2 <= u < n + 2:
                        turn(u - 2)
                    if u >= 3:
                        mix(u - 3)

            @block.vector
            def _(dve):
                steps = [0]

                def step(ins):
                    steps[0] += 1
                    ins.then_inc(small, 1)
                    dve.wait_ge(small, steps[0])

                def slopes(h):
                    step(dve.tensor_scalar(bias[:, h % 2, :], far[:, :], 2.0 ** -(5 + h), None, ALU.mult))

                def maxima(u):
                    h, t = units[u]
                    s = u % 2
                    width = (t + 1) * P
                    if t == 0:
                        slopes(h)
                    dve.wait_ge(scored, u + 1)
                    if u >= 3:
                        dve.wait_ge(turned, u - 2)
                    for m in range(2):
                        last = dve.tensor_tensor_reduce(
                            p[:, u % 3, m, 0:width], bank(core, 2 * m)[:, 0:width], bias[:, h % 2, D - width:D],
                            1.0, -3e38, ALU.add, ALU.max, top[:, s, m:m + 1])
                    step(last)
                    dve.tensor_scalar(low[:, s, :], top[:, s, :], -1.0, None, ALU.mult).then_inc(maxed, 1)

                def weights(u):
                    h, t = units[u]
                    s = u % 2
                    width = (t + 1) * P
                    dve.wait_ge(exped, u + 1)
                    step(dve.reciprocal(inv[:, s, :], total[:, s, :]))
                    step(dve.tensor_scalar(inv[:, s, 1:2], inv[:, s, 1:2], neg_lam, None, ALU.mult))
                    p1, p2 = p[:, u % 3, 0, 0:width], p[:, u % 3, 1, 0:width]
                    step(dve.tensor_scalar(p2, p2, inv[:, s, 1:2], None, ALU.mult))
                    dve.scalar_tensor_tensor(out=p1, in0=p1, scalar=inv[:, s, 0:1], in1=p2, op0=ALU.mult,
                                             op1=ALU.add).then_inc(weighted, 1)

                def move(u):
                    h, t = units[u]
                    dve.wait_ge(turned, u + 1)
                    if u >= 2:
                        dve.wait_ge(mixed, u - 1)
                    if t == 0:
                        dve.sem_inc(moved_dve, 1)
                        return
                    odd = (t + 1) // 2 * P
                    dve.tensor_copy(pT[:, u % 2, HALF:HALF + odd],
                                    bank(core, 5, 1)[:, 0:odd]).then_inc(moved_dve, 1)

                def store(u):
                    h, t = units[u]
                    dve.wait_ge(mixed, u + 1)
                    dve.tensor_copy(out[:, t, h * P:(h + 1) * P], bank(core, 6 + u % 2, 1)[:, 0:P])\
                       .then_inc(stored, 1)

                dve.wait_ge(far_loaded, 16)
                for u in range(n + 4):
                    if 1 <= u <= n:
                        weights(u - 1)
                    if u < n:
                        maxima(u)
                    if 2 <= u < n + 2:
                        move(u - 2)
                    if u >= 4:
                        store(u - 4)

            @block.scalar
            def _(act):
                def move(u):
                    h, t = units[u]
                    act.wait_ge(turned, u + 1)
                    if u >= 2:
                        act.wait_ge(mixed, u - 1)
                    even = (t + 2) // 2 * P
                    act.copy(pT[:, u % 2, 0:even], bank(core, 4, 1)[:, 0:even]).then_inc(moved_act, 1)

                def exps(u):
                    h, t = units[u]
                    s = u % 2
                    width = (t + 1) * P
                    act.wait_ge(maxed, u + 1)
                    if u >= 2:
                        act.wait_ge(weighted, u - 1)
                    for m in range(2):
                        last = act.activation(p[:, u % 3, m, 0:width], p[:, u % 3, m, 0:width], ACT.Exp,
                                              bias=low[:, s, m:m + 1], accum_out=total[:, s, m:m + 1])
                    last.then_inc(exped, 1)

                for u in range(n + 2):
                    if u < n:
                        exps(u)
                    if u >= 2:
                        move(u - 2)


def stage_diff_norm(core, o, subln, ident, eps, yT):
    nc = core.nc
    with ExitStack() as stack:
        sq = core.sb(stack, "dn_sq", [P, TT * 512])
        r = core.sb(stack, "dn_r", [P, 4 * TT])
        sub = core.sb(stack, "dn_sub", [P, 1])
        squared = core.sem("dn_squared")
        rooted = core.sem("dn_rooted")
        chain = core.sem("dn_chain")
        scaled = core.sem("dn_scaled")
        turned = core.sem("dn_turned")
        moved = core.sem("dn_moved")
        heads = lambda a: a.rearrange("p (h d) -> p h d", d=P)
        with nc.Block(no_gpsimd_drain=True) as block:

            @block.vector
            def _(dve):
                dve.tensor_scalar(sub[:, :], subln, 1.0 - LAM_INIT, None, ALU.mult).then_inc(chain, 1)
                flat = o.rearrange("p t d -> p (t d)")
                dve.tensor_tensor(sq[:, :], flat, flat, ALU.mult).then_inc(chain, 1)
                dve.wait_ge(chain, 2)
                dve.tensor_reduce(r[:, :], heads(sq[:, :]), AX_X, ALU.add).then_inc(squared, 1)
                dve.wait_ge(rooted, 1)
                dve.reciprocal(r[:, :], r[:, :]).then_inc(chain, 1)
                dve.wait_ge(chain, 3)
                for t in range(TT):
                    dve.tensor_tensor(heads(o[:, t, :]), heads(o[:, t, :]),
                                      r[:, 4 * t:4 * t + 4].unsqueeze(2).to_broadcast([P, 4, P]),
                                      ALU.mult).then_inc(scaled, 1)
                for t in range(TT):
                    dve.wait_ge(turned, t + 1)
                    y = yT[:, 2:6, t * P:(t + 1) * P]
                    dve.scalar_tensor_tensor(out=y, in0=heads(bank(core, t % 4, 1)), scalar=sub[:, 0:1], in1=y,
                                             op0=ALU.mult, op1=ALU.mult).then_inc(moved, 1)

            @block.scalar
            def _(act):
                act.wait_ge(squared, 1)
                act.activation(r[:, :], r[:, :], ACT.Sqrt, bias=eps[:, 0:1], scale=1 / P).then_inc(rooted, 1)

            @block.tensor
            def _(pe):
                for t in range(TT):
                    pe.wait_ge(scaled, t + 1)
                    if t >= 4:
                        pe.wait_ge(moved, t - 3)
                    for h in range(4):
                        last = pe.transpose(bank(core, t % 4, 1)[:, h * P:(h + 1) * P],
                                            o[:, t, h * P:(h + 1) * P], ident)
                    last.then_inc(turned, 1)


def stage_swa_inputs(core, far_dram, table, v, ident):
    nc = core.nc
    with ExitStack() as stack:
        far = core.sb(stack, "swa_far", [P, 256])
        loaded = core.sem("swa_far_loaded")
        turned = core.sem("swa_v_turned")
        with nc.Block(no_gpsimd_drain=True) as block:

            @block.sync
            def _(sp):
                sp.dma_start(far[:, :], far_dram).then_inc(loaded, 16)

            @block.tensor
            def _(pe):
                for t in range(TT):
                    last = pe.transpose(bank(core, 0)[:, t * P:(t + 1) * P], v[:, t * P:(t + 1) * P], ident)
                last.then_inc(turned, 1)

            @block.scalar
            def _(act):
                act.wait_ge(turned, 1)
                act.copy(v, bank(core, 0))

            @block.vector
            def _(dve):
                dve.wait_ge(loaded, 16)
                for h in range(4):
                    dve.tensor_scalar(table[:, h, :], far[:, :], 2.0 ** -(1 + h), None, ALU.mult)


def first_block(core, A, const, cols, x1):
    nc = core.nc
    ident, same64, ones, eps = const[:, 0:128], const[:, 128:256], const[:, 256:384], const[:, 384:385]
    col = lambda n: cols[:, COL[n][0]:COL[n][1]]
    by_rows = lambda name: A[name].rearrange("(k p) n -> p k n", p=P)
    with ExitStack() as out_stack:
        mergedT = core.sb(out_stack, "mergedT", [P, KT, S])
        stack = out_stack.enter_context(ExitStack())
        hT = core.sb(stack, "hT", [P, 2, KT, S], F32R)
        x_rows = A["x"].rearrange("b (t p) d -> (b t) p d", p=P)
        w_in = A["w_in"].rearrange("(k p) n -> p k n", p=P)
        ybT = x1[:, 6:8, :]

        def columns(first):
            return lambda j: w_in[:, :, bass.ds(j * P + first, P)]

        with ExitStack() as b_stack:
            oT = x1[:, 0:6, :].rearrange("p (g c) s -> p g c s", g=3)
            maxima = core.sb(b_stack, "maxima", [P, 96])
            sums = core.sb(b_stack, "sums", [P, 96])
            v = mergedT[:, 0:6, :].rearrange("p a b -> p (a b)").rearrange("p (t g d) -> p t g d", t=TT, g=3)
            with ExitStack() as w_stack:
                gate_b = [Features(2, columns(4608), ACT.Silu, lambda j: tile_of(ybT, j))]
                w_z = feature_weights(core, w_stack, gate_b)
                stage_norm_transpose(core, TT, x_rows, col("norm_w"), None, hT, ident, eps, ahead=w_z)
                w_v = SplitMatrix(core, w_stack, w_in[:, :, 3840:4608], 768)
                stage_features(core, hT, gate_b, w_z, ahead=w_v)
                stage_rows(core, [(lambda part, k, g=g, t=t: in_order(hT[:, part, k, :], g, t), 256 * g, 256,
                                   v[:, t, g, :]) for g in range(3) for t in range(TT)], w_v, 768)
            with ExitStack() as qkv_stack:
                qkT = core.sb(qkv_stack, "qkT", [P, 12, S])
                stage_heads(core, 12, hT, S, columns(2304), same64, 1 / 64,
                            lambda j: cols[:, bass.ds(j + COL["bqk"][0], 1)], qkT, eps, room=mergedT[:, 6:8, :])
                table = core.sb(qkv_stack, "bias_table", [P, 8, 256])
                table16 = core.sb(qkv_stack, "bias_table16", [P, 4, 128])
                scratch = nc.dram_tensor("bias_scratch", (3, 4, 384), F32, kind="Internal").ap()
                stage_bias_tables(core, A["rel"], A["onehot"], scratch,
                                  x1[:, 0:3, :].rearrange("p a (b c) -> p (a b) c", b=4), table[:, :, :], table16[:, :, :])
                stage_attention(core, window_units(qkT, v, oT, table, table16, maxima, sums), ident)
            stage_combine(core, maxima, sums, oT, ybT, ident, const[:, SEL:SEL + 256])

        core.clear_semaphores()
        ymT = core.sb(stack, "ymT", [P, 4, S])
        yaT = x1[:, 0:6, :]
        stage_features(core, hT, [
            Features(4, columns(5376), ACT.Silu, lambda j: tile_of(ymT, j)),
            Features(6, columns(0), ACT.Gelu, lambda j: tile_of(yaT, j)),
            Features(6, columns(2 * A_WIDTH), ACT.Silu, lambda j: tile_of(yaT, j),
                     times=lambda j: tile_of(yaT, j))])
        with ExitStack() as m_stack:
            memT = core.sb(m_stack, "memT", [P, 2, KT, MEM], F32R)
            stage_norm_transpose(core, 2, A["mem"].rearrange("b (t p) d -> (b t) p d", p=P),
                                 col("mem_norm_w"), None, memT, ident, eps)
            w_kv = A["m_w_kv"].rearrange("(k p) n -> p k n", p=P)
            mkT = mergedT[:, 0, :].rearrange("p (h t) -> p h t", h=4)
            stage_heads(core, 4, memT, MEM, lambda j: w_kv[:, :, bass.ds(j * P, P)], ones, 1 / 128,
                        lambda j: cols[:, bass.ds(j + COL["mk"][0], 1)], mkT, eps)
            mv = mergedT[:, 1, :].rearrange("p (t d) -> p t d", t=2)
            stage_rows(core, [(lambda part, k, t=t: memT[:, part, k, t * P:(t + 1) * P], 0, M_WIDTH, mv[:, t, :])
                              for t in range(2)], w_kv[:, :, M_WIDTH:2 * M_WIDTH], M_WIDTH)
            mqT = mergedT[:, 2:6, :]
            stage_heads(core, 4, hT, S, columns(4864), ones, 1 / 128,
                        lambda j: cols[:, bass.ds(j + COL["mq"][0], 1)], mqT, eps)
            units = [dict(width=MEM, q=[mqT[:, h, t * P:(t + 1) * P] for h in range(4)],
                          k=[mkT[:, h, :] for h in range(4)], bias=None, sink=None, keep=None,
                          values=lambda h, b: mv[:, b, h * P:(h + 1) * P],
                          out=lambda h, o: o[:, h * P:(h + 1) * P],
                          store=(ymT[:, :, t * P:(t + 1) * P], lambda b: b.rearrange("p (h q) -> p h q", h=4)))
                     for t in range(TT)]
            stage_attention(core, units, ident)

        vv = mergedT[:, 0:6, :].rearrange("p a b -> p (a b)").rearrange("p (t d) -> p t d", t=TT)
        wide = mergedT[:, 6:8, 0:A_WIDTH]
        stage_gated_values(core, hT, w_in[:, :, A_WIDTH:2 * A_WIDTH], A["ln_rows"], wide, vv, eps)
        core.clear_semaphores()
        gate_tile = lambda b, j: w_in[:, :, bass.ds(j * P + 5888 + D * b, P)]
        w_gates = SplitTiles(core, stack, [(24, lambda n: gate_tile(0, 0))])
        stage_mix_chunks(core, vv, A["spatial_w"], A["spatial_b"], yaT, ahead=w_gates)

        projs = [lambda j, w=by_rows(n): w[:, :, bass.ds(j * P, P)] for n in ("proj_a", "proj_b", "proj_m")]
        gate0 = COL["gate_b"][0]
        stage_merge(core, hT, [(yaT, 6), (ybT, 2), (ymT, 4)], w_gates, gate_tile, projs,
                    lambda b, j: cols[:, bass.ds(j + gate0 + KT * b, 1)], mergedT)
        stack.close()
        stage_output(core, mergedT, by_rows("w_out"), lambda t: x_rows[t], None, x1)


def second_block(core, A, const, cols, x1, out):
    nc = core.nc
    ident, eps = const[:, 0:128], const[:, 384:385]
    col = lambda n: cols[:, COL[n][0]:COL[n][1]]
    by_rows = lambda name: A[name].rearrange("(k p) n -> p k n", p=P)
    N = SSM_GROUPS
    with ExitStack() as stack:
        gate = core.sb(stack, "x_gate", [P, D])
        yT = core.sb(stack, "yT", [P, KT, S])
        powers = core.sb(stack, "ssm_powers", [P, 2, LEVELS, N])
        d_cols = core.sb(stack, "ssm_d", [P, N])
        shift = core.sb(stack, "shift", [P, KT])
        gain = core.sb(stack, "gain", [P, KT])
        shapes = ((P, N, 2 * P), (P, N, P), (P, N, N))
        kept = [nc.dram_tensor(f"ssm_kept_{n}", s, F32, kind="Internal").ap() for n, s in enumerate(shapes)]
        with ExitStack() as m_stack:
            stage_modulation(core, A["c"], by_rows("ada_w"), col("ada_b"), A["ada_gate_b"],
                             col("norm_gain"), shift, gain, gate,
                             ssm_matrices_beside(core, m_stack, A["ssm_prm"], A["ssm_bc"], const, kept,
                                                 powers, d_cols))
        room_stack = stack.enter_context(ExitStack())
        room = core.sb(room_stack, "room", [P, 12, S])
        scratch_u = nc.dram_tensor("u_scratch", (N, N, 8, P), F32, kind="Internal").ap()
        scratch_y = nc.dram_tensor("y_scratch", (N, N, 8, P), F32, kind="Internal").ap()
        qT, kT = room[:, 0:4, :], room[:, 4:8, :]
        v = room[:, 8:12, :].rearrange("p a b -> p (a b)").rearrange("p (t d) -> p t d", t=TT)
        with ExitStack() as h_stack:
            h2T = core.sb(h_stack, "h2T", [P, 2, KT, S], F32R)
            w_in = by_rows("w_in_2")

            def columns(first):
                return lambda j: w_in[:, :, bass.ds(j * P + first, P)]

            wqT, wkT = room[:, 8:10, :], room[:, 10:11, :]
            wv = room[:, 11, :].rearrange("p (t d) -> p t d", t=TT)
            window_q = lambda j: [w_in[:, :, 2560 + P * n + 64 * j:][:, :, 0:64] for n in range(2)]
            groups = [
                Features(2, columns(0), ACT.Copy, lambda j: room[:, j, :].rearrange("p (t c) -> p c t", t=8),
                         view=lambda a: a.rearrange("p (c t) -> p c t", t=8),
                         save=[(scratch_u[8 * j:8 * j + 8].rearrange("g h t c -> (g h) (t c)"), room[:, j, :])
                               for j in range(2)]),
                Features(2, columns(256), ACT.Silu, lambda j: tile_of(yT, j)),
                Features(4, columns(2048), ACT.Silu, lambda j: tile_of(yT, j + 2)),
                Features(2, columns(3072), ACT.Silu, lambda j: tile_of(yT, j + 6)),
                Features(4, columns(512), ACT.Copy, lambda j: tile_of(qT, j), scale=64 ** -0.5, after_save=True),
                Features(4, columns(1024), ACT.Copy, lambda j: tile_of(kT, j)),
                Features(2, window_q, ACT.Copy, lambda j: tile_of(wqT, j),
                         scale=64 ** -0.5),
                Features(2, columns(2816), ACT.Copy, lambda j: room[:, 10 + j, :])]
            with ExitStack() as w_stack:
                w_2 = feature_weights(core, w_stack, groups, double=(18, 19))
                stage_norm_transpose(core, TT, x1, gain[:, :], shift[:, :], h2T, ident, eps, from_sbuf=True,
                                     ahead=w_2, room=room[:, 0:4, :])
                stage_features(core, h2T, groups, w_2)

            table = core.sb(h_stack, "window_table", [P, 4, 256])
            units = []
            for t in range(TT):
                width = 256 if t else P
                rows = [slice(64 * (n // 2), 64 * (n // 2) + 64) for n in range(4)]
                units.append(dict(
                    width=width, keep=None, sink=col("sinks"),
                    q=[wqT[rows[n], n % 2, t * P:(t + 1) * P] for n in range(4)],
                    k=[wkT[rows[n], 0, (t + 1) * P - width:(t + 1) * P] for n in range(4)],
                    bias=[table[:, n, 256 - width:256] for n in range(4)],
                    values=lambda n, b, t=t: wv[:, t - 1 + b if t else 0, 64 * (n // 2):64 * (n // 2) + 64],
                    out=lambda n, o: o[64 * (n % 2):64 * (n % 2) + 64, (n // 2) * P:(n // 2 + 1) * P],
                    store=(yT[:, 6:8, t * P:(t + 1) * P],
                           lambda b: b[:, 0:256].rearrange("p (h q) -> p h q", h=2))))
            core.clear_semaphores()
            stage_swa_inputs(core, A["far_window"], table, room[:, 11, :], ident)
            stage_attention(core, units, ident)

            for c in (0, 256):
                stage_rows(core, [(lambda part, k, t=t: h2T[:, part, k, t * P:(t + 1) * P], 0, 256, v[:, t, c:c + 256])
                                  for t in range(TT)], w_in[:, :, 1536 + c:1792 + c], 256)

        s_stack = room_stack.enter_context(ExitStack())
        G = core.sb(s_stack, "ssm_G", [P, N, 2 * P])
        M_out = core.sb(s_stack, "ssm_M", [P, N, P])
        c_stack = core.sb(s_stack, "ssm_C", [P, N, N])
        with ExitStack() as d_stack:
            neg_lam = core.sb(d_stack, "neg_lam", [P, 1])
            stage_diff_tables(core, A["lam"], neg_lam)
            o = core.sb(d_stack, "diff_o", [P, TT, 512])
            stage_diff_attention(core, qT, kT, v, A["far"], neg_lam[:, 0:1], ident, o,
                                 list(zip(kept, (G, M_out, c_stack))))
            stage_diff_norm(core, o, col("subln"), ident, eps, yT)

        core.clear_semaphores()
        Y = room[:, 0:2, :].rearrange("p a (g c) -> p (a g) c", c=P)
        L_room = room[:, 2:12, :].rearrange("p (k a) (g c) -> p k (a g) c", k=LEVELS - 2, c=P)
        stage_ssm_scan(core, L_room, scratch_u, const, ident, G, M_out, c_stack, powers, d_cols, Y)
        stage_ssm_output(core, Y, scratch_y, A["glu_w"].rearrange("(k p) n -> p k n", p=P),
                         col("glu_b"), yT)
        room_stack.close()
        stage_output(core, yT, by_rows("w_out_2"), None, gate[:, :], x1,
                     final=(A["final_gain"], eps, out.rearrange("b (t p) d -> (b t) p d", p=P)))


def layers(nc, A, out):
    with ExitStack() as stack:
        core = Core(nc, stack)
        const = core.sb(stack, "const", [P, CONST_COLS])
        cols = core.sb(stack, "cols", [P, COLS])
        x1 = core.sb(stack, "x1", [P, TT, D])
        stage_constants(core, A["const"], A["cols"], const, cols)
        first_block(core, A, const, cols, x1)
        core.clear_semaphores()
        second_block(core, A, const, cols, x1, out)


def pack_columns():
    sizes = [("norm_w", 8), ("mem_norm_w", 8), ("gate_b", 24), ("bqk", 12), ("mq", 4), ("mk", 4),
             ("norm_gain", 8), ("ada_b", 24), ("subln", 1), ("glu_b", 2), ("sinks", 4)]
    at, where = 0, {}
    for name, n in sizes:
        where[name] = (at, at + n)
        at += n
    return where, at


COL, COLS = pack_columns()
SEL, SWAP, SIGN = 512, 768, 385
CONST_COLS = 896


def bucket_rows():
    rows = np.zeros((33, 3, 384), np.float32)
    rows[32] = -1e30
    for g, dilation in enumerate((1, 4, 16)):
        for apart in range(129):
            if g == 2 and (apart % 2 or apart == 128):
                continue
            dist = (apart // 2 if g == 2 else apart) * dilation
            large = 16 + int(np.float32(np.log(np.float32(max(dist, 1)) / np.float32(16))
                                        / np.float32(math.log(2048 / 16))) * np.float32(16))
            rows[dist if dist < 16 else min(large, 31), g, 127 + apart] = 1.0
            rows[32, g, 127 + apart] = 0.0
    return rows


def distances(rows, width, at, limit):
    away = at + np.arange(rows)[:, None] - np.arange(width)[None, :]
    return np.where((away >= 0) & (away < limit), -away.astype(np.float32), np.float32(-1e30)).astype(np.float32)


def ssm_columns(I):
    twice = lambda v: np.concatenate([v, v])
    G = SSM_GROUPS
    return np.ascontiguousarray(np.stack([
        twice(I["ssm_lam_re_2"][0].T), twice(I["ssm_lam_im_2"][0].T),
        np.broadcast_to(I["ssm_log_step_2"][0][None], (P, G)),
        np.concatenate([I["ssm_d_2"][0].reshape(G, G).T] * 8)], axis=1))


def ssm_matrices(I):
    br, bi = (I[n][0].transpose(1, 0, 2) for n in ("ssm_b_re_2", "ssm_b_im_2"))
    cr, ci = (I[n][0].transpose(2, 0, 1) for n in ("ssm_c_re_2", "ssm_c_im_2"))
    stacks = [np.concatenate(pair) for pair in ((br, bi), (bi, br), (cr, ci), (ci, cr))]
    return np.ascontiguousarray(np.stack(stacks, axis=1))


def kernel(**inputs):
    import concourse.bacc as bacc
    from concourse.bass_utils import run_bass_kernel_spmd

    I = {k: np.asarray(v) for k, v in inputs.items()}
    const = np.zeros((P, CONST_COLS), np.float32)
    const[:, 0:128] = np.eye(P)
    const[:, 128:256] = np.kron(np.eye(2), np.ones((64, 64)))
    const[:, 256:384] = 1.0
    const[:, 384] = EPS
    for n, h in enumerate(HEAD_AT):
        at = SEL + P * (h // 2) + 64 * (h % 2)
        const[n, at:at + 64] = 1.0
    for p in range(P):
        const[p, SWAP + (p + 64) % P] = 1.0 if p < 64 else -1.0
    const[:, SIGN] = np.where(np.arange(P) < 64, -1.0, 1.0)

    def by_tile(v):
        return v.reshape(-1, P).T

    def over_partitions(v):
        return np.ascontiguousarray(np.broadcast_to(v[None], (P,) + v.shape))

    two = lambda v: np.concatenate([v, v])[:, None]
    parts = {
        "norm_w": by_tile(I["norm_w"]), "mem_norm_w": by_tile(I["mem_norm_w"]),
        "gate_b": by_tile(I["gate_b"]),
        "bqk": np.concatenate([two(I["b_q_norm_w"])] * 6 + [two(I["b_k_norm_w"])] * 6, 1),
        "mq": np.repeat(I["m_q_norm_w"][:, None], 4, 1), "mk": np.repeat(I["m_k_norm_w"][:, None], 4, 1),
        "norm_gain": by_tile(I["norm_gain_2"]), "ada_b": by_tile(I["ada_b_2"]),
        "subln": I["diff_subln_2"].reshape(P, 1), "glu_b": by_tile(I["glu_b_2"]),
        "sinks": over_partitions(I["swa_sinks_2"].reshape(4)),
    }
    arrays = {
        "const": const,
        "cols": np.ascontiguousarray(np.concatenate([parts[n] for n in COL], axis=1)),
        "x": I["x"], "w_in": I["w_in"], "mem": I["mem"], "m_w_kv": I["m_w_kv"],
        "proj_a": I["proj_a"], "proj_b": I["proj_b"], "proj_m": I["proj_m"], "w_out": I["w_out"],
        "c": by_tile(I["c_2"]), "ada_w": I["ada_w_2"][0], "ada_gate_b": over_partitions(I["ada_b_2"][0, 2 * D:]),
        "w_in_2": I["w_in_2"][0], "w_out_2": I["w_out_2"][0], "glu_w": I["glu_w_2"][0],
        "final_gain": over_partitions(I["final_gain_2"]),
        "lam": over_partitions(np.concatenate([I[n] for n in ("diff_lq1_2", "diff_lk1_2", "diff_lq2_2",
                                                              "diff_lk2_2")])),
        "ssm_prm": ssm_columns(I), "ssm_bc": ssm_matrices(I),
        "far": distances(P, D, 7 * P, D), "far_window": distances(P, 2 * P, P, P),
        "ln_rows": over_partitions(np.stack([I["a_v_norm_w"], I["a_v_norm_b"]])),
        "spatial_w": np.ascontiguousarray(I["a_spatial_w"].transpose(2, 0, 1)),
        "spatial_b": np.ascontiguousarray(np.repeat(I["a_spatial_b"], A_WIDTH // 4, axis=0)
                                          .reshape(6, P, P).transpose(1, 0, 2)), "onehot": bucket_rows(),
        "rel": np.concatenate([I["rel_bias"], np.ones((1, 12), np.float32)]),
    }
    nc = bacc.Bacc("TRN2", target_bir_lowering=False, num_devices=1)
    dram = {n: nc.dram_tensor(n, a.shape, mybir.dt.from_np(a.dtype), kind="ExternalInput").ap()
            for n, a in arrays.items()}
    out = nc.dram_tensor("out", (1, S, D), F32, kind="ExternalOutput").ap()
    layers(nc, dram, out)
    r = run_bass_kernel_spmd(nc, [arrays], core_ids=[0])
    return r.results[0]["out"]
```

```python
import math
from contextlib import ExitStack

import numpy as np

import concourse.bass as bass
from concourse import mybir

ALU = mybir.AluOpType
ACT = mybir.ActivationFunctionType
AX_X = mybir.AxisListType.X
F32 = mybir.dt.float32
I32 = mybir.dt.int32
F32R = mybir.dt.float32r

P = 128
D = 1024
S = 1024
KT = D // P
TT = S // P
HALF = 512
EPS = 1e-6
HEAD_AT = (0, 2, 1, 3)
MEM = 256
A_WIDTH = 768
M_WIDTH = 512
SSM_GROUPS = 16
LEVELS = 7
LAM_INIT = 0.8 - 0.6 * math.exp(0.0)


class Core:

    def __init__(self, nc, stack):
        self.nc, self.stack = nc, stack
        self.psum = stack.enter_context(nc.psum_tensor("psum", [P, 8, HALF], F32))
        self.names, self.sems = 0, []

    def sb(self, stack, name, shape, dt=F32):
        self.names += 1
        return stack.enter_context(self.nc.sbuf_tensor(f"{name}_{self.names}", shape, dt))

    def sem(self, name):
        self.names += 1
        self.sems.append(self.nc.alloc_semaphore(f"{name}_{self.names}"))
        return self.sems[-1]

    def clear_semaphores(self):
        self.nc.clear_and_free_semaphores(self.sems)
        self.nc.all_engine_barrier()
        self.sems = []


def bank(core, first, count=2):
    return core.psum[:, first:first + count, :].rearrange("p a b -> p (a b)")


HI, LO = 0, 1
PASSES = ((LO, HI), (HI, LO), (HI, HI))


def product(pe, out, lhs, rhs, tiles, depth=KT):
    for k in tiles:
        for n, (a, b) in enumerate(PASSES):
            last = pe.matmul(out, lhs(a, k), rhs(b, k), start=(k == 0 and n == 0),
                             stop=(k == depth - 1 and n == 2))
    return last


def walk(engine, n, body, base=0):
    assert base % 2 == 0 and (n % 2 == 0 or n == 1)
    pairs, start = (n + 1) // 2, base // 2
    for u in range(min(n, 2)):
        body(start, u, start == 0, pairs == 1)
    if pairs > 2:
        with engine.Fori(start + 1, start + pairs - 1) as i:
            for u in range(2):
                body(i, u, False, False)
    if pairs > 1:
        for u in range(2):
            body(start + pairs - 1, u, False, True)


class SplitTiles:

    def __init__(self, core, stack, tiles, double=()):
        self.tiles, self.double = tiles, double
        self.n = sum(n for n, _ in tiles)
        self.raw = core.sb(stack, "w_raw", [P, KT, P])
        self.parts = core.sb(stack, "w_parts", [P, 2, 2, KT, P], F32R)
        self.loaded = core.sem("w_loaded")
        self.high = core.sem("w_high")
        self.low = core.sem("w_low")
        self.ahead = False

    def load_tile(self, sp, view):
        if isinstance(view, list):
            for m, part in enumerate(view):
                sp.dma_start(self.raw[:, :, 64 * m:64 * m + 64], part).then_inc(self.loaded, 16)
        else:
            sp.dma_start(self.raw[:, :, :], view).then_inc(self.loaded, 16)

    def fetch(self, sp, group=0, between=lambda body: body):
        n, tile = self.tiles[group]
        base = sum(m for m, _ in self.tiles[:group])

        def one(i, u, first, last):
            if first and u == 0:
                if self.ahead:
                    return
            else:
                sp.wait_ge(self.low, 2 * i + u)
            self.load_tile(sp, tile(2 * i + (u - base)))

        walk(sp, n, between(one), base)

    def split_high(self, act, i, u):
        extra = 0
        if isinstance(i, int):
            extra = sum(1 for j in range(2 * i + u + 1) if j in self.double)
        act.wait_ge(self.loaded, 16 * (2 * i + (u + 1 + extra)))
        act.copy(self.parts[:, u, HI, :, :], self.raw[:, :, :]).then_inc(self.high, 1)

    def split_low(self, dve, i, u):
        dve.wait_ge(self.high, 2 * i + (u + 1))
        dve.tensor_tensor(self.parts[:, u, LO, :, :], self.raw[:, :, :],
                          self.parts[:, u, HI, :, :].bitcast(F32), ALU.subtract).then_inc(self.low, 1)

    def more(self, i, u, last):
        return not last or 2 * i + u + 2 < self.n

    def first_high(self, act):
        for u in range(1 if self.ahead else 0, min(self.n, 2)):
            self.split_high(act, 0, u)

    def first_low(self, dve):
        for u in range(1 if self.ahead else 0, min(self.n, 2)):
            self.split_low(dve, 0, u)

    def ahead_load(self, sp):
        self.ahead = True
        self.load_tile(sp, self.tiles[0][1](0))

    def ahead_high(self, act):
        self.split_high(act, 0, 0)

    def ahead_low(self, dve):
        self.split_low(dve, 0, 0)

    def ready(self, pe, i, u):
        pe.wait_ge(self.low, 2 * i + (u + 1))

    def lhs(self, u):
        return lambda part, k: self.parts[:, u, part, k, :]


class SplitMatrix:

    def __init__(self, core, stack, weights, ncols):
        self.weights, self.ncols = weights, ncols
        self.raw = core.sb(stack, "w_raw", [P, 2, ncols])
        self.parts = core.sb(stack, "w_parts", [P, 2, KT, ncols], F32R)
        self.loaded = [core.sem("w_loaded") for _ in range(2)]
        self.high = core.sem("w_high")
        self.low = core.sem("w_low")
        self.ahead = False

    def ahead_load(self, sp):
        self.fetch(sp)
        self.ahead = True

    def ahead_high(self, act):
        self.split_high(act, True)

    def ahead_low(self, dve):
        self.split_low(dve, True)

    def fetch(self, sp):
        if self.ahead:
            return
        for k in range(KT):
            if k >= 2:
                sp.wait_ge(self.low, k - 1)
            sp.dma_start(self.raw[:, k % 2, :], self.weights[:, k, :]).then_inc(self.loaded[k % 2], 16)

    def split_high(self, act, ahead=False):
        if self.ahead and not ahead:
            return
        for k in range(KT):
            act.wait_ge(self.loaded[k % 2], 16 * (k // 2 + 1))
            act.copy(self.parts[:, HI, k, :], self.raw[:, k % 2, :]).then_inc(self.high, 1)

    def split_low(self, dve, ahead=False):
        if self.ahead and not ahead:
            return
        for k in range(KT):
            dve.wait_ge(self.high, k + 1)
            dve.tensor_tensor(self.parts[:, LO, k, :], self.raw[:, k % 2, :],
                              self.parts[:, HI, k, :].bitcast(F32), ALU.subtract).then_inc(self.low, 1)

    def products(self, pe, first, *units):
        for k in range(KT):
            if first:
                pe.wait_ge(self.low, k + 1)
            for outs, lhs, c0s, width in units:
                for out, c0 in zip(outs, c0s):
                    last = product(pe, out, lhs, lambda part, j: self.parts[:, part, j, c0:c0 + width], [k])
        return last


def tile_of(ap, j):
    return ap[:, bass.ds(j, 1), :].rearrange("p j t -> p (j t)")


def stage_constants(core, const_dram, cols_dram, const, cols):
    nc = core.nc
    loaded = core.sem("const_loaded")
    with nc.Block(no_gpsimd_drain=True) as block:

        @block.sync
        def _(sp):
            sp.dma_start(const[:, :], const_dram).then_inc(loaded, 16)
            sp.dma_start(cols[:, :], cols_dram).then_inc(loaded, 16)
            sp.wait_ge(loaded, 32)

        @block.vector
        def _(dve):
            dve.wait_ge(loaded, 32)
            for name, factor in (("bqk", 64 ** -0.5), ("mq", 128 ** -0.5)):
                a, b = COL[name][0], COL[name][0] + (6 if name == "bqk" else 4)
                dve.tensor_scalar(cols[:, a:b], cols[:, a:b], factor, None, ALU.mult)


def stage_norm_transpose(core, tiles, src, gain, shift, dst, ident, eps, from_sbuf=False, ahead=None, room=None):
    nc = core.nc
    with ExitStack() as stack:
        xin = None if from_sbuf else core.sb(stack, "xin", [P, 2, D])
        sq = bank(core, 4)
        if room is None:
            room = core.sb(stack, "xn", [P, 4, D])
        xn = room[:, 0:2, :]
        whole = room[:, 2:4, :].rearrange("p s (k t) -> p s k t", k=KT)
        ssq = core.sb(stack, "ssq", [P, tiles])
        std = core.sb(stack, "std", [P, tiles])
        rstd = core.sb(stack, "rstd", [P, tiles])
        x_loaded = [core.sem("x_loaded") for _ in range(2)]
        summed = core.sem("norm_summed")
        rooted = core.sem("norm_rooted")
        inverted = core.sem("norm_inverted")
        scaled = core.sem("norm_scaled")
        turned = core.sem("norm_turned")
        moved = core.sem("norm_moved")
        shifted = core.sem("norm_shifted")
        high = core.sem("norm_high")
        low = core.sem("norm_low")
        rows = [(src[:, t, :] if from_sbuf else xin[:, t % 2, :]) for t in range(tiles)]

        with nc.Block(no_gpsimd_drain=True) as block:

            @block.sync
            def _(sp):
                if from_sbuf:
                    if ahead:
                        ahead.ahead_load(sp)
                    return
                for t in range(tiles):
                    if t >= 2:
                        sp.wait_ge(scaled, t - 1)
                        sp.wait_ge(summed, t - 1)
                    sp.dma_start(rows[t], src[t]).then_inc(x_loaded[t % 2], 16)
                    if ahead and t == 1:
                        ahead.ahead_load(sp)

            def split(act, t):
                act.wait_ge(moved if shift is None else shifted, t + 1)
                act.copy(dst[:, HI, :, t * P:(t + 1) * P], whole[:, t % 2, :, :]).then_inc(high, 1)

            @block.scalar
            def _(act):
                for t in range(tiles):
                    if not from_sbuf:
                        act.wait_ge(x_loaded[t % 2], 16 * (t // 2 + 1))
                    if t >= 1:
                        act.wait_ge(summed, t)
                    act.activation(sq, rows[t], ACT.Square,
                                   accum_out=ssq[:, t:t + 1]).then_inc(summed, 1)
                    act.wait_ge(summed, t + 1)
                    act.activation(std[:, t:t + 1], ssq[:, t:t + 1], ACT.Sqrt,
                                   bias=eps[:, 0:1], scale=1.0 / D).then_inc(rooted, 1)
                    if t >= 2:
                        split(act, t - 2)
                    if ahead and t == min(3, tiles - 1):
                        ahead.ahead_high(act)
                split(act, tiles - 2)
                split(act, tiles - 1)

            @block.gpsimd
            def _(pool):
                for t in range(tiles):
                    pool.wait_ge(high, t + 1)
                    pool.tensor_tensor(dst[:, LO, :, t * P:(t + 1) * P], whole[:, t % 2, :, :],
                                       dst[:, HI, :, t * P:(t + 1) * P].bitcast(F32), ALU.subtract).then_inc(low, 1)

            def move(dve, t):
                dve.wait_ge(turned, t + 1)
                part = whole[:, t % 2, :, :]
                if t >= 2:
                    dve.wait_ge(high, t - 1)
                    dve.wait_ge(low, t - 1)
                dve.tensor_tensor(part, bank(core, 2 * (t % 2)).rearrange("p (k s) -> p k s", k=KT),
                                  gain.unsqueeze(2).to_broadcast([P, KT, P]), ALU.mult).then_inc(moved, 1)
                if shift is not None:
                    dve.wait_ge(moved, t + 1)
                    dve.tensor_tensor(part, part, shift.unsqueeze(2).to_broadcast([P, KT, P]),
                                      ALU.add).then_inc(shifted, 1)

            @block.vector
            def _(dve):
                for t in range(tiles):
                    dve.wait_ge(rooted, t + 1)
                    dve.reciprocal(rstd[:, t:t + 1], std[:, t:t + 1]).then_inc(inverted, 1)
                    dve.wait_ge(inverted, t + 1)
                    if t >= 2:
                        dve.wait_ge(turned, t - 1)
                    dve.tensor_scalar(xn[:, t % 2, :], rows[t], rstd[:, t:t + 1], None,
                                      ALU.mult).then_inc(scaled, 1)
                    if t >= 1:
                        move(dve, t - 1)
                    if ahead and t == min(4, tiles - 1):
                        ahead.ahead_low(dve)
                move(dve, tiles - 1)
                dve.wait_ge(low, tiles)

            @block.tensor
            def _(pe):
                for t in range(tiles):
                    pe.wait_ge(scaled, t + 1)
                    if t >= 2:
                        pe.wait_ge(moved, t - 1)
                    for k in range(KT):
                        last = pe.transpose(bank(core, 2 * (t % 2))[:, k * P:(k + 1) * P],
                                            xn[:, t % 2, k * P:(k + 1) * P], ident)
                    last.then_inc(turned, 1)


def stage_heads(core, n, src, tokens, w, same, scale, norm_col, dst, eps, room=None):
    nc = core.nc
    width = min(tokens, HALF)
    halves = [slice(h * width, (h + 1) * width) for h in range(tokens // width)]
    early = 1
    with ExitStack() as stack:
        if not isinstance(w, SplitTiles):
            w = SplitTiles(core, stack, [(n, w)])
        if room is None:
            room = core.sb(stack, "squares_roots", [P, 2, tokens])
        sq, rs = room[:, 0, :], room[:, 1, :]
        projected = core.sem("projected")
        squared = core.sem("squared")
        summed = core.sem("summed")
        rooted = core.sem("rooted")
        inverted = core.sem("inverted")
        normed = core.sem("normed")

        def dense(u):
            return bank(core, 2 * u)[:, 0:tokens]

        sums = bank(core, 4)[:, 0:tokens]

        with nc.Block(no_gpsimd_drain=True) as block:

            @block.sync
            def _(sp):
                w.fetch(sp)

            @block.tensor
            def _(pe):
                def sum_squares(i, u, second):
                    pe.wait_ge(squared, 2 * i + u)
                    if not second:
                        pe.wait_ge(rooted, 2 * i + (u - 1))
                    for h in halves:
                        last = pe.matmul(sums[:, h], same, sq[:, h], start=True, stop=True)
                    last.then_inc(summed, 1)

                def tile(i, u, first, last):
                    w.ready(pe, i, u)
                    if not first:
                        pe.wait_ge(normed, 2 * i + (u - 1))
                    for m, h in enumerate(halves):
                        for tiles in (range(early), range(early, KT)):
                            done = product(pe, dense(u)[:, h], w.lhs(u), lambda part, k: src[:, part, k, h], tiles)
                            if m == 0 and tiles[0] == 0 and not (first and u == 0):
                                sum_squares(i, u, first)
                    done.then_inc(projected, 1)

                walk(pe, n, tile)
                sum_squares(n // 2, 0, False)

            @block.scalar
            def _(act):
                def tile(i, u, first, last):
                    act.wait_ge(projected, 2 * i + (u + 1))
                    if not (first and u == 0):
                        act.wait_ge(summed, 2 * i + u)
                    act.activation(sq[:, :], dense(u), ACT.Square).then_inc(squared, 1)
                    if not last:
                        w.split_high(act, i + 1, u)
                    act.wait_ge(summed, 2 * i + (u + 1))
                    if not (first and u == 0):
                        act.wait_ge(normed, 2 * i + u)
                    act.activation(rs[:, :], sums, ACT.Sqrt, bias=eps[:, 0:1],
                                   scale=scale).then_inc(rooted, 1)

                w.first_high(act)
                walk(act, n, tile)

            @block.vector
            def _(dve):
                def tile(i, u, first, last):
                    if not last:
                        w.split_low(dve, i + 1, u)
                    dve.wait_ge(rooted, 2 * i + (u + 1))
                    dve.reciprocal(rs[:, :], rs[:, :]).then_inc(inverted, 1)
                    dve.wait_ge(inverted, 2 * i + (u + 1))
                    dve.scalar_tensor_tensor(out=tile_of(dst, 2 * i + u),
                                             in0=dense(u), scalar=norm_col(2 * i + u),
                                             in1=rs[:, :], op0=ALU.mult, op1=ALU.mult).then_inc(normed, 1)

                w.first_low(dve)
                walk(dve, n, tile)


def stage_rows(core, src_units, weights, ncols, sync=None):
    nc = core.nc
    with ExitStack() as stack:
        w = weights if isinstance(weights, SplitMatrix) else SplitMatrix(core, stack, weights, ncols)
        made = core.sem("rows_made")
        kept = [core.sem("rows_kept_dve"), core.sem("rows_kept_act")]

        with nc.Block(no_gpsimd_drain=True) as block:

            @block.sync
            def _(sp):
                w.fetch(sp)
                if sync:
                    sync(sp)

            @block.tensor
            def _(pe):
                units = [([bank(core, n % 4, 1)[:, 0:width]], lhs, [c0], width)
                         for n, (lhs, c0, width, _) in enumerate(src_units)]
                w.products(pe, True, *units[:4]).then_inc(made, len(units[:4]))
                for n, unit in enumerate(units[4:], 4):
                    pe.wait_ge(kept[n % 2], n // 2 - 1)
                    w.products(pe, False, unit).then_inc(made, 1)

            @block.vector
            def _(dve):
                w.split_low(dve)
                for n, (_, _, width, dst) in enumerate(src_units):
                    if n % 2 == 0:
                        dve.wait_ge(made, n + 1)
                        dve.tensor_copy(dst, bank(core, n % 4, 1)[:, 0:width]).then_inc(kept[0], 1)

            @block.scalar
            def _(act):
                w.split_high(act)
                for n, (_, _, width, dst) in enumerate(src_units):
                    if n % 2 == 1:
                        act.wait_ge(made, n + 1)
                        act.copy(dst, bank(core, n % 4, 1)[:, 0:width]).then_inc(kept[1], 1)


class Features:

    def __init__(self, n, weights, func, dst, scale=1.0, times=None, view=None, save=(), after_save=False):
        self.n, self.weights, self.func, self.dst, self.scale = n, weights, func, dst, scale
        self.times, self.view, self.written, self.after_save = times, view or (lambda a: a), save, after_save


def feature_weights(core, stack, groups, double=()):
    return SplitTiles(core, stack, [(g.n, g.weights) for g in groups], double)


class Beside:

    def sync(self, sp, t):
        pass

    def sync_end(self, sp):
        pass

    def tensor(self, pe, t):
        pass

    def scalar(self, act, t):
        pass

    def vector(self, dve, t):
        pass

    def vector_end(self, dve):
        pass

    def gpsimd(self, pool):
        pass


def stage_features(core, src, groups, w=None, ahead=None, beside=()):
    nc = core.nc
    base = [sum(g.n for g in groups[:m]) for m in range(len(groups) + 1)]
    gates = [m for m, g in enumerate(groups) if g.times]
    with ExitStack() as stack:
        w = w or feature_weights(core, stack, groups)
        assert not gates or gates == [len(groups) - 1]
        projected = core.sem("projected")
        mapped = core.sem("mapped")
        gated = core.sem("gated")
        saved = core.sem("features_saved")
        saves = sum(len(g.written) for g in groups)

        def between(method, engine, body, after=False):
            def tile(i, u, first, last):
                if after:
                    body(i, u, first, last)
                if isinstance(i, int):
                    for work in beside:
                        method(work, engine, 2 * i + u)
                if not after:
                    body(i, u, first, last)

            return tile

        with nc.Block(no_gpsimd_drain=True) as block:

            @block.sync
            def _(sp):
                def save(m):
                    if groups[m].written:
                        sp.wait_ge(mapped, base[m + 1])
                    for there, made in groups[m].written:
                        sp.dma_start(there, made).then_inc(saved, 16)

                for m in range(len(groups)):
                    w.fetch(sp, m, lambda body: between(lambda work, *at: work.sync(*at), sp, body, after=True))
                    if m:
                        save(m - 1)
                save(len(groups) - 1)
                if ahead:
                    ahead.ahead_load(sp)
                for work in beside:
                    work.sync_end(sp)
                if saves:
                    sp.wait_ge(saved, 16 * saves)

            @block.tensor
            def _(pe):
                def project(i, u, first, last):
                    w.ready(pe, i, u)
                    start = base[m] // 2
                    if g.times and not (isinstance(i, int) and i == start):
                        pe.wait_ge(gated, 2 * i + (u - base[m] - 1))
                    elif not first:
                        pe.wait_ge(mapped, 2 * i + (u - 1))
                    for h in range(2):
                        done = product(pe, bank(core, 2 * u + h, 1), w.lhs(u),
                                       lambda part, k: src[:, part, k, h * HALF:(h + 1) * HALF], range(KT))
                    done.then_inc(projected, 1)

                for m, g in enumerate(groups):
                    walk(pe, g.n, between(lambda work, *at: work.tensor(*at), pe, project), base[m])

            @block.scalar
            def _(act):
                w.first_high(act)
                if ahead:
                    ahead.ahead_high(act)
                for m, g in enumerate(groups):
                    if g.after_save:
                        act.wait_ge(saved, 16 * saves)

                    def apply(i, u, first, last):
                        act.wait_ge(projected, 2 * i + (u + 1))
                        if w.more(i, u, last):
                            w.split_high(act, i + 1, u)
                        banks = bank(core, 2 * u)
                        act.activation(banks if g.times else g.dst(2 * i + (u - base[m])),
                                       g.view(banks), g.func, scale=g.scale).then_inc(mapped, 1)

                    walk(act, g.n, between(lambda work, *at: work.scalar(*at), act, apply), base[m])

            @block.vector
            def _(dve):
                w.first_low(dve)
                if ahead:
                    ahead.ahead_low(dve)
                for m, g in enumerate(groups):

                    def gate(i, u, first, last):
                        if w.more(i, u, last):
                            w.split_low(dve, i + 1, u)
                        if g.times:
                            j = 2 * i + (u - base[m])
                            dve.wait_ge(mapped, 2 * i + (u + 1))
                            dve.tensor_tensor(g.dst(j), g.times(j), bank(core, 2 * u), ALU.mult).then_inc(gated, 1)

                    walk(dve, g.n, between(lambda work, *at: work.vector(*at), dve, gate), base[m])
                for work in beside:
                    work.vector_end(dve)

            if beside:
                @block.gpsimd
                def _(pool):
                    for work in beside:
                        work.gpsimd(pool)


class BiasRows(Beside):

    def __init__(self, core, rel, onehot_dram, scratch, back, room):
        self.core, self.rel, self.onehot_dram, self.scratch, self.back = core, rel, onehot_dram, scratch, back
        self.hot = room[0:33, 0:3, 0:384]
        self.rb = room[0:33, 3, 0:12]
        self.rows = room[0:4, 6:8, :].rearrange("p a b -> p (a b)")[:, 0:1152].rearrange("p (g x) -> p g x", g=3)
        self.loaded, self.made, self.copied, self.saved, self.spread = (
            core.sem("bias_" + n) for n in ("loaded", "made", "copied", "saved", "spread"))

    def sync(self, sp, t):
        if t == 0:
            sp.dma_start(self.hot, self.onehot_dram).then_inc(self.loaded, 16)
            sp.dma_start(self.rb, self.rel).then_inc(self.loaded, 16)

    def spread_rows(self, sp):
        sp.wait_ge(self.copied, 3)
        sp.dma_start(self.scratch.rearrange("g h x -> h g x"), self.rows).then_inc(self.saved, 16)
        sp.wait_ge(self.saved, 16)
        for g in range(3):
            width = 256 if g < 2 else P
            src = bass.AP(self.scratch.tensor, g * 4 * 384, [[1, P], [384, 4], [1, width]])
            sp.dma_start(self.back[:, 4 * g:4 * g + 4, 0:width], src).then_inc(self.spread, 16)
        sp.wait_ge(self.spread, 48)

    def tensor(self, pe, t):
        if t == 1:
            pe.wait_ge(self.loaded, 32)
            for g in range(3):
                pe.matmul(bank(self.core, 4 + g, 1)[0:4, 0:384], self.rb[:, 4 * g:4 * g + 4], self.hot[:, g, :],
                          start=True, stop=True).then_inc(self.made, 1)

    def vector(self, dve, t):
        if t == 1:
            for g in range(3):
                dve.wait_ge(self.made, g + 1)
                dve.tensor_copy(self.rows[:, g, :], bank(self.core, 4 + g, 1)[0:4, 0:384]).then_inc(self.copied, 1)


def stage_bias_tables(core, back, table, table16):
    with core.nc.Block(no_gpsimd_drain=True) as block:

        @block.vector
        def _(dve):
            dve.tensor_copy(table, back[:, 0:8, ::-1])

        @block.scalar
        def _(act):
            act.copy(table16, back[:, 8:12, 127::-1])


def stage_attention(core, units, ident, width_max=256):
    nc = core.nc
    n = len(units)
    with ExitStack() as stack:
        p = core.sb(stack, "p", [P, 2, 4, 256])
        pT = core.sb(stack, "pT", [P, 2, 1024])
        top = core.sb(stack, "top", [P, 2, 4])
        low = core.sb(stack, "low", [P, 2, 4])
        total = core.sb(stack, "total", [P, 2, 4])
        inv = core.sb(stack, "inv", [P, 2, 4])
        extra = core.sb(stack, "extra", [P, 2, 4])
        scored = core.sem("scored")
        maxed = core.sem("maxed")
        small = core.sem("small_steps")
        exped = core.sem("exped")
        weighted = core.sem("weighted")
        turned = core.sem("turned")
        moved_act = core.sem("moved_act")
        moved_dve = core.sem("moved_dve")
        mixed = core.sem("mixed")
        stored = core.sem("stored")
        sinked = core.sem("sinked")
        steps = [0]

        def S_(u):
            return bank(core, 2 * (u % 2)).rearrange("p (h w) -> p h w", h=4)

        def T_():
            return bank(core, 4)

        def O_(u):
            return bank(core, 6 + u % 2, 1)

        with nc.Block(no_gpsimd_drain=True) as block:

            @block.tensor
            def _(pe):
                def scores(u):
                    d = units[u]
                    if u >= 2:
                        pe.wait_ge(maxed, u - 1)
                        pe.wait_ge(exped, u - 1)
                    for h in range(4):
                        last = pe.matmul(S_(u)[:, h, 0:d["width"]], d["q"][h], d["k"][h],
                                         start=True, stop=True)
                    last.then_inc(scored, 1)

                def turn(u):
                    d = units[u]
                    blocks = d["width"] // P
                    pe.wait_ge(weighted, u + 1) if d["keep"] is None else pe.wait_ge(exped, u + 1)
                    if u >= 1:
                        pe.wait_ge(moved_act, u)
                        pe.wait_ge(moved_dve, u)
                    for h in range(4):
                        for b in range(blocks):
                            last = pe.transpose(T_()[:, (2 * h + b) * P:(2 * h + b + 1) * P],
                                                p[:, u % 2, h, b * P:(b + 1) * P], ident)
                    last.then_inc(turned, 1)

                def mix(u):
                    d = units[u]
                    blocks = d["width"] // P
                    pe.wait_ge(moved_act, u + 1)
                    pe.wait_ge(moved_dve, u + 1)
                    if u >= 2:
                        pe.wait_ge(stored, u - 1)
                    for h in range(4):
                        for b in range(blocks):
                            last = pe.matmul(d["out"](h, O_(u)), d["values"](h, b),
                                             pT[:, u % 2, (2 * h + b) * P:(2 * h + b + 1) * P],
                                             start=(b == 0), stop=(b == blocks - 1))
                    last.then_inc(mixed, 1)

                for u in range(n + 2):
                    if u < n:
                        scores(u)
                    if 1 <= u <= n:
                        turn(u - 1)
                    if u >= 2:
                        mix(u - 2)

            @block.vector
            def _(dve):
                def step(ins):
                    steps[0] += 1
                    ins.then_inc(small, 1)
                    dve.wait_ge(small, steps[0])

                def maxima(u):
                    d = units[u]
                    s = u % 2
                    m = d["keep"][0] if d["keep"] else top[:, s, :]
                    dve.wait_ge(scored, u + 1)
                    if u >= 2:
                        dve.wait_ge(turned, u - 1)
                    if d["bias"] is None:
                        step(dve.tensor_reduce(m, S_(u)[:, :, 0:d["width"]], AX_X, ALU.max))
                    else:
                        for h in range(4):
                            last = dve.tensor_tensor_reduce(
                                p[:, s, h, 0:d["width"]], S_(u)[:, h, 0:d["width"]], d["bias"][h],
                                1.0, -3e38, ALU.add, ALU.max, m[:, h:h + 1])
                        step(last)
                    if d["sink"] is not None:
                        step(dve.tensor_tensor(m, m, d["sink"], ALU.max))
                        step(dve.tensor_tensor(extra[:, s, :], d["sink"], m, ALU.subtract))
                    dve.tensor_scalar(low[:, s, :], m, -1.0, None, ALU.mult).then_inc(maxed, 1)

                def weights(u):
                    d = units[u]
                    s = u % 2
                    if d["keep"]:
                        return
                    dve.wait_ge(exped, u + 1)
                    if d["sink"] is not None:
                        step(dve.tensor_tensor(total[:, s, :], total[:, s, :], extra[:, s, :], ALU.add))
                    step(dve.reciprocal(inv[:, s, :], total[:, s, :]))
                    for h in range(4):
                        w = p[:, s, h, 0:d["width"]]
                        last = dve.tensor_scalar(w, w, inv[:, s, h:h + 1], None, ALU.mult)
                    last.then_inc(weighted, 1)

                def move(u):
                    d = units[u]
                    dve.wait_ge(turned, u + 1)
                    if u >= 2:
                        dve.wait_ge(mixed, u - 1)
                    view = lambda a: a[:, 512:1024].rearrange("p (h w) -> p h w", h=2)[:, :, 0:d["width"]]
                    dve.tensor_copy(view(pT[:, u % 2, :]), view(T_())).then_inc(moved_dve, 1)

                def store(u):
                    dve.wait_ge(mixed, u + 1)
                    dst, view = units[u]["store"]
                    if units[u]["keep"]:
                        dve.tensor_copy(dst, view(O_(u))).then_inc(stored, 1)
                    else:
                        dve.tensor_tensor(dst, view(O_(u)), dst, ALU.mult).then_inc(stored, 1)

                for u in range(n + 3):
                    if 2 <= u < n + 2:
                        move(u - 2)
                    if 1 <= u <= n:
                        weights(u - 1)
                    if u < n:
                        maxima(u)
                    if u >= 3:
                        store(u - 3)

            @block.scalar
            def _(act):
                def move(u):
                    d = units[u]
                    act.wait_ge(turned, u + 1)
                    if u >= 2:
                        act.wait_ge(mixed, u - 1)
                    view = lambda a: a[:, 0:512].rearrange("p (h w) -> p h w", h=2)[:, :, 0:d["width"]]
                    act.copy(view(pT[:, u % 2, :]), view(T_())).then_inc(moved_act, 1)

                def exps(u):
                    d = units[u]
                    s = u % 2
                    sums = d["keep"][1] if d["keep"] else total[:, s, :]
                    act.wait_ge(maxed, u + 1)
                    if u >= 2 and not d["keep"]:
                        act.wait_ge(weighted, u - 1)
                    if d["sink"] is not None:
                        act.activation(extra[:, s, :], extra[:, s, :], ACT.Exp)
                    for h in range(4):
                        into = p[:, s, h, 0:d["width"]]
                        src = S_(u)[:, h, 0:d["width"]] if d["bias"] is None else into
                        last = act.activation(into, src, ACT.Exp, bias=low[:, s, h:h + 1],
                                              accum_out=sums[:, h:h + 1])
                    last.then_inc(exped, 1)

                for u in range(n + 2):
                    if u >= 2:
                        move(u - 2)
                    if u < n:
                        exps(u)


def in_order(ap, g, t):
    if g == 0:
        return ap[:, t * P:(t + 1) * P]
    if g == 1:
        return ap.rearrange("p (l r) -> p r l", r=4)[:, t // 2, (t % 2) * P:(t % 2 + 1) * P]
    return ap.rearrange("p (l r) -> p r l", r=8)[:, t, :]


def window_units(qkT, v, oT, table, table16, maxima, sums):
    units = []
    for g in range(3):
        for t in range(TT):
            before = (g == 0 and t > 0) or (g == 1 and t % 2 == 1)
            width = 256 if before else 128
            q, k, bias = [], [], []
            for h in HEAD_AT:
                rows = slice(64 * (h % 2), 64 * (h % 2) + 64)
                q.append(in_order(qkT[rows, 2 * g + h // 2, :], g, t))
                kk = qkT[rows, 6 + 2 * g + h // 2, :]
                if not before:
                    k.append(in_order(kk, g, t))
                elif g == 0:
                    k.append(kk[:, (t - 1) * P:(t + 1) * P])
                else:
                    k.append(kk.rearrange("p (l r) -> p r l", r=4)[:, t // 2, :])
                bias.append(table16[:, h, :] if g == 2 else table[:, 4 * g + h, 256 - width:256])
            at = 4 * (g * TT + t)

            def values(n, b, g=g, t=t, before=before):
                h = HEAD_AT[n]
                return v[:, t - 1 + b if before else t, g, 64 * h:64 * h + 64]

            def out(n, o):
                h = HEAD_AT[n]
                return o[64 * (h % 2):64 * (h % 2) + 64, (h // 2) * P:(h // 2 + 1) * P]

            o = oT[:, g, :, :]
            if g == 0:
                dst = o[:, :, t * P:(t + 1) * P]
                view = lambda b: b[:, 0:256].rearrange("p (h q) -> p h q", h=2)
            elif g == 1:
                dst = o.rearrange("p h (l r) -> p h r l", r=4)[:, :, t // 2, (t % 2) * P:(t % 2 + 1) * P]
                view = lambda b: b[:, 0:256].rearrange("p (h q) -> p h q", h=2)
            else:
                dst = o.rearrange("p h (l r) -> p h r l", r=8)[:, :, t, :]
                view = lambda b: b[:, 0:256].rearrange("p (h q) -> p h q", h=2)
            units.append(dict(width=width, q=q, k=k, bias=bias, sink=None, values=values, out=out,
                              store=(dst, view), keep=(maxima[:, at:at + 4], sums[:, at:at + 4])))
    return units


def stage_combine(core, maxima, sums, oT, ybT, ident, sel):
    nc = core.nc
    with ExitStack() as stack:
        rows = core.sb(stack, "lse_rows", [4, 2, 3, S])
        top = core.sb(stack, "lse_top", [4, S])
        prod = core.sb(stack, "prod", [P, S])
        acc = core.sb(stack, "weighed_sum", [P, S])
        turned = core.sem("lse_turned")
        moved = core.sem("lse_moved")
        chain = core.sem("lse_chain")
        topped = core.sem("lse_topped")
        exped = core.sem("lse_exped")
        ready = core.sem("lse_ready")
        spread = core.sem("lse_spread")
        used = core.sem("lse_used")
        m = rows[:, 0, :, :]
        l = rows[:, 1, :, :]
        with nc.Block(no_gpsimd_drain=True) as block:

            @block.tensor
            def _(pe):
                for n in range(6):
                    w, g = n // 3, n % 3
                    if n >= 2:
                        pe.wait_ge(moved, n - 1)
                    for t in range(TT):
                        src = (maxima, sums)[w][:, 4 * (g * TT + t):4 * (g * TT + t) + 4]
                        last = pe.transpose(bank(core, 2 * (n % 2))[0:4, t * P:(t + 1) * P], src, ident)
                    last.then_inc(turned, 1)
                pe.wait_ge(ready, 1)
                for n in range(6):
                    pair, g = n // 3, n % 3
                    if n >= 2:
                        pe.wait_ge(used, n - 1)
                    for h in range(2):
                        last = pe.matmul(bank(core, 4 + 2 * (n % 2) + h, 1), sel[0:4, pair * P:(pair + 1) * P],
                                         m[:, g, h * HALF:(h + 1) * HALF], start=True, stop=True)
                    last.then_inc(spread, 1)

            @block.vector
            def _(dve):
                done = [0]

                def step(ins):
                    done[0] += 1
                    ins.then_inc(chain, 1)
                    dve.wait_ge(chain, done[0])

                for n in range(6):
                    w, g = n // 3, n % 3
                    dve.wait_ge(turned, n + 1)
                    r = (1, 4, 8)[g]
                    dst = rows[:, w, g, :].rearrange("p (l r) -> p r l", r=r)
                    dve.tensor_copy(dst, bank(core, 2 * (n % 2))[0:4, :].rearrange("p (r l) -> p r l", r=r))\
                       .then_inc(moved, 1)
                dve.wait_ge(moved, 6)
                step(dve.tensor_tensor(top[:, :], m[:, 0, :], m[:, 1, :], ALU.max))
                step(dve.tensor_tensor(top[:, :], top[:, :], m[:, 2, :], ALU.max))
                for g in range(3):
                    last = dve.tensor_tensor(m[:, g, :], m[:, g, :], top[:, :], ALU.subtract)
                last.then_inc(topped, 1)
                dve.wait_ge(exped, 1)
                step(dve.tensor_tensor(l, l, m, ALU.mult))
                step(dve.tensor_tensor(top[:, :], l[:, 0, :], l[:, 1, :], ALU.add))
                step(dve.tensor_tensor(top[:, :], top[:, :], l[:, 2, :], ALU.add))
                step(dve.reciprocal(top[:, :], top[:, :]))
                for g in range(3):
                    last = dve.tensor_tensor(m[:, g, :], m[:, g, :], top[:, :], ALU.mult)
                last.then_inc(ready, 1)
                for n in range(6):
                    pair, g = n // 3, n % 3
                    dve.wait_ge(spread, n + 1)
                    y = acc[:, :]
                    dst = y if g == 0 else prod[:, :]
                    dve.tensor_tensor(dst, bank(core, 4 + 2 * (n % 2)), oT[:, g, pair, :],
                                      ALU.mult).then_inc(used, 1)
                    if g > 0:
                        dve.wait_ge(used, n + 1)
                        step(dve.tensor_tensor(y, y, prod[:, :], ALU.add))
                    if g == 2:
                        step(dve.tensor_tensor(ybT[:, pair, :], ybT[:, pair, :], y, ALU.mult))

            @block.scalar
            def _(act):
                act.wait_ge(topped, 1)
                act.activation(m, m, ACT.Exp).then_inc(exped, 1)


def stage_gated_values(core, src, weights, wide_dram, wide, vv, eps):
    nc = core.nc
    width = A_WIDTH // 2
    with ExitStack() as stack:
        w = SplitMatrix(core, stack, weights, A_WIDTH)
        act_v = w.raw
        sq = bank(core, 4)[:, 0:A_WIDTH]
        part = core.sb(stack, "ln_part", [P, 2, 2])
        mean = core.sb(stack, "ln_mean", [P, 2])
        ssq = core.sb(stack, "ln_ssq", [P, 2])
        rstd = core.sb(stack, "ln_rstd", [P, 2])
        wide_loaded = core.sem("ln_rows_loaded")
        made = core.sem("values_made")
        mapped = core.sem("values_mapped")
        squared = core.sem("values_squared")
        rooted = core.sem("values_rooted")
        done = core.sem("values_done")
        chain = core.sem("values_chain")

        with nc.Block(no_gpsimd_drain=True) as block:

            @block.sync
            def _(sp):
                sp.dma_start(wide[:, :, :], wide_dram).then_inc(wide_loaded, 16)
                w.fetch(sp)

            @block.tensor
            def _(pe):
                units = [([bank(core, 2 * (t % 2) + h, 1)[:, 0:width] for h in range(2)],
                          lambda part, k, t=t: src[:, part, k, t * P:(t + 1) * P], [0, width], width)
                         for t in range(TT)]
                w.products(pe, True, *units[:2]).then_inc(made, 2)
                for t in range(2, TT):
                    pe.wait_ge(mapped, t - 1)
                    w.products(pe, False, units[t]).then_inc(made, 1)

            @block.scalar
            def _(act):
                def gelu(t):
                    act.wait_ge(made, t + 1)
                    if t >= 2:
                        act.wait_ge(done, t - 1)
                    for h in range(2):
                        last = act.activation(act_v[:, t % 2, h * width:(h + 1) * width],
                                              bank(core, 2 * (t % 2) + h, 1)[:, 0:width], ACT.Gelu,
                                              accum_out=part[:, t % 2, h:h + 1])
                    last.then_inc(mapped, 1)

                def root(t):
                    act.wait_ge(squared, t + 1)
                    act.activation(rstd[:, t % 2:t % 2 + 1], ssq[:, t % 2:t % 2 + 1], ACT.Sqrt,
                                   bias=eps[:, 0:1], scale=1 / A_WIDTH).then_inc(rooted, 1)

                w.split_high(act)
                act.wait_ge(w.low, KT)
                for t in range(TT + 1):
                    if t < TT:
                        gelu(t)
                    if t >= 1:
                        root(t - 1)

            @block.vector
            def _(dve):
                steps = [0]

                def step(ins):
                    steps[0] += 1
                    ins.then_inc(chain, 1)
                    dve.wait_ge(chain, steps[0])

                w.split_low(dve)
                for t in range(TT):
                    s = t % 2
                    dve.wait_ge(mapped, t + 1)
                    dve.wait_ge(wide_loaded, 16)
                    step(dve.tensor_tensor(mean[:, s:s + 1], part[:, s, 0:1], part[:, s, 1:2], ALU.add))
                    step(dve.tensor_scalar(mean[:, s:s + 1], mean[:, s:s + 1], 1 / A_WIDTH, None, ALU.mult))
                    x = act_v[:, s, :]
                    step(dve.tensor_scalar(x, x, mean[:, s:s + 1], None, ALU.subtract))
                    dve.tensor_tensor_reduce(sq[:, :], x, x, 1.0, 0.0, ALU.mult, ALU.add,
                                             ssq[:, s:s + 1]).then_inc(squared, 1)
                    dve.wait_ge(rooted, t + 1)
                    step(dve.reciprocal(rstd[:, s:s + 1], rstd[:, s:s + 1]))
                    step(dve.scalar_tensor_tensor(out=vv[:, t, :], in0=x, scalar=rstd[:, s:s + 1],
                                                  in1=wide[:, 0, :], op0=ALU.mult, op1=ALU.mult))
                    dve.tensor_tensor(vv[:, t, :], vv[:, t, :], wide[:, 1, :], ALU.add).then_inc(done, 1)


def stage_merge(core, hT, ys, w, gate_tile, proj_tiles, gate_b, mergedT):
    nc = core.nc
    depth = [y[1] for y in ys]
    with ExitStack() as stack:
        wp = core.sb(stack, "w_proj", [P, 2, 6, P])
        gate = core.sb(stack, "gate", [P, 2, S])
        prod = core.sb(stack, "gated", [P, 2, S])
        loaded = [core.sem("merge_loaded") for _ in range(2)]
        made = core.sem("merge_made")
        opened = core.sem("merge_opened")
        used = core.sem("merge_used")
        summed = core.sem("merge_summed")

        def unit(i, n):
            return 2 * i + n // 3, n % 3, n % 2, 6 * i + n

        def sixes(engine, body):
            for n in range(6):
                body(0, n, n < 2, False)
            with engine.Fori(1, 3) as i:
                for n in range(6):
                    body(i, n, False, False)
            for n in range(6):
                body(3, n, False, n >= 4)

        def next_split(split, engine, i, n):
            split(engine, 3 * i + (n // 2 + 1), n % 2)

        with nc.Block(no_gpsimd_drain=True) as block:

            @block.sync
            def _(sp):
                def load_projection(i, n):
                    j, b, s, u = unit(i, n)
                    sp.dma_start(wp[:, s, 0:depth[b], :], proj_tiles[b](j)).then_inc(loaded[s], 16)

                def load(i, n, first, last):
                    j, b, s, u = unit(i, n)
                    if not (first and n == 0):
                        sp.wait_ge(w.low, u)
                        w.load_tile(sp, gate_tile(b, j))
                    if not (first and n == 0):
                        load_projection(i if n else i - 1, n - 1 if n else 5)

                sixes(sp, load)
                sp.wait_ge(w.low, 24)
                load_projection(3, 5)

            @block.tensor
            def _(pe):
                def products(i, n, first, last):
                    j, b, s, u = unit(i, n)
                    w.ready(pe, 3 * i + n // 2, s)
                    if not first:
                        pe.wait_ge(used, u - 1)
                    for h in range(2):
                        product(pe, bank(core, 4 * s + h, 1), w.lhs(s),
                                lambda part, k: hT[:, part, k, h * HALF:(h + 1) * HALF], range(KT))
                    pe.wait_ge(loaded[s], 48 * i + 16 * (n // 2) + 16)
                    for h in range(2):
                        for k in range(depth[b]):
                            last = pe.matmul(bank(core, 4 * s + 2 + h, 1), wp[:, s, k, :],
                                             ys[b][0][:, k, h * HALF:(h + 1) * HALF],
                                             start=(k == 0), stop=(k == depth[b] - 1))
                    last.then_inc(made, 1)

                sixes(pe, products)

            @block.scalar
            def _(act):
                def sigmoid(i, n, first, last):
                    j, b, s, u = unit(i, n)
                    act.wait_ge(made, u + 1)
                    if not last:
                        next_split(w.split_high, act, i, n)
                    if not first:
                        act.wait_ge(used, u - 1)
                    act.activation(gate[:, s, :], bank(core, 4 * s), ACT.Sigmoid,
                                   bias=gate_b(b, j)).then_inc(opened, 1)

                w.first_high(act)
                sixes(act, sigmoid)

            @block.vector
            def _(dve):
                def gated_sum(i, n, first, last):
                    j, b, s, u = unit(i, n)
                    if not last:
                        next_split(w.split_low, dve, i, n)
                    dve.wait_ge(opened, u + 1)
                    dst = mergedT[:, j, :] if b == 0 else prod[:, s, :]
                    if b == 1 and not first:
                        dve.wait_ge(summed, 4 * i + 2 * (n // 3))
                    dve.tensor_tensor(dst, bank(core, 4 * s + 2), gate[:, s, :], ALU.mult).then_inc(used, 1)
                    if b > 0:
                        dve.wait_ge(used, u + 1)
                        if b == 2:
                            dve.wait_ge(summed, 4 * i + 2 * (n // 3) + 1)
                        dve.tensor_tensor(mergedT[:, j, :], mergedT[:, j, :], prod[:, s, :],
                                          ALU.add).then_inc(summed, 1)

                w.first_low(dve)
                sixes(dve, gated_sum)


def stage_mix_chunks(core, vv, spatial_dram, spatial_b_dram, yaT, ahead):
    nc = core.nc
    with ExitStack() as stack:
        wT = core.sb(stack, "spatial_w", [P, 4, P])
        bias = core.sb(stack, "spatial_b", [P, 6, P])
        held = core.sb(stack, "spatial_sum", [P, 2, S])
        loaded = core.sem("spatial_loaded")
        masked = core.sem("spatial_masked")
        made = core.sem("spatial_made")
        added = core.sem("spatial_added")
        with nc.Block(no_gpsimd_drain=True) as block:

            @block.sync
            def _(sp):
                sp.dma_start(wT[:, :, :], spatial_dram).then_inc(loaded, 16)
                sp.dma_start(bias[:, :, :], spatial_b_dram).then_inc(loaded, 16)
                ahead.ahead_load(sp)

            @block.scalar
            def _(act):
                ahead.ahead_high(act)

            @block.gpsimd
            def _(pool):
                pool.wait_ge(loaded, 32)
                pool.affine_select(out=wT[:, :, :], in_=wT[:, :, :], compare_op=ALU.is_ge, fill=0.0, base=0,
                                   pattern=[[0, 4], [1, P]], channel_multiplier=-1).then_inc(masked, 1)

            @block.tensor
            def _(pe):
                pe.wait_ge(masked, 1)
                for c in range(6):
                    if c >= 2:
                        pe.wait_ge(added, c - 1)
                    for t in range(TT):
                        for rows in ([slice(0, 64), slice(64, 128)] if c in (1, 4) else [slice(0, 128)]):
                            first = c * P + rows.start
                            last = pe.matmul(bank(core, 2 * (c % 2))[rows, t * P:(t + 1) * P],
                                             vv[:, t, first:first + rows.stop - rows.start],
                                             wT[:, first // 192, :], start=True, stop=True)
                    last.then_inc(made, 1)

            @block.vector
            def _(dve):
                for c in range(6):
                    s = c % 2
                    dve.wait_ge(made, c + 1)
                    split = lambda a: a.rearrange("p (n t) -> p n t", t=P)
                    dve.tensor_tensor(split(held[:, s, :]), split(bank(core, 2 * s)),
                                      bias[:, c, :].unsqueeze(1).to_broadcast([P, TT, P]),
                                      ALU.add).then_inc(added, 1)
                    dve.wait_ge(added, c + 1)
                    if c == 1:
                        ahead.ahead_low(dve)
                    dve.tensor_tensor(yaT[:, c, :], yaT[:, c, :], held[:, s, :], ALU.mult)


def stage_output(core, yT, weights, base_tile, gate, dst, final=None):
    nc = core.nc
    with ExitStack() as stack:
        w = SplitMatrix(core, stack, weights, D)
        y = core.sb(stack, "y_parts", [P, 4, 2, KT, P], F32R)
        base = core.sb(stack, "base", [P, 2, D]) if base_tile else None
        base_loaded = [core.sem("base_loaded") for _ in range(2)]
        y_high = core.sem("y_high")
        y_low = core.sem("y_low")
        made = core.sem("out_made")
        gated = core.sem("out_gated")
        added = core.sem("out_added")
        if final:
            final_gain, eps, out_tiles = final
            gain = core.sb(stack, "final_gain", [P, D])
            sq = core.sb(stack, "final_sq", [P, D])
            rows_out = core.sb(stack, "final_y", [P, 2, D])
            stat = core.sb(stack, "final_stat", [P, 2, TT])
            gain_loaded = core.sem("final_gain_loaded")
            summed = core.sem("final_summed")
            rooted = core.sem("final_rooted")
            inverted = core.sem("final_inverted")
            scaled = core.sem("final_scaled")
            stored = [core.sem("final_stored") for _ in range(2)]
        tokens = lambda t: yT[:, :, t * P:(t + 1) * P]
        with nc.Block(no_gpsimd_drain=True) as block:

            @block.sync
            def _(sp):
                w.fetch(sp)
                if base_tile:
                    for t in range(TT):
                        if t >= 2:
                            sp.wait_ge(added, t - 1)
                        sp.dma_start(base[:, t % 2, :], base_tile(t)).then_inc(base_loaded[t % 2], 16)
                if final:
                    sp.dma_start(gain[:, :], final_gain).then_inc(gain_loaded, 16)
                    for t in range(TT):
                        sp.wait_ge(scaled, t + 1)
                        sp.dma_start(out_tiles[t], rows_out[:, t % 2, :]).then_inc(stored[t % 2], 16)
                    for s in stored:
                        sp.wait_ge(s, 16 * TT // 2)

            @block.tensor
            def _(pe):
                units = [([bank(core, 2 * (t % 4) + h, 1) for h in range(2)],
                          lambda part, k, t=t: y[:, t % 4, part, k, :], [0, HALF], HALF) for t in range(TT)]
                pe.wait_ge(y_low, 2)
                w.products(pe, True, *units[:2]).then_inc(made, 2)
                for t in range(2, TT):
                    pe.wait_ge(y_low, t + 1)
                    if t >= 4:
                        pe.wait_ge(added, t - 3)
                    w.products(pe, False, units[t]).then_inc(made, 1)

            @block.scalar
            def _(act):
                def split(t):
                    if t >= 4:
                        act.wait_ge(made, t - 3)
                    act.copy(y[:, t % 4, HI, :, :], tokens(t)).then_inc(y_high, 1)

                def root(t):
                    act.wait_ge(added, t + 1)
                    if t >= 1:
                        act.wait_ge(summed, t)
                    act.activation(sq[:, :], dst[:, t, :], ACT.Square,
                                   accum_out=stat[:, 0, t:t + 1]).then_inc(summed, 1)
                    act.wait_ge(summed, t + 1)
                    act.activation(stat[:, 1, t:t + 1], stat[:, 0, t:t + 1], ACT.Sqrt, bias=eps[:, 0:1],
                                   scale=1 / D).then_inc(rooted, 1)

                split(0)
                split(1)
                w.split_high(act)
                for t in range(2, TT + 4):
                    if t < TT:
                        split(t)
                    if final and t >= 4:
                        root(t - 4)

            @block.vector
            def _(dve):
                def split(t):
                    dve.wait_ge(y_high, t + 1)
                    dve.tensor_tensor(y[:, t % 4, LO, :, :], tokens(t), y[:, t % 4, HI, :, :].bitcast(F32),
                                      ALU.subtract).then_inc(y_low, 1)

                def scale(t):
                    dve.wait_ge(rooted, t + 1)
                    dve.reciprocal(stat[:, 1, t:t + 1], stat[:, 1, t:t + 1]).then_inc(inverted, 1)
                    dve.wait_ge(inverted, t + 1)
                    if t >= 2:
                        dve.wait_ge(stored[t % 2], 16 * (t // 2))
                    dve.scalar_tensor_tensor(out=rows_out[:, t % 2, :], in0=dst[:, t, :],
                                             scalar=stat[:, 1, t:t + 1], in1=gain[:, :], op0=ALU.mult,
                                             op1=ALU.mult).then_inc(scaled, 1)

                split(0)
                split(1)
                w.split_low(dve)
                split(2)
                split(3)
                if final:
                    dve.wait_ge(gain_loaded, 16)
                for t in range(TT):
                    dve.wait_ge(made, t + 1)
                    if t + 4 < TT:
                        split(t + 4)
                    rows = bank(core, 2 * (t % 4))
                    if base_tile:
                        dve.wait_ge(base_loaded[t % 2], 16 * (t // 2) + 16)
                        dve.tensor_tensor(dst[:, t, :], rows, base[:, t % 2, :], ALU.add).then_inc(added, 1)
                    else:
                        dve.tensor_tensor(rows, rows, gate, ALU.mult).then_inc(gated, 1)
                        dve.wait_ge(gated, t + 1)
                        dve.tensor_tensor(dst[:, t, :], rows, dst[:, t, :], ALU.add).then_inc(added, 1)
                    if final and t >= 1:
                        scale(t - 1)
                if final:
                    scale(TT - 1)


class Modulation(Beside):

    AT = (2, 3, 4, 5, 8, 9, 10, 11)
    SUM_AT = 14
    PART = 3 * D // 2

    def __init__(self, core, stack, cond_cols, ada, ada_b, gate_b, ones, norm_gain, mod, gate_dram, gate):
        self.core, self.cond_cols, self.ada, self.ada_b, self.gate_b = core, cond_cols, ada, ada_b, gate_b
        self.ones, self.norm_gain, self.mod, self.gate_dram, self.gate = ones, norm_gain, mod, gate_dram, gate
        self.w = core.sb(stack, "ada_w", [P, 2, self.PART])
        self.acc = core.sb(stack, "ada_sum", [P, 3 * D])
        self.cond = core.sb(stack, "cond", [P, KT])
        self.loaded = [core.sem("ada_loaded") for _ in range(2)]
        self.cond_loaded, self.silued, self.weighed, self.summed, self.added, self.final, self.saved = (
            core.sem("mod_" + n) for n in ("cond_loaded", "silued", "weighed", "summed", "added", "final", "saved"))

    def sync(self, sp, t):
        if t == 0:
            sp.dma_start(self.cond[:, :], self.cond_cols).then_inc(self.cond_loaded, 16)
            sp.dma_start(self.gate, self.gate_b).then_inc(self.cond_loaded, 16)
        if t in self.AT:
            k = self.AT.index(t)
            for h in range(2):
                if k:
                    sp.wait_ge(self.weighed, 2 * k + h - 1)
                sp.dma_start(self.w[:, h, :], self.ada[:, k, h * self.PART:(h + 1) * self.PART])\
                  .then_inc(self.loaded[h], 16)

    def sync_end(self, sp):
        sp.wait_ge(self.final, 2)
        sp.dma_start(self.gate_dram, self.gate).then_inc(self.saved, 16)
        sp.wait_ge(self.saved, 16)

    def scalar(self, act, t):
        if t == 0:
            act.wait_ge(self.cond_loaded, 32)
            act.activation(self.cond[:, :], self.cond[:, :], ACT.Silu).then_inc(self.silued, 1)

    def tensor(self, pe, t):
        if t == self.SUM_AT:
            pe.wait_ge(self.weighed, 2 * KT)
            for j in range(2 * KT):
                pe.matmul(bank(self.core, 4, 1)[:, j:j + 1], self.acc[:, j * P:(j + 1) * P],
                          self.ones[:, 0:1], start=True, stop=True)
            for h in range(2):
                last = pe.matmul(bank(self.core, 5 + h, 1), self.ones,
                                 self.acc[:, 2 * D + h * HALF:2 * D + (h + 1) * HALF], start=True, stop=True)
            last.then_inc(self.summed, 1)

    def vector(self, dve, t):
        if t in self.AT:
            k = self.AT.index(t)
            if k == 0:
                dve.wait_ge(self.silued, 1)
            for h in range(2):
                dve.wait_ge(self.loaded[h], 16 * k + 16)
                acc = self.acc[:, h * self.PART:(h + 1) * self.PART]
                if k == 0:
                    dve.tensor_scalar(acc, self.w[:, h, :], self.cond[:, 0:1], None, ALU.mult)\
                       .then_inc(self.weighed, 1)
                else:
                    dve.wait_ge(self.weighed, 2 * k + h - 1)
                    dve.scalar_tensor_tensor(out=acc, in0=self.w[:, h, :], scalar=self.cond[:, k:k + 1], in1=acc,
                                             op0=ALU.mult, op1=ALU.add).then_inc(self.weighed, 1)

    def vector_end(self, dve):
        dve.wait_ge(self.summed, 1)
        dve.tensor_tensor(self.mod[:, :], bank(self.core, 4, 1)[:, 0:2 * KT], self.ada_b[:, 0:2 * KT],
                          ALU.add).then_inc(self.added, 1)
        dve.wait_ge(self.added, 1)
        gain = self.mod[:, KT:2 * KT]
        dve.scalar_tensor_tensor(out=gain, in0=gain, scalar=1.0, in1=self.norm_gain,
                                 op0=ALU.add, op1=ALU.mult).then_inc(self.final, 1)
        dve.wait_ge(self.cond_loaded, 32)
        dve.tensor_tensor(self.gate, bank(self.core, 5), self.gate, ALU.add).then_inc(self.final, 1)


LN2_HI = 0.693359375
LN2_LO = -2.12194440e-4
ROUND = 1.5 * 2 ** 23
TWO_PI = (6.28125, 1.9340515e-3, 1.2556660e-6)


class SsmMatrices(Beside):

    def __init__(self, core, stack, prm_dram, bc_dram, const, kept, powers, d_cols, room):
        N = SSM_GROUPS
        G = room[:, 0:4, :].rearrange("p a (b c) -> p (a b) c", c=2 * P)
        M_out = room[:, 4:6, :].rearrange("p a (b c) -> p (a b) c", c=P)
        c_stack = core.sb(stack, "ssm_C", [P, N, N])
        prm = core.sb(stack, "ssm_prm", [P, 4, N])
        bc = core.sb(stack, "ssm_bc", [P, 4, N, N])
        tiny = core.sb(stack, "ssm_tiny", [P, 13, N])
        whole = core.sb(stack, "ssm_int", [P, N], I32)
        pre = core.sb(stack, "ssm_pw_re", [P, 9, N])
        pim = core.sb(stack, "ssm_pw_im", [P, 9, N])
        mats = core.sb(stack, "ssm_mats", [P, 4, N, N])
        tmp = core.sb(stack, "ssm_tmp", [P, N, N])
        self.kept, self.inputs = list(zip(kept, (G, M_out, c_stack))), ((prm, prm_dram), (bc, bc_dram))
        self.sign = const[:, SIGN:SIGN + 1]
        self.memory = G, M_out, c_stack, prm, bc, tiny, whole, pre, pim, mats, tmp, powers, d_cols
        self.loaded, self.chain, self.finished, self.saved = (
            core.sem("ssm_" + n) for n in ("loaded", "chain", "finished", "saved"))

    def sync(self, sp, t):
        if t == 0:
            for into, there in self.inputs:
                sp.dma_start(into[:], there).then_inc(self.loaded, 16)
        if t == 14:
            sp.wait_ge(self.finished, 1)
            for there, made in self.kept:
                sp.dma_start(there, made[:, :, :]).then_inc(self.saved, 16)

    def sync_end(self, sp):
        sp.wait_ge(self.saved, 16 * len(self.kept))

    def gpsimd(self, pool):
        G, M_out, c_stack, prm, bc, tiny, whole, pre, pim, mats, tmp, powers, d_cols = self.memory
        chain, loaded, finished, sign, N = self.chain, self.loaded, self.finished, self.sign, SSM_GROUPS
        steps = [0]

        def step(ins):
            steps[0] += 1
            ins.then_inc(chain, 1)
            pool.wait_ge(chain, steps[0])

        def tt(out, a, b, op):
            step(pool.tensor_tensor(out, a, b, op))

        def ts(out, a, s1, op1, s2=None, op2=ALU.bypass):
            if s2 is None:
                step(pool.tensor_scalar(out, a, s1, None, op1))
            else:
                step(pool.tensor_scalar(out, a, s1, s2, op1, op2))

        def stt(out, a, s, b, op1, op2):
            ts(tiny[:, 12, :], a, s, op1)
            tt(out, tiny[:, 12, :], b, op2)

        def horner(acc, x, coeffs):
            ts(acc, x, coeffs[-1], ALU.mult)
            for c in reversed(coeffs[:-1]):
                stt(acc, acc, c, x, ALU.add, ALU.mult)

        def exponential(out, x, k, r):
            ts(x, x, -87.0, ALU.max, 88.7, ALU.min)
            ts(k, x, 1 / math.log(2), ALU.mult)
            ts(k, k, ROUND, ALU.add)
            ts(k, k, ROUND, ALU.subtract)
            stt(r, k, -LN2_HI, x, ALU.mult, ALU.add)
            stt(r, k, -LN2_LO, r, ALU.mult, ALU.add)
            horner(out, r, [1 / math.factorial(i) for i in range(1, 10)])
            ts(out, out, 1.0, ALU.add)
            ts(k, k, 127.0, ALU.add)
            ts(k, k, 2.0 ** 23, ALU.mult)
            step(pool.tensor_copy(whole[:, :], k))
            tt(out, out, whole[:, :].bitcast(F32), ALU.mult)

        pool.wait_ge(loaded, 32)
        lr, li, ls, dd = (prm[:, i, :] for i in range(4))
        stepv, mag, ang, cosv, sinv, a, b, c, den, fr, fi, ai = (tiny[:, i, :] for i in range(12))
        step(pool.tensor_copy(d_cols[:, :], dd))
        exponential(stepv, ls, a, b)
        tt(c, lr, stepv, ALU.mult)
        exponential(mag, c, a, b)
        tt(ang, li, stepv, ALU.mult)
        ts(a, ang, 1 / (2 * math.pi), ALU.mult)
        ts(a, a, ROUND, ALU.add)
        ts(a, a, ROUND, ALU.subtract)
        for part in TWO_PI:
            stt(ang, a, -part, ang, ALU.mult, ALU.add)
        ts(ang, ang, 0.5, ALU.mult)
        tt(b, ang, ang, ALU.mult)
        horner(sinv, b, [(-1) ** i / math.factorial(2 * i + 1) for i in range(1, 8)])
        stt(sinv, sinv, 1.0, ang, ALU.add, ALU.mult)
        horner(cosv, b, [(-1) ** i / math.factorial(2 * i) for i in range(1, 9)])
        ts(cosv, cosv, 1.0, ALU.add)
        tt(c, sinv, cosv, ALU.mult)
        tt(cosv, sinv, sinv, ALU.mult)
        ts(cosv, cosv, -2.0, ALU.mult, 1.0, ALU.add)
        stt(pim[:, 1, :], c, 2.0, mag, ALU.mult, ALU.mult)
        tt(pre[:, 1, :], cosv, mag, ALU.mult)
        ar, ai = pre[:, 1, :], pim[:, 1, :]
        tt(a, lr, lr, ALU.mult)
        tt(den, li, li, ALU.mult)
        tt(den, den, a, ALU.add)
        step(pool.memset(c, -1.0))
        tt(den, den, c, ALU.pow)
        ts(c, ar, -1.0, ALU.add)
        tt(a, c, lr, ALU.mult)
        tt(b, ai, li, ALU.mult)
        tt(fr, a, b, ALU.add)
        tt(fr, fr, den, ALU.mult)
        tt(a, ai, lr, ALU.mult)
        tt(b, c, li, ALU.mult)
        tt(fi, a, b, ALU.subtract)
        tt(fi, fi, den, ALU.mult)

        def times(outr, outi, xr, xi, yr, yi):
            tt(a, xr, yr, ALU.mult)
            tt(b, xi, yi, ALU.mult)
            tt(outr, a, b, ALU.subtract)
            tt(a, xr, yi, ALU.mult)
            tt(b, xi, yr, ALU.mult)
            tt(outi, a, b, ALU.add)

        for k in range(1, 8):
            times(pre[:, k + 1, :], pim[:, k + 1, :], pre[:, k, :], pim[:, k, :], ar, ai)
        step(pool.tensor_copy(powers[:, 0, 0, :], pre[:, 8, :]))
        step(pool.tensor_copy(powers[:, 1, 0, :], pim[:, 8, :]))
        for k in range(1, LEVELS):
            r, i = powers[:, 0, k - 1, :], powers[:, 1, k - 1, :]
            times(powers[:, 0, k, :], powers[:, 1, k, :], r, i, r, i)

        wide = lambda v: v.unsqueeze(2).to_broadcast([P, N, N])
        B, iB, C, iC = (mats[:, i, :, :] for i in range(4))
        b1, b2, c1, c2 = (bc[:, i, :, :] for i in range(4))
        ts(b2, b2, sign, ALU.mult)
        tt(B, b1, wide(fr), ALU.mult)
        tt(tmp[:, :, :], b2, wide(fi), ALU.mult)
        tt(B, B, tmp[:, :, :], ALU.add)
        tt(iB, b2, wide(fr), ALU.mult)
        tt(tmp[:, :, :], b1, wide(fi), ALU.mult)
        tt(iB, iB, tmp[:, :, :], ALU.subtract)
        ts(C, c1, sign, ALU.mult, -1.0, ALU.mult)
        ts(iC, c2, -1.0, ALU.mult)
        step(pool.memset(G[:, :, P:2 * P], 0.0))

        def mix(out, r, i, x, y):
            tt(out, x, wide(r), ALU.mult)
            tt(tmp[:, :, :], y, wide(i), ALU.mult)
            tt(out, out, tmp[:, :, :], ALU.add)

        step(pool.tensor_copy(G[:, :, 7 * N:8 * N], B))
        for k in range(1, 8):
            mix(G[:, :, (7 - k) * N:(8 - k) * N], pre[:, k, :], pim[:, k, :], B, iB)
        for t in range(8):
            mix(M_out[:, :, t * N:(t + 1) * N], pre[:, t + 1, :], pim[:, t + 1, :], C, iC)
        pool.tensor_copy(c_stack[:, :, :], C).then_inc(finished, 1)


def stage_ssm_scan(core, L_room, scratch_u, const, ident, G, M_out, c_stack, powers, d_cols, Y):
    nc = core.nc
    N = SSM_GROUPS
    with ExitStack() as stack:
        U = core.sb(stack, "ssm_U", [P, N, P])
        Gt = core.sb(stack, "ssm_Gt", [P, N, P])
        T = core.sb(stack, "ssm_T", [P, N, P])
        X = core.sb(stack, "ssm_X", [P, N, P])
        L_late = core.sb(stack, "ssm_L", [P, 2, N, P])
        spread = core.sem("u_spread")
        turned = core.sem("g_turned")
        g_kept = core.sem("g_kept")
        t_made = core.sem("t_made")
        t_kept = core.sem("t_kept")
        v_made = core.sem("v_made")
        x_new = core.sem("x_new")
        diag = core.sem("level_diag")
        level = core.sem("level_ready")
        carried = core.sem("carried")
        y_made = core.sem("y_made")
        swap = const[:, SWAP:SWAP + P]

        def L(k):
            return L_room[:, k, :, :] if k < LEVELS - 2 else L_late[:, k - LEVELS + 2, :, :]

        with nc.Block(no_gpsimd_drain=True) as block:

            @block.sync
            def _(sp):
                for t in range(8):
                    sp.dma_start(U[N * t:N * t + N, :, :],
                                 scratch_u[:, :, t, :].rearrange("g h c -> h g c")).then_inc(spread, 16)

            @block.tensor
            def _(pe):
                for a in range(4):
                    for g in range(4 * a, 4 * a + 4):
                        last = pe.transpose(bank(core, a, 1)[:, (g % 4) * P:(g % 4 + 1) * P],
                                            G[:, g, 0:P], ident)
                    last.then_inc(turned, 1)
                for a in range(4):
                    for g in range(4 * a, 4 * a + 4):
                        for t in range(8):
                            at = (g % 4) * P + t * N
                            last = pe.matmul(bank(core, 4 + a, 1)[:, at:at + N],
                                             G[:, g, (7 - t) * N:(7 - t) * N + P], c_stack[:, g, :],
                                             start=True, stop=True)
                    last.then_inc(t_made, 1)
                pe.wait_ge(spread, 128)
                for a in range(4):
                    pe.wait_ge(g_kept, a + 1)
                    for g in range(4 * a, 4 * a + 4):
                        last = pe.matmul(bank(core, a, 1)[:, (g % 4) * P:(g % 4 + 1) * P],
                                         Gt[:, g, :], U[:, g, :], start=True, stop=True)
                    last.then_inc(v_made, 1)
                for k in range(LEVELS):
                    pe.wait_ge(level, k + 1)
                    for a in range(4):
                        pe.wait_ge(x_new, 4 * k + a + 1)
                        for g in range(4 * a, 4 * a + 4):
                            width = P - 2 ** k
                            last = pe.matmul(bank(core, a, 1)[:, (g % 4) * P:(g % 4) * P + width],
                                             L(k)[:, g, :], X[:, g, 0:width], start=True, stop=True)
                        last.then_inc(carried, 1)
                pe.wait_ge(t_kept, 1)
                for a in range(4):
                    pe.wait_ge(x_new, 4 * LEVELS + a + 1)
                    for g in range(4 * a, 4 * a + 4):
                        at = (g % 4) * P
                        pe.matmul(bank(core, 4 + a, 1)[:, at:at + P], T[:, g, :], U[:, g, :],
                                  start=True, stop=False)
                        last = pe.matmul(bank(core, 4 + a, 1)[:, at + 1:at + P], M_out[:, g, :],
                                         X[:, g, 0:P - 1], start=False, stop=True)
                    last.then_inc(y_made, 1)

            @block.scalar
            def _(act):
                def diagonals(k):
                    for g in range(N):
                        last = act.activation(L(k)[:, g, :], ident, ACT.Copy, scale=powers[:, 0, k, g:g + 1])
                    last.then_inc(diag, 1)

                for k in range(LEVELS):
                    diagonals(k)
                    if 2 <= k < 6:
                        a = k - 2
                        act.wait_ge(turned, a + 1)
                        act.copy(Gt[:, 4 * a:4 * a + 4, :].rearrange("p g s -> p (g s)"),
                                 bank(core, a, 1)).then_inc(g_kept, 1)
                for a in range(4):
                    act.wait_ge(y_made, a + 1)
                    act.copy(Y[:, 4 * a:4 * a + 4, :].rearrange("p g s -> p (g s)"), bank(core, 4 + a, 1))

            @block.vector
            def _(dve):
                def level_matrices(k):
                    dve.wait_ge(diag, k + 1)
                    for g in range(N):
                        m = L(k)[:, g, :]
                        last = dve.scalar_tensor_tensor(out=m, in0=swap, scalar=powers[:, 1, k, g:g + 1],
                                                        in1=m, op0=ALU.mult, op1=ALU.add)
                    last.then_inc(level, 1)

                for k in range(5):
                    level_matrices(k)
                for a in range(4):
                    dve.wait_ge(t_made, a + 1)
                    for g in range(4 * a, 4 * a + 4):
                        last = dve.scalar_tensor_tensor(
                            out=T[:, g, :], in0=ident, scalar=d_cols[:, g:g + 1],
                            in1=bank(core, 4 + a, 1)[:, (g % 4) * P:(g % 4 + 1) * P],
                            op0=ALU.mult, op1=ALU.add)
                last.then_inc(t_kept, 1)
                level_matrices(5)
                level_matrices(6)
                for a in range(4):
                    dve.wait_ge(v_made, a + 1)
                    dve.tensor_copy(X[:, 4 * a:4 * a + 4, :].rearrange("p g s -> p (g s)"),
                                    bank(core, a, 1)).then_inc(x_new, 1)
                for k in range(LEVELS):
                    for a in range(4):
                        dve.wait_ge(carried, 4 * k + a + 1)
                        later = X[:, 4 * a:4 * a + 4, 2 ** k:P]
                        dve.tensor_tensor(later, later,
                                          bank(core, a, 1).rearrange("p (g s) -> p g s", g=4)[:, :, 0:P - 2 ** k],
                                          ALU.add).then_inc(x_new, 1)


def stage_ssm_output(core, Y, scratch_y, glu_dram, glu_b, yT):
    nc = core.nc
    N = SSM_GROUPS
    with ExitStack() as stack:
        ys = core.sb(stack, "ssm_ys", [P, 2, S])
        sig = core.sb(stack, "ssm_sig", [P, 2, S])
        w = core.sb(stack, "glu_w", [P, 2, 2 * P])
        saved = core.sem("y_saved")
        loaded = core.sem("y_loaded")
        mapped = core.sem("y_mapped")
        made = core.sem("glu_made")
        opened = core.sem("glu_opened")
        gated = core.sem("glu_gated")
        with nc.Block(no_gpsimd_drain=True) as block:

            @block.sync
            def _(sp):
                sp.dma_start(w[:, :, :], glu_dram).then_inc(loaded, 16)
                for t in range(8):
                    sp.dma_start(scratch_y[:, :, t, :].rearrange("g h c -> h g c"),
                                 Y[N * t:N * t + N, :, :]).then_inc(saved, 16)
                sp.wait_ge(saved, 128)
                for j in range(2):
                    sp.dma_start(ys[:, j, :], scratch_y[8 * j:8 * j + 8].rearrange("g h t c -> (g h) (t c)"))\
                      .then_inc(loaded, 16)

            @block.scalar
            def _(act):
                act.wait_ge(loaded, 48)
                act.activation(ys[:, :, :], ys[:, :, :], ACT.Gelu_apprx_tanh).then_inc(mapped, 1)
                for m in range(2):
                    act.wait_ge(made, m + 1)
                    act.activation(sig[:, m, :], bank(core, 2 * m), ACT.Sigmoid,
                                   bias=glu_b[:, m:m + 1]).then_inc(opened, 1)

            @block.tensor
            def _(pe):
                pe.wait_ge(mapped, 1)
                for m in range(2):
                    for h in range(2):
                        for k in range(2):
                            last = pe.matmul(bank(core, 2 * m + h, 1), w[:, k, m * P:(m + 1) * P],
                                             ys[:, k, h * HALF:(h + 1) * HALF], start=(k == 0), stop=(k == 1))
                    last.then_inc(made, 1)

            @block.vector
            def _(dve):
                for m in range(2):
                    dve.wait_ge(opened, m + 1)
                    dve.tensor_tensor(sig[:, m, :], ys[:, m, :], sig[:, m, :], ALU.mult).then_inc(gated, 1)
                    dve.wait_ge(gated, m + 1)
                    by_chunk = yT[:, m, :].rearrange("p (c t) -> p c t", t=8)
                    dve.tensor_tensor(by_chunk, by_chunk, sig[:, m, :].rearrange("p (t c) -> p c t", t=8),
                                      ALU.mult)


def stage_diff_tables(core, lam_dram, neg_lam):
    nc = core.nc
    with ExitStack() as stack:
        rows = core.sb(stack, "lam_rows", [P, 4, 64])
        prod = core.sb(stack, "lam_prod", [P, 64])
        dots = core.sb(stack, "lam_dots", [P, 2])
        loaded = core.sem("lam_loaded")
        dotted = core.sem("lam_dotted")
        exped = core.sem("lam_exped")
        with nc.Block(no_gpsimd_drain=True) as block:

            @block.sync
            def _(sp):
                sp.dma_start(rows[:, :, :], lam_dram).then_inc(loaded, 16)

            @block.vector
            def _(dve):
                dve.wait_ge(loaded, 16)
                for i in range(2):
                    dve.tensor_tensor_reduce(prod[:, :], rows[:, 2 * i, :], rows[:, 2 * i + 1, :], 1.0, 0.0,
                                             ALU.mult, ALU.add, dots[:, i:i + 1]).then_inc(dotted, 1)
                    dve.wait_ge(dotted, i + 1)
                dve.wait_ge(exped, 1)
                dve.tensor_tensor(neg_lam[:, :], dots[:, 1:2], dots[:, 0:1], ALU.subtract).then_inc(dotted, 1)
                dve.wait_ge(dotted, 3)
                dve.tensor_scalar(neg_lam[:, :], neg_lam[:, :], -LAM_INIT, None, ALU.add)

            @block.scalar
            def _(act):
                act.wait_ge(dotted, 2)
                act.activation(dots[:, :], dots[:, :], ACT.Exp).then_inc(exped, 1)


def stage_diff_attention(core, qT, kT, v, far_dram, neg_lam, ident, out, loads):
    nc = core.nc
    units = [(h, t if h % 2 == 0 else TT - 1 - t) for h in range(4) for t in range(TT)]
    n = len(units)
    with ExitStack() as stack:
        far = core.sb(stack, "far", [P, D])
        bias = core.sb(stack, "alibi", [P, 2, D])
        p = core.sb(stack, "diff_p", [P, 3, 2, D])
        pT = core.sb(stack, "diff_pT", [P, 2, D])
        top = core.sb(stack, "diff_top", [P, 2, 2])
        low = core.sb(stack, "diff_low", [P, 2, 2])
        total = core.sb(stack, "diff_total", [P, 2, 2])
        inv = core.sb(stack, "diff_inv", [P, 8, 2])
        far_loaded = core.sem("far_loaded")
        loaded = core.sem("later_inputs_loaded")
        scored = core.sem("diff_scored")
        maxed = core.sem("diff_maxed")
        small = core.sem("diff_small")
        exped = core.sem("diff_exped")
        weighted = core.sem("diff_weighted")
        turned = core.sem("diff_turned")
        moved_act = core.sem("diff_moved_act")
        moved_dve = core.sem("diff_moved_dve")
        mixed = core.sem("diff_mixed")
        stored = core.sem("diff_stored")

        def place(b):
            return HALF * (b % 2) + P * (b // 2)

        with nc.Block(no_gpsimd_drain=True) as block:

            @block.sync
            def _(sp):
                sp.dma_start(far[:, :], far_dram).then_inc(far_loaded, 16)
                for there, into in loads:
                    sp.dma_start(into[:], there).then_inc(loaded, 16)
                sp.wait_ge(loaded, 16 * len(loads))

            @block.tensor
            def _(pe):
                def scores(u):
                    h, t = units[u]
                    width = (t + 1) * P
                    if u >= 1:
                        pe.wait_ge(maxed, u)
                    for c0 in range(0, width, HALF):
                        cw = min(HALF, width - c0)
                        for m in range(2):
                            rows = slice(64 * m, 64 * m + 64)
                            last = pe.matmul(bank(core, 2 * m)[:, c0:c0 + cw], qT[rows, h, t * P:(t + 1) * P],
                                             kT[rows, h, c0:c0 + cw], start=True, stop=True)
                    last.then_inc(scored, 1)

                def turn(u):
                    h, t = units[u]
                    pe.wait_ge(weighted, u + 1)
                    if u >= 1:
                        pe.wait_ge(moved_act, u)
                        pe.wait_ge(moved_dve, u)
                    for b in range(t + 1):
                        last = pe.transpose(bank(core, 4)[:, place(b):place(b) + P],
                                            p[:, u % 3, 0, b * P:(b + 1) * P], ident)
                    last.then_inc(turned, 1)

                def mix(u):
                    h, t = units[u]
                    pe.wait_ge(moved_act, u + 1)
                    pe.wait_ge(moved_dve, u + 1)
                    if u >= 2:
                        pe.wait_ge(stored, u - 1)
                    for b in range(t + 1):
                        last = pe.matmul(bank(core, 6 + u % 2, 1)[:, 0:P], pT[:, u % 2, place(b):place(b) + P],
                                         v[:, b, h * P:(h + 1) * P], start=(b == 0), stop=(b == t))
                    last.then_inc(mixed, 1)

                for u in range(n + 3):
                    if u < n:
                        scores(u)
                    if 2 <= u < n + 2:
                        turn(u - 2)
                    if u >= 3:
                        mix(u - 3)

            @block.vector
            def _(dve):
                steps = [0]

                def step(ins):
                    steps[0] += 1
                    ins.then_inc(small, 1)
                    dve.wait_ge(small, steps[0])

                def slopes(h):
                    step(dve.tensor_scalar(bias[:, h % 2, :], far[:, :], 2.0 ** -(5 + h), None, ALU.mult))

                def maxima(u):
                    h, t = units[u]
                    s = u % 2
                    width = (t + 1) * P
                    if u % TT == 0:
                        slopes(h)
                    dve.wait_ge(scored, u + 1)
                    if u >= 3:
                        dve.wait_ge(turned, u - 2)
                    for m in range(2):
                        last = dve.tensor_tensor_reduce(
                            p[:, u % 3, m, 0:width], bank(core, 2 * m)[:, 0:width], bias[:, h % 2, D - width:D],
                            1.0, -3e38, ALU.add, ALU.max, top[:, s, m:m + 1])
                    step(last)
                    dve.tensor_scalar(low[:, s, :], top[:, s, :], -1.0, None, ALU.mult).then_inc(maxed, 1)

                def weights(u):
                    h, t = units[u]
                    s = u % 2
                    width = (t + 1) * P
                    dve.wait_ge(exped, u + 1)
                    step(dve.reciprocal(inv[:, u % 8, :], total[:, s, :]))
                    ratio = inv[:, u % 8, 1:2]
                    step(dve.tensor_scalar(ratio, ratio, neg_lam, total[:, s, 0:1], ALU.mult, ALU.mult))
                    p1, p2 = p[:, u % 3, 0, 0:width], p[:, u % 3, 1, 0:width]
                    dve.scalar_tensor_tensor(out=p1, in0=p2, scalar=ratio, in1=p1, op0=ALU.mult,
                                             op1=ALU.add).then_inc(weighted, 1)

                def move(u):
                    h, t = units[u]
                    dve.wait_ge(turned, u + 1)
                    if u >= 2:
                        dve.wait_ge(mixed, u - 1)
                    if t == 0:
                        dve.sem_inc(moved_dve, 1)
                        return
                    odd = (t + 1) // 2 * P
                    dve.tensor_copy(pT[:, u % 2, HALF:HALF + odd],
                                    bank(core, 5, 1)[:, 0:odd]).then_inc(moved_dve, 1)

                def store(u):
                    h, t = units[u]
                    dve.wait_ge(mixed, u + 1)
                    dve.tensor_scalar(out[:, t, h * P:(h + 1) * P], bank(core, 6 + u % 2, 1)[:, 0:P],
                                      inv[:, u % 8, 0:1], None, ALU.mult).then_inc(stored, 1)

                dve.wait_ge(far_loaded, 16)
                for u in range(n + 4):
                    if 1 <= u <= n:
                        weights(u - 1)
                    if u < n:
                        maxima(u)
                    if 2 <= u < n + 2:
                        move(u - 2)
                    if u >= 4:
                        store(u - 4)

            @block.scalar
            def _(act):
                def move(u):
                    h, t = units[u]
                    act.wait_ge(turned, u + 1)
                    if u >= 2:
                        act.wait_ge(mixed, u - 1)
                    even = (t + 2) // 2 * P
                    act.copy(pT[:, u % 2, 0:even], bank(core, 4, 1)[:, 0:even]).then_inc(moved_act, 1)

                def exps(u):
                    h, t = units[u]
                    s = u % 2
                    width = (t + 1) * P
                    act.wait_ge(maxed, u + 1)
                    if u >= 2:
                        act.wait_ge(weighted, u - 1)
                    for m in range(2):
                        last = act.activation(p[:, u % 3, m, 0:width], p[:, u % 3, m, 0:width], ACT.Exp,
                                              bias=low[:, s, m:m + 1], accum_out=total[:, s, m:m + 1])
                    last.then_inc(exped, 1)

                for u in range(n + 2):
                    if u < n:
                        exps(u)
                    if u >= 2:
                        move(u - 2)


def stage_diff_norm(core, o, subln, ident, eps, yT):
    nc = core.nc
    with ExitStack() as stack:
        sq = core.sb(stack, "dn_sq", [P, TT * 512])
        r = core.sb(stack, "dn_r", [P, 4 * TT])
        sub = core.sb(stack, "dn_sub", [P, 1])
        squared = core.sem("dn_squared")
        rooted = core.sem("dn_rooted")
        chain = core.sem("dn_chain")
        scaled = core.sem("dn_scaled")
        turned = core.sem("dn_turned")
        moved = core.sem("dn_moved")
        heads = lambda a: a.rearrange("p (h d) -> p h d", d=P)
        with nc.Block(no_gpsimd_drain=True) as block:

            @block.vector
            def _(dve):
                dve.tensor_scalar(sub[:, :], subln, 1.0 - LAM_INIT, None, ALU.mult).then_inc(chain, 1)
                flat = o.rearrange("p t d -> p (t d)")
                dve.tensor_tensor(sq[:, :], flat, flat, ALU.mult).then_inc(chain, 1)
                dve.wait_ge(chain, 2)
                dve.tensor_reduce(r[:, :], heads(sq[:, :]), AX_X, ALU.add).then_inc(squared, 1)
                dve.wait_ge(rooted, 1)
                dve.reciprocal(r[:, :], r[:, :]).then_inc(chain, 1)
                dve.wait_ge(chain, 3)
                for t in range(TT):
                    dve.tensor_tensor(heads(o[:, t, :]), heads(o[:, t, :]),
                                      r[:, 4 * t:4 * t + 4].unsqueeze(2).to_broadcast([P, 4, P]),
                                      ALU.mult).then_inc(scaled, 1)
                for t in range(TT):
                    dve.wait_ge(turned, t + 1)
                    y = yT[:, 2:6, t * P:(t + 1) * P]
                    dve.scalar_tensor_tensor(out=y, in0=heads(bank(core, t % 4, 1)), scalar=sub[:, 0:1], in1=y,
                                             op0=ALU.mult, op1=ALU.mult).then_inc(moved, 1)

            @block.scalar
            def _(act):
                act.wait_ge(squared, 1)
                act.activation(r[:, :], r[:, :], ACT.Sqrt, bias=eps[:, 0:1], scale=1 / P).then_inc(rooted, 1)

            @block.tensor
            def _(pe):
                for t in range(TT):
                    pe.wait_ge(scaled, t + 1)
                    if t >= 4:
                        pe.wait_ge(moved, t - 3)
                    for h in range(4):
                        last = pe.transpose(bank(core, t % 4, 1)[:, h * P:(h + 1) * P],
                                            o[:, t, h * P:(h + 1) * P], ident)
                    last.then_inc(turned, 1)


def stage_swa_inputs(core, far_dram, table, v, ident):
    nc = core.nc
    with ExitStack() as stack:
        far = core.sb(stack, "swa_far", [P, 256])
        loaded = core.sem("swa_far_loaded")
        turned = core.sem("swa_v_turned")
        with nc.Block(no_gpsimd_drain=True) as block:

            @block.sync
            def _(sp):
                sp.dma_start(far[:, :], far_dram).then_inc(loaded, 16)

            @block.tensor
            def _(pe):
                for t in range(TT):
                    last = pe.transpose(bank(core, 0)[:, t * P:(t + 1) * P], v[:, t * P:(t + 1) * P], ident)
                last.then_inc(turned, 1)

            @block.scalar
            def _(act):
                act.wait_ge(turned, 1)
                act.copy(v, bank(core, 0))

            @block.vector
            def _(dve):
                dve.wait_ge(loaded, 16)
                for h in range(4):
                    dve.tensor_scalar(table[:, h, :], far[:, :], 2.0 ** -(1 + h), None, ALU.mult)


class Later:

    def __init__(self, core, stack):
        N, dram = SSM_GROUPS, core.nc.dram_tensor
        self.mod = core.sb(stack, "modulation", [P, 2 * KT])
        self.powers = core.sb(stack, "ssm_powers", [P, 2, LEVELS, N])
        self.d_cols = core.sb(stack, "ssm_d", [P, N])
        self.gate_dram = dram("gate_kept", (P, D), F32, kind="Internal").ap()
        shapes = ((P, N, 2 * P), (P, N, P), (P, N, N))
        self.kept = [dram(f"ssm_kept_{n}", s, F32, kind="Internal").ap() for n, s in enumerate(shapes)]


def first_block(core, A, const, cols, x1, later):
    nc = core.nc
    ident, same64, ones, eps = const[:, 0:128], const[:, 128:256], const[:, 256:384], const[:, 384:385]
    col = lambda n: cols[:, COL[n][0]:COL[n][1]]
    by_rows = lambda name: A[name].rearrange("(k p) n -> p k n", p=P)
    with ExitStack() as out_stack:
        mergedT = core.sb(out_stack, "mergedT", [P, KT, S])
        stack = out_stack.enter_context(ExitStack())
        hT = core.sb(stack, "hT", [P, 2, KT, S], F32R)
        x_rows = A["x"].rearrange("b (t p) d -> (b t) p d", p=P)
        w_in = A["w_in"].rearrange("(k p) n -> p k n", p=P)
        ybT = x1[:, 6:8, :]

        def columns(first):
            return lambda j: w_in[:, :, bass.ds(j * P + first, P)]

        with ExitStack() as b_stack:
            oT = x1[:, 0:6, :].rearrange("p (g c) s -> p g c s", g=3)
            maxima = core.sb(b_stack, "maxima", [P, 96])
            sums = core.sb(b_stack, "sums", [P, 96])
            v = mergedT[:, 0:6, :].rearrange("p a b -> p (a b)").rearrange("p (t g d) -> p t g d", t=TT, g=3)
            with ExitStack() as w_stack:
                gate_b = [Features(2, columns(4608), ACT.Silu, lambda j: tile_of(ybT, j))]
                w_z = feature_weights(core, w_stack, gate_b)
                stage_norm_transpose(core, TT, x_rows, col("norm_w"), None, hT, ident, eps, ahead=w_z)
                w_v = SplitMatrix(core, w_stack, w_in[:, :, 3840:4608], 768)
                scratch = nc.dram_tensor("bias_scratch", (3, 4, 384), F32, kind="Internal").ap()
                back = x1[:, 0:3, :].rearrange("p a (b c) -> p (a b) c", b=4)
                biases = BiasRows(core, A["rel"], A["onehot"], scratch, back, mergedT)
                stage_features(core, hT, gate_b, w_z, ahead=w_v, beside=[biases])
                stage_rows(core, [(lambda part, k, g=g, t=t: in_order(hT[:, part, k, :], g, t), 256 * g, 256,
                                   v[:, t, g, :]) for g in range(3) for t in range(TT)], w_v, 768, sync=biases.spread_rows)
            with ExitStack() as qkv_stack:
                qkT = core.sb(qkv_stack, "qkT", [P, 12, S])
                stage_heads(core, 12, hT, S, columns(2304), same64, 1 / 64,
                            lambda j: cols[:, bass.ds(j + COL["bqk"][0], 1)], qkT, eps, room=mergedT[:, 6:8, :])
                table = core.sb(qkv_stack, "bias_table", [P, 8, 256])
                table16 = core.sb(qkv_stack, "bias_table16", [P, 4, 128])
                stage_bias_tables(core, back, table[:, :, :], table16[:, :, :])
                stage_attention(core, window_units(qkT, v, oT, table, table16, maxima, sums), ident)
            stage_combine(core, maxima, sums, oT, ybT, ident, const[:, SEL:SEL + 256])

        core.clear_semaphores()
        ymT = core.sb(stack, "ymT", [P, 4, S])
        yaT = x1[:, 0:6, :]
        with ExitStack() as beside_stack:
            beside = [Modulation(core, beside_stack, A["c"], by_rows("ada_w"), col("ada_b"), A["ada_gate_b"],
                                 ones, col("norm_gain"), later.mod, later.gate_dram, mergedT[:, 6, :]),
                      SsmMatrices(core, beside_stack, A["ssm_prm"], A["ssm_bc"], const, later.kept,
                                  later.powers, later.d_cols, mergedT[:, 0:6, :])]
            stage_features(core, hT, [
                Features(4, columns(5376), ACT.Silu, lambda j: tile_of(ymT, j)),
                Features(6, columns(0), ACT.Gelu, lambda j: tile_of(yaT, j)),
                Features(6, columns(2 * A_WIDTH), ACT.Silu, lambda j: tile_of(yaT, j),
                         times=lambda j: tile_of(yaT, j))], beside=beside)
        with ExitStack() as m_stack:
            memT = core.sb(m_stack, "memT", [P, 2, KT, MEM], F32R)
            w_kv = A["m_w_kv"].rearrange("(k p) n -> p k n", p=P)
            mkT = mergedT[:, 0, :].rearrange("p (h t) -> p h t", h=4)
            with ExitStack() as w_stack:
                w_k = SplitTiles(core, w_stack, [(4, lambda j: w_kv[:, :, bass.ds(j * P, P)])])
                stage_norm_transpose(core, 2, A["mem"].rearrange("b (t p) d -> (b t) p d", p=P),
                                     col("mem_norm_w"), None, memT, ident, eps, ahead=w_k,
                                     room=mergedT[:, 4:8, :])
                stage_heads(core, 4, memT, MEM, w_k, ones, 1 / 128,
                            lambda j: cols[:, bass.ds(j + COL["mk"][0], 1)], mkT, eps)
            mv = mergedT[:, 1, :].rearrange("p (t d) -> p t d", t=2)
            stage_rows(core, [(lambda part, k, t=t: memT[:, part, k, t * P:(t + 1) * P], 0, M_WIDTH, mv[:, t, :])
                              for t in range(2)], w_kv[:, :, M_WIDTH:2 * M_WIDTH], M_WIDTH)
            mqT = mergedT[:, 2:6, :]
            stage_heads(core, 4, hT, S, columns(4864), ones, 1 / 128,
                        lambda j: cols[:, bass.ds(j + COL["mq"][0], 1)], mqT, eps)
            units = [dict(width=MEM, q=[mqT[:, h, t * P:(t + 1) * P] for h in range(4)],
                          k=[mkT[:, h, :] for h in range(4)], bias=None, sink=None, keep=None,
                          values=lambda h, b: mv[:, b, h * P:(h + 1) * P],
                          out=lambda h, o: o[:, h * P:(h + 1) * P],
                          store=(ymT[:, :, t * P:(t + 1) * P], lambda b: b.rearrange("p (h q) -> p h q", h=4)))
                     for t in range(TT)]
            stage_attention(core, units, ident)

        vv = mergedT[:, 0:6, :].rearrange("p a b -> p (a b)").rearrange("p (t d) -> p t d", t=TT)
        wide = mergedT[:, 6:8, 0:A_WIDTH]
        stage_gated_values(core, hT, w_in[:, :, A_WIDTH:2 * A_WIDTH], A["ln_rows"], wide, vv, eps)
        core.clear_semaphores()
        gate_tile = lambda b, j: w_in[:, :, bass.ds(j * P + 5888 + D * b, P)]
        w_gates = SplitTiles(core, stack, [(24, lambda n: gate_tile(0, 0))])
        stage_mix_chunks(core, vv, A["spatial_w"], A["spatial_b"], yaT, ahead=w_gates)

        projs = [lambda j, w=by_rows(n): w[:, :, bass.ds(j * P, P)] for n in ("proj_a", "proj_b", "proj_m")]
        gate0 = COL["gate_b"][0]
        stage_merge(core, hT, [(yaT, 6), (ybT, 2), (ymT, 4)], w_gates, gate_tile, projs,
                    lambda b, j: cols[:, bass.ds(j + gate0 + KT * b, 1)], mergedT)
        stack.close()
        stage_output(core, mergedT, by_rows("w_out"), lambda t: x_rows[t], None, x1)


def second_block(core, A, const, cols, x1, later, out):
    nc = core.nc
    ident, eps = const[:, 0:128], const[:, 384:385]
    col = lambda n: cols[:, COL[n][0]:COL[n][1]]
    by_rows = lambda name: A[name].rearrange("(k p) n -> p k n", p=P)
    N = SSM_GROUPS
    with ExitStack() as stack:
        gate = core.sb(stack, "x_gate", [P, D])
        yT = core.sb(stack, "yT", [P, KT, S])
        powers, d_cols, kept = later.powers, later.d_cols, later.kept
        shift, gain = later.mod[:, 0:KT], later.mod[:, KT:2 * KT]
        room_stack = stack.enter_context(ExitStack())
        room = core.sb(room_stack, "room", [P, 12, S])
        scratch_u = nc.dram_tensor("u_scratch", (N, N, 8, P), F32, kind="Internal").ap()
        scratch_y = nc.dram_tensor("y_scratch", (N, N, 8, P), F32, kind="Internal").ap()
        qT, kT = room[:, 0:4, :], room[:, 4:8, :]
        v = room[:, 8:12, :].rearrange("p a b -> p (a b)").rearrange("p (t d) -> p t d", t=TT)
        with ExitStack() as h_stack:
            h2T = core.sb(h_stack, "h2T", [P, 2, KT, S], F32R)
            w_in = by_rows("w_in_2")

            def columns(first):
                return lambda j: w_in[:, :, bass.ds(j * P + first, P)]

            wqT, wkT = room[:, 8:10, :], room[:, 10:11, :]
            wv = room[:, 11, :].rearrange("p (t d) -> p t d", t=TT)
            window_q = lambda j: [w_in[:, :, 2560 + P * n + 64 * j:][:, :, 0:64] for n in range(2)]
            groups = [
                Features(2, columns(0), ACT.Copy, lambda j: room[:, j, :].rearrange("p (t c) -> p c t", t=8),
                         view=lambda a: a.rearrange("p (c t) -> p c t", t=8),
                         save=[(scratch_u[8 * j:8 * j + 8].rearrange("g h t c -> (g h) (t c)"), room[:, j, :])
                               for j in range(2)]),
                Features(2, columns(256), ACT.Silu, lambda j: tile_of(yT, j)),
                Features(4, columns(2048), ACT.Silu, lambda j: tile_of(yT, j + 2)),
                Features(2, columns(3072), ACT.Silu, lambda j: tile_of(yT, j + 6)),
                Features(4, columns(512), ACT.Copy, lambda j: tile_of(qT, j), scale=64 ** -0.5, after_save=True),
                Features(4, columns(1024), ACT.Copy, lambda j: tile_of(kT, j)),
                Features(2, window_q, ACT.Copy, lambda j: tile_of(wqT, j),
                         scale=64 ** -0.5),
                Features(2, columns(2816), ACT.Copy, lambda j: room[:, 10 + j, :])]
            with ExitStack() as w_stack:
                w_2 = feature_weights(core, w_stack, groups, double=(18, 19))
                stage_norm_transpose(core, TT, x1, gain, shift, h2T, ident, eps, from_sbuf=True,
                                     ahead=w_2, room=room[:, 0:4, :])
                stage_features(core, h2T, groups, w_2)

            table = core.sb(h_stack, "window_table", [P, 4, 256])
            units = []
            for t in range(TT):
                width = 256 if t else P
                rows = [slice(64 * (n // 2), 64 * (n // 2) + 64) for n in range(4)]
                units.append(dict(
                    width=width, keep=None, sink=col("sinks"),
                    q=[wqT[rows[n], n % 2, t * P:(t + 1) * P] for n in range(4)],
                    k=[wkT[rows[n], 0, (t + 1) * P - width:(t + 1) * P] for n in range(4)],
                    bias=[table[:, n, 256 - width:256] for n in range(4)],
                    values=lambda n, b, t=t: wv[:, t - 1 + b if t else 0, 64 * (n // 2):64 * (n // 2) + 64],
                    out=lambda n, o: o[64 * (n % 2):64 * (n % 2) + 64, (n // 2) * P:(n // 2 + 1) * P],
                    store=(yT[:, 6:8, t * P:(t + 1) * P],
                           lambda b: b[:, 0:256].rearrange("p (h q) -> p h q", h=2))))
            core.clear_semaphores()
            stage_swa_inputs(core, A["far_window"], table, room[:, 11, :], ident)
            stage_attention(core, units, ident)

            for c in (0, 256):
                stage_rows(core, [(lambda part, k, t=t: h2T[:, part, k, t * P:(t + 1) * P], 0, 256, v[:, t, c:c + 256])
                                  for t in range(TT)], w_in[:, :, 1536 + c:1792 + c], 256)

        s_stack = room_stack.enter_context(ExitStack())
        G = core.sb(s_stack, "ssm_G", [P, N, 2 * P])
        M_out = core.sb(s_stack, "ssm_M", [P, N, P])
        c_stack = core.sb(s_stack, "ssm_C", [P, N, N])
        with ExitStack() as d_stack:
            neg_lam = core.sb(d_stack, "neg_lam", [P, 1])
            stage_diff_tables(core, A["lam"], neg_lam)
            o = core.sb(d_stack, "diff_o", [P, TT, 512])
            stage_diff_attention(core, qT, kT, v, A["far"], neg_lam[:, 0:1], ident, o,
                                 [(kept[0], G), (kept[1], M_out), (kept[2], c_stack), (later.gate_dram, gate)])
            stage_diff_norm(core, o, col("subln"), ident, eps, yT)

        core.clear_semaphores()
        Y = room[:, 0:2, :].rearrange("p a (g c) -> p (a g) c", c=P)
        L_room = room[:, 2:12, :].rearrange("p (k a) (g c) -> p k (a g) c", k=LEVELS - 2, c=P)
        stage_ssm_scan(core, L_room, scratch_u, const, ident, G, M_out, c_stack, powers, d_cols, Y)
        stage_ssm_output(core, Y, scratch_y, A["glu_w"].rearrange("(k p) n -> p k n", p=P),
                         col("glu_b"), yT)
        room_stack.close()
        stage_output(core, yT, by_rows("w_out_2"), None, gate[:, :], x1,
                     final=(A["final_gain"], eps, out.rearrange("b (t p) d -> (b t) p d", p=P)))


def layers(nc, A, out):
    with ExitStack() as stack:
        core = Core(nc, stack)
        const = core.sb(stack, "const", [P, CONST_COLS])
        cols = core.sb(stack, "cols", [P, COLS])
        x1 = core.sb(stack, "x1", [P, TT, D])
        stage_constants(core, A["const"], A["cols"], const, cols)
        later = Later(core, stack)
        first_block(core, A, const, cols, x1, later)
        core.clear_semaphores()
        second_block(core, A, const, cols, x1, later, out)


def pack_columns():
    sizes = [("norm_w", 8), ("mem_norm_w", 8), ("gate_b", 24), ("bqk", 12), ("mq", 4), ("mk", 4),
             ("norm_gain", 8), ("ada_b", 24), ("subln", 1), ("glu_b", 2), ("sinks", 4)]
    at, where = 0, {}
    for name, n in sizes:
        where[name] = (at, at + n)
        at += n
    return where, at


COL, COLS = pack_columns()
SEL, SWAP, SIGN = 512, 768, 385
CONST_COLS = 896


def bucket_rows():
    rows = np.zeros((33, 3, 384), np.float32)
    rows[32] = -1e30
    for g, dilation in enumerate((1, 4, 16)):
        for apart in range(129):
            if g == 2 and (apart % 2 or apart == 128):
                continue
            dist = (apart // 2 if g == 2 else apart) * dilation
            large = 16 + int(np.float32(np.log(np.float32(max(dist, 1)) / np.float32(16))
                                        / np.float32(math.log(2048 / 16))) * np.float32(16))
            rows[dist if dist < 16 else min(large, 31), g, 127 + apart] = 1.0
            rows[32, g, 127 + apart] = 0.0
    return rows


def distances(rows, width, at, limit):
    away = at + np.arange(rows)[:, None] - np.arange(width)[None, :]
    return np.where((away >= 0) & (away < limit), -away.astype(np.float32), np.float32(-1e30)).astype(np.float32)


def ssm_columns(I):
    twice = lambda v: np.concatenate([v, v])
    G = SSM_GROUPS
    return np.ascontiguousarray(np.stack([
        twice(I["ssm_lam_re_2"][0].T), twice(I["ssm_lam_im_2"][0].T),
        np.broadcast_to(I["ssm_log_step_2"][0][None], (P, G)),
        np.concatenate([I["ssm_d_2"][0].reshape(G, G).T] * 8)], axis=1))


def ssm_matrices(I):
    br, bi = (I[n][0].transpose(1, 0, 2) for n in ("ssm_b_re_2", "ssm_b_im_2"))
    cr, ci = (I[n][0].transpose(2, 0, 1) for n in ("ssm_c_re_2", "ssm_c_im_2"))
    stacks = [np.concatenate(pair) for pair in ((br, bi), (bi, br), (cr, ci), (ci, cr))]
    return np.ascontiguousarray(np.stack(stacks, axis=1))


def kernel(**inputs):
    import concourse.bacc as bacc
    from concourse.bass_utils import run_bass_kernel_spmd

    I = {k: np.asarray(v) for k, v in inputs.items()}
    const = np.zeros((P, CONST_COLS), np.float32)
    const[:, 0:128] = np.eye(P)
    const[:, 128:256] = np.kron(np.eye(2), np.ones((64, 64)))
    const[:, 256:384] = 1.0
    const[:, 384] = EPS
    for n, h in enumerate(HEAD_AT):
        at = SEL + P * (h // 2) + 64 * (h % 2)
        const[n, at:at + 64] = 1.0
    for p in range(P):
        const[p, SWAP + (p + 64) % P] = 1.0 if p < 64 else -1.0
    const[:, SIGN] = np.where(np.arange(P) < 64, -1.0, 1.0)

    def by_tile(v):
        return v.reshape(-1, P).T

    def over_partitions(v):
        return np.ascontiguousarray(np.broadcast_to(v[None], (P,) + v.shape))

    two = lambda v: np.concatenate([v, v])[:, None]
    parts = {
        "norm_w": by_tile(I["norm_w"]), "mem_norm_w": by_tile(I["mem_norm_w"]),
        "gate_b": by_tile(I["gate_b"]),
        "bqk": np.concatenate([two(I["b_q_norm_w"])] * 6 + [two(I["b_k_norm_w"])] * 6, 1),
        "mq": np.repeat(I["m_q_norm_w"][:, None], 4, 1), "mk": np.repeat(I["m_k_norm_w"][:, None], 4, 1),
        "norm_gain": by_tile(I["norm_gain_2"]), "ada_b": by_tile(I["ada_b_2"]),
        "subln": I["diff_subln_2"].reshape(P, 1), "glu_b": by_tile(I["glu_b_2"]),
        "sinks": over_partitions(I["swa_sinks_2"].reshape(4)),
    }
    arrays = {
        "const": const,
        "cols": np.ascontiguousarray(np.concatenate([parts[n] for n in COL], axis=1)),
        "x": I["x"], "w_in": I["w_in"], "mem": I["mem"], "m_w_kv": I["m_w_kv"],
        "proj_a": I["proj_a"], "proj_b": I["proj_b"], "proj_m": I["proj_m"], "w_out": I["w_out"],
        "c": by_tile(I["c_2"]), "ada_w": I["ada_w_2"][0], "ada_gate_b": over_partitions(I["ada_b_2"][0, 2 * D:]),
        "w_in_2": I["w_in_2"][0], "w_out_2": I["w_out_2"][0], "glu_w": I["glu_w_2"][0],
        "final_gain": over_partitions(I["final_gain_2"]),
        "lam": over_partitions(np.concatenate([I[n] for n in ("diff_lq1_2", "diff_lk1_2", "diff_lq2_2",
                                                              "diff_lk2_2")])),
        "ssm_prm": ssm_columns(I), "ssm_bc": ssm_matrices(I),
        "far": distances(P, D, 7 * P, D), "far_window": distances(P, 2 * P, P, P),
        "ln_rows": over_partitions(np.stack([I["a_v_norm_w"], I["a_v_norm_b"]])),
        "spatial_w": np.ascontiguousarray(I["a_spatial_w"].transpose(2, 0, 1)),
        "spatial_b": np.ascontiguousarray(np.repeat(I["a_spatial_b"], A_WIDTH // 4, axis=0)
                                          .reshape(6, P, P).transpose(1, 0, 2)), "onehot": bucket_rows(),
        "rel": np.concatenate([I["rel_bias"], np.ones((1, 12), np.float32)]),
    }
    nc = bacc.Bacc("TRN2", target_bir_lowering=False, num_devices=1)
    dram = {n: nc.dram_tensor(n, a.shape, mybir.dt.from_np(a.dtype), kind="ExternalInput").ap()
            for n, a in arrays.items()}
    out = nc.dram_tensor("out", (1, S, D), F32, kind="ExternalOutput").ap()
    layers(nc, dram, out)
    r = run_bass_kernel_spmd(nc, [arrays], core_ids=[0])
    return r.results[0]["out"]
```
